# Optimizing a Trainium2 kernel written in Bass

```python
import math
import jax, jax.numpy as jnp
from jax import lax
import numpy as np

D_MODEL = 1024
BATCH = 1
SEQ = 256
DEPTH = 1

N_META = 16
BLOCK = 128
PAD_FRONT = BLOCK - N_META
HEAD_DIM = 64
FOX_HEADS = 8
SWA_Q_HEADS = 8
SWA_KV_HEADS = 2
WINDOW = 128
N_BUCKETS = 32
MAX_DISTANCE = 128
D_FF = 2816
EPS = 1e-6
NEG = -1e30
FORGET_BIAS_INIT = 2.0
FOX_W = FOX_HEADS * HEAD_DIM
SWA_QW = SWA_Q_HEADS * HEAD_DIM
SWA_KVW = SWA_KV_HEADS * HEAD_DIM
D_IN = 3 * FOX_W + FOX_HEADS + SWA_QW + 2 * SWA_KVW + 2 * D_MODEL


def rms_norm(x, g):
    xf = x.astype(jnp.float32)
    ms = jnp.mean(xf * xf, axis=-1, keepdims=True)
    return (xf * lax.rsqrt(ms + EPS) * g.astype(jnp.float32)).astype(x.dtype)

def swiglu(h, w_in, w_out):
    gu = h @ w_in
    gate, up = jnp.split(gu, 2, axis=-1)
    return (jax.nn.silu(gate) * up) @ w_out

def t5_bucket(dist):
    n = jnp.maximum(dist, 0)
    max_exact = N_BUCKETS // 2
    nf = jnp.maximum(n, 1).astype(jnp.float32)
    large = max_exact + (jnp.log(nf / max_exact) / math.log(MAX_DISTANCE / max_exact)
                         * (N_BUCKETS - max_exact)).astype(jnp.int32)
    large = jnp.minimum(large, N_BUCKETS - 1)
    return jnp.where(n < max_exact, n, large)

def fox_attention(q, k, v, log_f):
    b, p, h, dh = q.shape
    nb = p // BLOCK
    c_k = jnp.cumsum(log_f, axis=1).transpose(0, 2, 1)
    k_pos = jnp.arange(p)
    k_valid = k_pos >= PAD_FRONT
    qb = q.reshape(b, nb, BLOCK, h, dh).transpose(1, 0, 2, 3, 4)
    cqb = c_k.reshape(b, h, nb, BLOCK).transpose(2, 0, 1, 3)
    scale = dh ** -0.5

    def one_block(args):
        qi, cqi, i = args
        q_pos = i * BLOCK + jnp.arange(BLOCK)
        s = jnp.einsum('bqhd,bkhd->bhqk', qi, k, preferred_element_type=jnp.float32) * scale
        s = s + cqi[..., :, None] - c_k[:, :, None, :]
        mask = (k_pos[None, :] <= q_pos[:, None]) & k_valid[None, :]
        s = jnp.where(mask[None, None], s, NEG)
        pr = jax.nn.softmax(s, axis=-1)
        return jnp.einsum('bhqk,bkhd->bqhd', pr.astype(v.dtype), v)

    out = lax.map(one_block, (qb, cqb, jnp.arange(nb)))
    return out.transpose(1, 0, 2, 3, 4).reshape(b, p, h * dh)

def swa_attention(q, k, v, sinks, rel_bias_table):
    b, p, hq, dh = q.shape
    kv = k.shape[2]
    r = hq // kv
    nb = p // BLOCK
    scale = dh ** -0.5
    qb = q.reshape(b, nb, BLOCK, kv, r, dh)

    def band(a):
        a_ext = jnp.concatenate([jnp.zeros_like(a[:, :BLOCK]), a], axis=1)
        a_ext = a_ext.reshape(b, nb + 1, BLOCK, kv, dh)
        return jnp.concatenate([a_ext[:, :-1], a_ext[:, 1:]], axis=2)

    kb, vb = band(k), band(v)
    km, vm = k[:, PAD_FRONT:BLOCK], v[:, PAD_FRONT:BLOCK]
    q_pos = jnp.arange(nb)[:, None] * BLOCK + jnp.arange(BLOCK)[None, :]
    band_pos = (jnp.arange(nb)[:, None] - 1) * BLOCK + jnp.arange(2 * BLOCK)[None, :]
    meta_pos = PAD_FRONT + jnp.arange(N_META)
    d_band = q_pos[:, :, None] - band_pos[:, None, :]
    m_band = (d_band >= 0) & (d_band < WINDOW) & (band_pos[:, None, :] >= PAD_FRONT)
    d_meta = q_pos[:, :, None] - meta_pos[None, None, :]
    m_meta = d_meta >= WINDOW
    table = rel_bias_table.astype(jnp.float32)
    bias_band = table[t5_bucket(d_band)].transpose(0, 3, 1, 2).reshape(nb, kv, r, BLOCK, 2 * BLOCK)
    bias_meta = table[t5_bucket(d_meta)].transpose(0, 3, 1, 2).reshape(nb, kv, r, BLOCK, N_META)

    s_band = jnp.einsum('bnqgrd,bnkgd->bngrqk', qb, kb, preferred_element_type=jnp.float32) * scale + bias_band[None]
    s_band = jnp.where(m_band[None, :, None, None], s_band, NEG)
    s_meta = jnp.einsum('bnqgrd,bmgd->bngrqm', qb, km, preferred_element_type=jnp.float32) * scale + bias_meta[None]
    s_meta = jnp.where(m_meta[None, :, None, None], s_meta, NEG)
    s = jnp.concatenate([s_band, s_meta], axis=-1)
    sink = sinks.astype(jnp.float32).reshape(kv, r)[None, None, :, :, None, None]
    mx = jnp.maximum(jnp.max(s, axis=-1, keepdims=True), sink)
    pr = jnp.exp(s - mx)
    pr = pr / (jnp.sum(pr, axis=-1, keepdims=True) + jnp.exp(sink - mx))
    pr = pr.astype(v.dtype)
    out = (jnp.einsum('bngrqk,bnkgd->bnqgrd', pr[..., :2 * BLOCK], vb)
           + jnp.einsum('bngrqm,bmgd->bnqgrd', pr[..., 2 * BLOCK:], vm))
    return out.reshape(b, p, hq * dh)

def token_mixer(h, rel_bias_table, w_in, forget_bias, fox_q_norm, fox_k_norm,
                swa_q_norm, swa_k_norm, swa_sinks, w_branch_fox, w_branch_swa, w_out):
    b, p, _ = h.shape
    proj = h @ w_in
    widths = [FOX_W, FOX_W, FOX_W, FOX_HEADS, SWA_QW, SWA_KVW, SWA_KVW, D_MODEL]
    idx = list(np.cumsum(widths))
    qa, ka, va, fa, qb, kb, vb, ga, gb = jnp.split(proj, idx, axis=-1)
    qa = rms_norm(qa.reshape(b, p, FOX_HEADS, HEAD_DIM), fox_q_norm)
    ka = rms_norm(ka.reshape(b, p, FOX_HEADS, HEAD_DIM), fox_k_norm)
    va = va.reshape(b, p, FOX_HEADS, HEAD_DIM)
    log_f = jax.nn.log_sigmoid(fa.astype(jnp.float32) + forget_bias.astype(jnp.float32))
    qb = rms_norm(qb.reshape(b, p, SWA_Q_HEADS, HEAD_DIM), swa_q_norm)
    kb = rms_norm(kb.reshape(b, p, SWA_KV_HEADS, HEAD_DIM), swa_k_norm)
    vb = vb.reshape(b, p, SWA_KV_HEADS, HEAD_DIM)
    o_fox = fox_attention(qa, ka, va, log_f)
    o_swa = swa_attention(qb, kb, vb, swa_sinks, rel_bias_table)
    y = jax.nn.sigmoid(ga) * (o_fox @ w_branch_fox) + jax.nn.sigmoid(gb) * (o_swa @ w_branch_swa)
    return y @ w_out

def first_inputs(seed: int = 0) -> dict:
    key = jax.random.key(seed)
    ks = jax.random.split(key, 24)
    f32 = jnp.float32

    def nrm(k, shape, scale):
        return jax.random.normal(k, shape, f32) * scale

    def gain(k, shape):
        return 1.0 + 0.1 * jax.random.normal(k, shape, f32)

    return {
        "x": nrm(ks[0], (BATCH, SEQ, D_MODEL), 1.0),
        "meta_tokens": nrm(ks[1], (N_META, D_MODEL), 1.0),
        "rel_bias_table": nrm(ks[2], (N_BUCKETS, SWA_Q_HEADS), 0.5),
        "ffn1_norm": gain(ks[3], (DEPTH, D_MODEL)),
        "ffn1_w_in": nrm(ks[4], (DEPTH, D_MODEL, 2 * D_FF), D_MODEL ** -0.5),
        "ffn1_w_out": nrm(ks[5], (DEPTH, D_FF, D_MODEL), D_FF ** -0.5),
        "mix_norm": gain(ks[6], (DEPTH, D_MODEL)),
        "w_in": nrm(ks[7], (DEPTH, D_MODEL, D_IN), D_MODEL ** -0.5),
        "forget_bias": FORGET_BIAS_INIT + 0.1 * jax.random.normal(ks[8], (DEPTH, FOX_HEADS), f32),
        "fox_q_norm": gain(ks[9], (DEPTH, HEAD_DIM)),
        "fox_k_norm": gain(ks[10], (DEPTH, HEAD_DIM)),
        "swa_q_norm": gain(ks[11], (DEPTH, HEAD_DIM)),
        "swa_k_norm": gain(ks[12], (DEPTH, HEAD_DIM)),
        "swa_sinks": nrm(ks[13], (DEPTH, SWA_Q_HEADS), 0.5),
        "w_branch_fox": nrm(ks[14], (DEPTH, FOX_W, D_MODEL), FOX_W ** -0.5),
        "w_branch_swa": nrm(ks[15], (DEPTH, SWA_QW, D_MODEL), SWA_QW ** -0.5),
        "w_out": nrm(ks[16], (DEPTH, D_MODEL, D_MODEL), D_MODEL ** -0.5),
        "ffn2_norm": gain(ks[17], (DEPTH, D_MODEL)),
        "ffn2_w_in": nrm(ks[18], (DEPTH, D_MODEL, 2 * D_FF), D_MODEL ** -0.5),
        "ffn2_w_out": nrm(ks[19], (DEPTH, D_FF, D_MODEL), D_FF ** -0.5),
    }

def first_block(x, meta_tokens, rel_bias_table, ffn1_norm, ffn1_w_in, ffn1_w_out, mix_norm,
              w_in, forget_bias, fox_q_norm, fox_k_norm, swa_q_norm, swa_k_norm, swa_sinks,
              w_branch_fox, w_branch_swa, w_out, ffn2_norm, ffn2_w_in, ffn2_w_out):
    b = x.shape[0]
    pad = jnp.zeros((b, PAD_FRONT, D_MODEL), x.dtype)
    meta = jnp.broadcast_to(meta_tokens.astype(x.dtype)[None], (b, N_META, D_MODEL))
    h = jnp.concatenate([pad, meta, x], axis=1)
    for l in range(DEPTH):
        h = h + 0.5 * swiglu(rms_norm(h, ffn1_norm[l]), ffn1_w_in[l], ffn1_w_out[l])
        h = h + token_mixer(rms_norm(h, mix_norm[l]), rel_bias_table, w_in[l], forget_bias[l],
                            fox_q_norm[l], fox_k_norm[l], swa_q_norm[l], swa_k_norm[l],
                            swa_sinks[l], w_branch_fox[l], w_branch_swa[l], w_out[l])
        h = h + 0.5 * swiglu(rms_norm(h, ffn2_norm[l]), ffn2_w_in[l], ffn2_w_out[l])
    return h[:, BLOCK:]


CHUNK = 64
CONV_CH = D_MODEL // 2
CONV_WIDTH = 31
RET_HEADS = 8
RET_DV = (D_MODEL // 2) // RET_HEADS
RET_DK = RET_DV // 2
D_MIX = CONV_CH + RET_HEADS * RET_DV
N_MEM = 256
XATTN_HEADS = 4
XATTN_HEAD_DIM = D_MODEL // XATTN_HEADS
D_FF_2 = 4 * D_MODEL
ROPE_BASE = 10000.0

IN_SPLITS = (CONV_CH, CONV_CH, RET_HEADS * RET_DK, RET_HEADS * RET_DK, RET_HEADS * RET_DV, RET_HEADS * RET_DV)
D_IN_2 = sum(IN_SPLITS)


def rmsnorm(x, w):
    xf = x.astype(jnp.float32)
    y = xf * lax.rsqrt(jnp.mean(xf * xf, axis=-1, keepdims=True) + EPS)
    return (y * w.astype(jnp.float32)).astype(x.dtype)

def apply_rotary(t, positions):
    half = t.shape[-1] // 2
    inv_freq = ROPE_BASE ** (-jnp.arange(half, dtype=jnp.float32) / half)
    ang = positions.astype(jnp.float32)[..., None] * inv_freq
    cos = jnp.cos(ang)[:, :, None, :]
    sin = jnp.sin(ang)[:, :, None, :]
    t1, t2 = t[..., :half].astype(jnp.float32), t[..., half:].astype(jnp.float32)
    return jnp.concatenate([t1 * cos - t2 * sin, t1 * sin + t2 * cos], axis=-1)

def conv_module(a, b, conv_w, conv_b, ln_w, ln_b):
    u = a * jax.nn.sigmoid(b)
    y = lax.conv_general_dilated(
        u, conv_w[:, None, :], window_strides=(1,), padding=[(CONV_WIDTH - 1, 0)],
        dimension_numbers=("NWC", "WIO", "NWC"), feature_group_count=CONV_CH) + conv_b
    yf = y.astype(jnp.float32)
    mu = jnp.mean(yf, axis=-1, keepdims=True)
    var = jnp.mean(jnp.square(yf - mu), axis=-1, keepdims=True)
    yn = (yf - mu) * lax.rsqrt(var + EPS) * ln_w + ln_b
    return jax.nn.silu(yn)

def retention(q, k, v, positions):
    B, S = q.shape[:2]
    N = S // CHUNK
    q = apply_rotary(q.reshape(B, S, RET_HEADS, RET_DK), positions) * (RET_DK ** -0.5)
    k = apply_rotary(k.reshape(B, S, RET_HEADS, RET_DK), positions)
    v = v.reshape(B, S, RET_HEADS, RET_DV).astype(jnp.float32)
    qc = q.reshape(B, N, CHUNK, RET_HEADS, RET_DK)
    kc = k.reshape(B, N, CHUNK, RET_HEADS, RET_DK)
    vc = v.reshape(B, N, CHUNK, RET_HEADS, RET_DV)

    log_g = jnp.log1p(-jnp.exp2(-5.0 - jnp.arange(RET_HEADS, dtype=jnp.float32)))
    idx = jnp.arange(CHUNK, dtype=jnp.float32)
    dist = jnp.abs(idx[:, None] - idx[None, :])
    decay_in = jnp.exp(log_g[:, None, None] * dist)
    zeta = jnp.exp(log_g[:, None] * (CHUNK - 1 - idx)[None, :])
    xi = jnp.exp(log_g[:, None] * (idx + 1.0)[None, :])
    g_chunk = jnp.exp(log_g * CHUNK)

    scores = jnp.einsum('bnihd,bnjhd->bnhij', qc, kc) * decay_in
    y_in = jnp.einsum('bnhij,bnjhe->bnihe', scores, vc)

    kv = jnp.einsum('bnjhd,bnjhe,hj->nbhde', kc, vc, zeta)

    def step(state, kv_n):
        return g_chunk[None, :, None, None] * state + kv_n, state

    init = jnp.zeros((B, RET_HEADS, RET_DK, RET_DV), jnp.float32)
    _, state_prev = lax.scan(step, init, kv)
    y_x = jnp.einsum('bnihd,nbhde,hi->bnihe', qc, state_prev, xi)
    return (y_in + y_x).reshape(B, S, RET_HEADS, RET_DV)

def head_group_mixer(h, positions, w_in, conv_w, conv_b, conv_ln_w, conv_ln_b, ret_gn_w, w_out):
    B, S, _ = h.shape
    proj = h @ w_in
    cuts = list(np.cumsum(IN_SPLITS)[:-1])
    ca, cb, rq, rk, rv, rg = jnp.split(proj, cuts, axis=-1)
    y_conv = conv_module(ca, cb, conv_w, conv_b, conv_ln_w, conv_ln_b)
    y = retention(rq, rk, rv, positions)
    mu = jnp.mean(y, axis=-1, keepdims=True)
    var = jnp.mean(jnp.square(y - mu), axis=-1, keepdims=True)
    y = (y - mu) * lax.rsqrt(var + EPS) * ret_gn_w.reshape(RET_HEADS, RET_DV)
    y_ret = jax.nn.silu(rg.astype(jnp.float32)) * y.reshape(B, S, RET_HEADS * RET_DV)
    merged = jnp.concatenate([y_conv, y_ret], axis=-1).astype(h.dtype)
    return merged @ w_out

def memory_cross_attention(h, mem_n, xq_w, xkv_w, xo_w):
    B, S, _ = h.shape
    q = (h @ xq_w).reshape(B, S, XATTN_HEADS, XATTN_HEAD_DIM)
    kv = (mem_n @ xkv_w).reshape(B, N_MEM, 2, XATTN_HEADS, XATTN_HEAD_DIM)
    k, v = kv[:, :, 0], kv[:, :, 1]
    s = jnp.einsum('bshd,bmhd->bhsm', q.astype(jnp.float32), k.astype(jnp.float32)) * (XATTN_HEAD_DIM ** -0.5)
    p = jax.nn.softmax(s, axis=-1)
    o = jnp.einsum('bhsm,bmhd->bshd', p, v.astype(jnp.float32)).reshape(B, S, D_MODEL)
    return o.astype(h.dtype) @ xo_w

def sq_relu_mlp(h, up_w, down_w):
    return jnp.square(jax.nn.relu(h @ up_w)) @ down_w

def second_inputs(seed: int = 0) -> dict:
    key = jax.random.key(seed)
    ks = jax.random.split(key, 24)
    f32 = jnp.float32

    def w(k, shape, fan_in):
        return jax.random.normal(k, shape, f32) * (fan_in ** -0.5)

    def gain(k, n):
        return 1.0 + 0.02 * jax.random.normal(k, (n,), f32)

    x = jax.random.normal(ks[0], (BATCH, SEQ, D_MODEL), f32)
    mem = jax.random.normal(ks[1], (BATCH, N_MEM, D_MODEL), f32)
    start = jax.random.randint(ks[2], (BATCH, 1), 0, 1000, dtype=jnp.int32) * CHUNK
    positions = (start + jnp.arange(SEQ, dtype=jnp.int32)[None, :]).astype(jnp.int32)
    return {
        "x": x,
        "mem": mem,
        "positions": positions,
        "norm_mix_w": gain(ks[3], D_MODEL),
        "w_in": w(ks[4], (D_MODEL, D_IN_2), D_MODEL),
        "conv_w": w(ks[5], (CONV_WIDTH, CONV_CH), CONV_WIDTH),
        "conv_b": 0.02 * jax.random.normal(ks[6], (CONV_CH,), f32),
        "conv_ln_w": gain(ks[7], CONV_CH),
        "conv_ln_b": 0.02 * jax.random.normal(ks[8], (CONV_CH,), f32),
        "ret_gn_w": gain(ks[9], RET_HEADS * RET_DV),
        "w_out": w(ks[10], (D_MIX, D_MODEL), D_MIX),
        "norm_xattn_w": gain(ks[11], D_MODEL),
        "norm_mem_w": gain(ks[12], D_MODEL),
        "xq_w": w(ks[13], (D_MODEL, D_MODEL), D_MODEL),
        "xkv_w": w(ks[14], (D_MODEL, 2 * D_MODEL), D_MODEL),
        "xo_w": w(ks[15], (D_MODEL, D_MODEL), D_MODEL),
        "norm_mlp_w": gain(ks[16], D_MODEL),
        "mlp_up_w": w(ks[17], (D_MODEL, D_FF_2), D_MODEL),
        "mlp_down_w": w(ks[18], (D_FF_2, D_MODEL), D_FF_2),
        "norm_f_w": gain(ks[19], D_MODEL),
    }

def second_block(x, mem, positions, norm_mix_w, w_in, conv_w, conv_b, conv_ln_w, conv_ln_b, ret_gn_w, w_out,
              norm_xattn_w, norm_mem_w, xq_w, xkv_w, xo_w, norm_mlp_w, mlp_up_w, mlp_down_w, norm_f_w):
    h = x
    mem_n = rmsnorm(mem, norm_mem_w)
    for _ in range(DEPTH):
        h = h + head_group_mixer(rmsnorm(h, norm_mix_w), positions, w_in, conv_w, conv_b,
                                 conv_ln_w, conv_ln_b, ret_gn_w, w_out)
        h = h + memory_cross_attention(rmsnorm(h, norm_xattn_w), mem_n, xq_w, xkv_w, xo_w)
        h = h + sq_relu_mlp(rmsnorm(h, norm_mlp_w), mlp_up_w, mlp_down_w)
    return rmsnorm(h, norm_f_w).astype(x.dtype)


def setup_inputs(seed=0):
    out = dict(first_inputs(seed))
    for name, value in second_inputs(seed + 1).items():
        if name != "x":
            out[name + "_2"] = value
    return out


def reference(
    x, meta_tokens, rel_bias_table, ffn1_norm, ffn1_w_in, ffn1_w_out, mix_norm, w_in,
    forget_bias, fox_q_norm, fox_k_norm, swa_q_norm, swa_k_norm, swa_sinks, w_branch_fox,
    w_branch_swa, w_out, ffn2_norm, ffn2_w_in, ffn2_w_out, mem_2, positions_2, norm_mix_w_2,
    w_in_2, conv_w_2, conv_b_2, conv_ln_w_2, conv_ln_b_2, ret_gn_w_2, w_out_2, norm_xattn_w_2,
    norm_mem_w_2, xq_w_2, xkv_w_2, xo_w_2, norm_mlp_w_2, mlp_up_w_2, mlp_down_w_2, norm_f_w_2,
):
    x = first_block(
        x, meta_tokens, rel_bias_table, ffn1_norm, ffn1_w_in, ffn1_w_out, mix_norm, w_in,
        forget_bias, fox_q_norm, fox_k_norm, swa_q_norm, swa_k_norm, swa_sinks, w_branch_fox,
        w_branch_swa, w_out, ffn2_norm, ffn2_w_in, ffn2_w_out,
    )
    return second_block(
        x, mem_2, positions_2, norm_mix_w_2, w_in_2, conv_w_2, conv_b_2, conv_ln_w_2,
        conv_ln_b_2, ret_gn_w_2, w_out_2, norm_xattn_w_2, norm_mem_w_2, xq_w_2, xkv_w_2, xo_w_2,
        norm_mlp_w_2, mlp_up_w_2, mlp_down_w_2, norm_f_w_2,
    )


_drawn_inputs = setup_inputs


def setup_inputs(seed=0):
    import zlib

    import numpy as np

    out = dict(_drawn_inputs(seed))
    spreads = {}
    factors = {'forget_bias': 2.85,
     'swa_q_norm': 4.727,
     'swa_k_norm': 5.326,
     'swa_sinks': 8.0,
     'norm_mix_w_2': 3.348,
     'conv_b_2': 3.731,
     'conv_ln_w_2': 6.958,
     'conv_ln_b_2': 7.993,
     'ret_gn_w_2': 8.0,
     'norm_xattn_w_2': 8.0,
     'norm_mem_w_2': 8.0,
     'norm_mlp_w_2': 12.037}
    for name, (base, spread) in spreads.items():
        noise = np.random.default_rng([zlib.crc32(name.encode()), seed]).standard_normal(out[name].shape)
        drawn = base * np.exp(spread * noise) if base else spread * noise
        out[name] = __import__('jax').numpy.asarray(drawn.astype(out[name].dtype))
    for name, factor in factors.items():
        out[name] = (out[name] * factor).astype(out[name].dtype)
    return out
```

```python
from contextlib import ExitStack

import numpy as np

import concourse.bass as bass
from concourse import mybir

F32 = mybir.dt.float32
F32R = mybir.dt.float32r
I32 = mybir.dt.int32
ALU = mybir.AluOpType
ACT = mybir.ActivationFunctionType
AX = mybir.AxisListType

P = 128
D = 1024
KT = D // P
NX = 256
META = 16
T = NX + META
SEG = P + META
W2 = 2 * SEG
FF = 2816
FT = FF // P
FF2 = 4096
F2T = FF2 // P
HEADS = 8
HD = 64
EPS = 1e-6
NEG = -1e30
WINDOW = 128
BUCKETS = 32
CONV = 512
TAPS = 31
XH_DIM = 256
XHEADS = 4
RDK = 32
RING = 4
LEAD = 3
WIDE = 11

PHASES = [
    ("f1in", 2 * FT, KT, 2 * FT, 4), ("f1out", 2 * KT, WIDE, KT, 2),
    ("mix", 35, KT, 35, 3), ("branch", KT, KT, 2 * KT, 4), ("wo", KT, KT, KT, 4),
    ("f2in", 2 * FT, KT, 2 * FT, 4), ("f2out", 2 * KT, WIDE, KT, 2),
    ("mixb", 20, KT, 20, 4), ("xkv", 16, KT, 16, 4), ("wo2", KT, KT, KT, 4),
    ("xq", KT, KT, KT, 4), ("xo", KT, KT, KT, 4),
    ("up", F2T, KT, F2T, 4), ("down", 4 * KT, KT, KT, 2),
]
V_FOXQ, V_FOXK, V_SWAQ, V_SWAK, V_FBIAS, V_FREQ, V_CONVB, V_LNW, V_LNB, V_GNW, V_SINK = (
    0, 1, 2, 3, 4, 5, 6, 10, 14, 18, 22)
V_COLS = V_SINK + HEADS
N_F1, N_MIX, N_F2, N_MIXB, N_XATT, N_MLP, N_FINAL, N_MEM = range(8)

ANGLE_STEPS = 19
REL_X = 384
REL_M = 272


def plan():
    first, sizes, banks = {}, [], []
    for name, n, tiles, groups, ring in PHASES:
        first[name] = (len(sizes), len(banks))
        sizes += [tiles] * n
        banks += [(len(banks) + i) % ring for i in range(groups)]
    need = [max([p + 1 for p in range(g) if banks[p] == b], default=0) for g, b in enumerate(banks)]
    return first, sizes, banks, need


def build(nc, io):
    first, sizes, banks, need = plan()
    C = len(sizes)
    counts = {name: n for name, n, *_ in PHASES}

    ctx = ExitStack()
    with ctx:
        def sem(name):
            return ctx.enter_context(nc.semaphore(name))

        top = [((nc.sbuf_base + 63) // 64) * 64]

        def place(name, shape, dt=F32, at=None):
            size = int(np.prod(shape[1:])) * 4
            size = (size + 31) // 32 * 32
            where = top[0] if at is None else at[0]
            t = nc.alloc_sbuf_tensor_at(name, shape, dt, offset=where)
            if at is None:
                top[0] += size
            else:
                at[0] += size
                assert at[0] <= nc.sbuf_usable_end, (name, at[0])
            return t

        raw = place("raw", [P, RING, WIDE * P])
        whi = place("whi", [P, RING, WIDE * P], F32R)
        wlo = place("wlo", [P, RING, WIDE * P], F32R)
        xhi = place("xhi", [P, KT, W2], F32R)
        xlo = place("xlo", [P, KT, W2], F32R)
        res = place("res", [P, KT, W2])
        ones = place("ones", [P, P])
        same = place("same_head", [P, P])
        ident = place("ident", [P, P])
        swap = place("swap", [P, P])
        selneg = place("selneg", [HEADS, HEADS * P])
        gains = place("gains", [P, 8 * KT])
        vecs = place("vecs", [P, V_COLS])
        convw = place("convw", [P, 4 * TAPS])
        epsc = place("epsc", [P, 2])
        rstd = place("rstd", [P, W2])
        sd = place("sd", [P, W2])
        work_at = top[0]
        sq = place("sq", [P, 2, W2])
        tg = place("tg", [P, W2])
        tu = place("tu", [P, W2])
        sg = place("sg", [P, W2])
        hd = place("hd", [P, W2])
        rtok = place("rtok", [P, 4])
        angle = place("angle", [P, NX])
        area = top[0]

        at = [area]
        hid_hi = place("hid_hi", [P, F2T * NX], F32R, at)
        hid_lo = place("hid_lo", [P, F2T * NX], F32R, at)

        at = [area]
        oy_hi = place("oy_hi", [P, 16, NX], F32R, at)
        oy_lo = place("oy_lo", [P, 16, NX], F32R, at)
        qn = place("qn", [P, 8, NX], F32, at)
        kn = place("kn", [P, 5, T], F32, at)
        v0 = place("v0", [P, 640], F32, at)
        v1 = place("v1", [P, 640], F32, at)
        vm = place("vm", [META, 640], F32, at)
        gate_at = at[0]
        gate = place("gate", [P, 16, NX], F32, at)
        ckb = place("ckb", [P, HEADS, T], F32, at)
        rel = place("rel", [P, HEADS, SEG + T], F32, at)
        att = place("att", [P, 2, SEG + T], F32, at)
        mask = place("mask", [P, SEG + T], F32, at)
        cq = place("cq", [P, 16], F32, at)
        small = place("small", [P, 2, 12], F32, at)
        at = [work_at]
        bm = place("bm", [P, SEG + T], F32, at)
        pts = place("pts", [P, 2, 384], F32, at)
        ptm = place("ptm", [META, 2, NX], F32, at)
        at = [gate_at]
        fa = place("fa", [HEADS, T], F32, at)
        fabs = place("fabs", [HEADS, T], F32, at)
        fexp = place("fexp", [HEADS, T], F32, at)
        fmin = place("fmin", [HEADS, T], F32, at)
        flog = place("flog", [HEADS, T], F32, at)
        fones = place("fones", [HEADS, T], F32, at)
        cum = place("cum", [HEADS, T], F32, at)
        table = place("table", [BUCKETS + 1, HEADS], F32, at)
        onehot = place("onehot", [BUCKETS + 1, REL_X + REL_M], F32, at)
        relrow = place("relrow", [HEADS, REL_X + REL_M], F32, at)

        at = [area]
        oz_hi = place("oz_hi", [P, 8, NX], F32R, at)
        oz_lo = place("oz_lo", [P, 8, NX], F32R, at)
        mem_hi = place("mem_hi", [P, KT, NX], F32R, at)
        mem_lo = place("mem_lo", [P, KT, NX], F32R, at)
        mem_at = at[0]
        mem = place("mem", [P, KT, NX], F32, at)
        glu_at = at[0]
        glu = place("glu", [P, 4, TAPS - 1 + NX], F32, at)
        cy = place("cy", [P, 4, NX], F32, at)
        qr = place("qr", [P, 4, NX], F32, at)
        v2 = place("v2", [P, 2, 512], F32, at)
        rg = place("rg", [P, 4, NX], F32, at)
        cosv = place("cosv", [P, NX], F32, at)
        sinv = place("sinv", [P, NX], F32, at)
        vmem = place("vmem", [P, 2, D], F32, at)
        amat = place("amat", [P, 2, 384], F32, at)
        yr = place("yr", [P, 2, NX], F32, at)
        zt = place("zt", [P, 2, NX], F32, at)
        memr = place("memr", [P, NX], F32, at)
        memsd = place("memsd", [P, NX], F32, at)
        msq = place("msq", [P, 2, NX], F32, at)
        decay_at = at[0]
        decay = place("decay", [P, HEADS, 384], F32, at)
        at = [mem_at]
        km = place("km", [P, KT, NX], F32, at)
        at = [glu_at]
        qx = place("qx", [P, KT, NX], F32, at)
        at = [decay_at]
        xatt = place("xatt", [P, 2, 512], F32, at)
        xpt = place("xpt", [P, 2, 512], F32, at)
        xsmall = place("xsmall", [P, 2, 8], F32, at)

        at = [area + 2 * F2T * NX * 4]
        posi = place("posi", [P, NX], I32, at)
        posf = place("posf", [P, NX], F32, at)
        turns = place("turns", [P, NX], F32, at)
        part = place("part", [P, NX], F32, at)
        at = [area]
        outb = place("outb", [P, KT, NX], F32, at)

        ps = [ctx.enter_context(nc.psum_tensor(f"bank{i}", [P, 512], F32)) for i in range(8)]
        STAT = ps[4]

        rel_dram = nc.dram_tensor("rel_rows", (HEADS, REL_X + REL_M), F32, kind="Internal")
        rel_wide = nc.dram_tensor("rel_copies", (P, HEADS, REL_X + REL_M), F32, kind="Internal")

        w_in = [sem(f"w_in{s}") for s in range(RING)]
        w_hi = sem("w_hi")
        w_lo = sem("w_lo")
        pe_done = sem("pe_done")
        acc_free = sem("acc_free")
        x_hi, x_lo = sem("x_hi"), sem("x_lo")
        sq_ready = sem("sq_ready")
        stat_mm = sem("stat_mm")
        norm_sd, norm_r = sem("norm_sd"), sem("norm_r")
        res_in, gain_in = sem("res_in"), sem("gain_in")
        const_in, pos_in = sem("const_in"), sem("pos_in")
        ones_set, mask_set = sem("ones_set"), sem("mask_set")
        angle_step = sem("angle_step")
        ffs = {f: {s: sem(f"{f}_{s}") for s in ("silu", "prod", "hhi", "hlo")} for f in ("f1", "f2")}
        up_prod, up_hhi, up_hlo = sem("up_prod"), sem("up_hhi"), sem("up_hlo")
        out_tile, out_done = sem("out_tile"), sem("out_done")
        qk_sq, qk_ss, qk_sd, qk_r, qk_n = (sem(s) for s in ("qk_sq", "qk_ss", "qk_sd", "qk_r", "qk_n"))
        rt_mm, rt_copied = sem("rt_mm"), sem("rt_copied")
        f_act, f_dve = sem("f_act"), sem("f_dve")
        cq_mm, cq_copied, ck_mm, ck_copied = (sem(s) for s in ("cq_mm", "cq_copied", "ck_mm", "ck_copied"))
        table_set, rel_const, rel_mm, rel_row, rel_out, rel_in = (
            sem(s) for s in ("table_set", "rel_const", "rel_mm", "rel_row", "rel_out", "rel_in"))
        at_s, at_bias, at_max, at_neg, at_exp, at_sum, at_inv, at_norm = (
            sem(s) for s in ("at_s", "at_bias", "at_max", "at_neg", "at_exp", "at_sum", "at_inv", "at_norm"))
        at_tr, at_pt, at_pv, o_hi, o_lo = (sem(s) for s in ("at_tr", "at_pt", "at_pv", "o_hi", "o_lo"))
        sig_done, y_step, y_hi, y_lo = (sem(s) for s in ("sig_done", "y_step", "y_hi", "y_lo"))
        decay_in, mem_in, glu_zero = sem("decay_in"), sem("mem_in"), sem("glu_zero")
        cs_act, cs_dve = sem("cs_act"), sem("cs_dve")
        cb_sig, glu_done, conv_step = sem("cb_sig"), sem("glu_done"), sem("conv_step")
        rot_mm, rot_step, rg_done = sem("rot_mm"), sem("rot_step"), sem("rg_done")
        m_hi, m_lo, m_sq, m_stat, m_sd, m_r = (sem(s) for s in ("m_hi", "m_lo", "m_sq", "m_stat", "m_sd", "m_r"))
        ra_mm, ra_dec, ry_mm, ry_copied = (sem(s) for s in ("ra_mm", "ra_dec", "ry_mm", "ry_copied"))
        gn_mu, gn_cen, gn_sq, gn_var, gn_sd, gn_r, gn_n, gn_z = (
            sem(s) for s in ("gn_mu", "gn_cen", "gn_sq", "gn_var", "gn_sd", "gn_r", "gn_n", "gn_z"))
        ln_mu, ln_cen, ln_sq, ln_var, ln_sd, ln_r, ln_n, ln_z = (
            sem(s) for s in ("ln_mu", "ln_cen", "ln_sq", "ln_var", "ln_sd", "ln_r", "ln_n", "ln_z"))
        z_hi, z_lo = sem("z_hi"), sem("z_lo")
        xs_s, xs_max, xs_neg, xs_exp, xs_inv, xs_norm, xs_tr, xs_pt, xs_pv, xo_hi, xo_lo = (
            sem(s) for s in ("xs_s", "xs_max", "xs_neg", "xs_exp", "xs_inv", "xs_norm", "xs_tr", "xs_pt",
                             "xs_pv", "xo_hi", "xo_lo"))

        def seg(ap):
            return ap.rearrange("p (s t) -> p s t", s=2)[:, :, 0:P]

        def two(ap):
            return ap.rearrange("p (s t) -> p s t", s=2)

        def res_tile(m, full):
            return res[:, m, 0:T] if full else seg(res[:, m, :])

        def x_tile(t, m, full):
            return t[:, m, 0:T] if full else two(t[:, m, 0:NX])

        def flat_or_two(ap, full):
            return ap[:, 0:T] if full else two(ap[:, 0:NX])

        def gain(n, m):
            return gains[:, n * KT + m:n * KT + m + 1] if isinstance(m, int) else gains[:, bass.ds(m + n * KT, 1)]

        def hid(t, j, n):
            return t[:, 0:FT * T].rearrange("p (j t) -> p j t", t=n)[:, j, :] if n == T else \
                t[:, 0:F2T * NX].rearrange("p (j t) -> p j t", t=n)[:, j, :]

        def bodies(eng, n, per, body):
            count = n // per
            body(0, True)
            if count > 3:
                with eng.Fori(1, count - 1) as i:
                    body(i, False)
            else:
                for i in range(1, count - 1):
                    body(i, False)
            if count > 1:
                body(count - 1, True)

        def split_hi(act, c0, per, i, j):
            static = isinstance(i, int)
            c = c0 + per * i + j
            if static and c >= C:
                return
            s = (c if static else c0 + j) % RING
            tiles = sizes[c] if static else sizes[c0 + per + j]
            act.wait_ge(w_in[s], (c // RING + 1) * 16 if static else (per // RING * i + ((c0 + j) // RING + 1)) * 16)
            if not (static and c < RING):
                act.wait_ge(pe_done, c - (RING - 1))
            nc.scalar.activation(whi[:, s, 0:tiles * P], raw[:, s, 0:tiles * P], ACT.Copy).then_inc(w_hi, 1)

        def split_lo(dve, c0, per, i, j):
            static = isinstance(i, int)
            c = c0 + per * i + j
            if static and c >= C:
                return
            s = (c if static else c0 + j) % RING
            tiles = sizes[c] if static else sizes[c0 + per + j]
            dve.wait_ge(w_hi, c + 1)
            nc.vector.tensor_tensor(wlo[:, s, 0:tiles * P], raw[:, s, 0:tiles * P], whi[:, s, 0:tiles * P],
                                    ALU.subtract).then_inc(w_lo, 1)

        def start_group(pe, g0, per, i, j):
            if isinstance(i, int):
                if need[g0 + per * i + j]:
                    pe.wait_ge(acc_free, need[g0 + per * i + j])
            else:
                pe.wait_ge(acc_free, need[g0 + per + j] + per * (i - 1))
            return ps[banks[g0 + (per if not isinstance(i, int) else per * i) + j]]

        def strip(out, s, tiles, rhs_hi, rhs_lo, start=True, stop=True, at=0, before=None):
            for t in range(tiles):
                if before is not None:
                    before(t)
                w = slice((at + t) * P, (at + t + 1) * P)
                nc.tensor.matmul(out, whi[:, s, w], rhs_hi(t), start=start and t == 0, stop=False)
                nc.tensor.matmul(out, whi[:, s, w], rhs_lo(t), start=False, stop=False)
                mm = nc.tensor.matmul(out, wlo[:, s, w], rhs_hi(t), start=False, stop=stop and t == tiles - 1)
            return mm

        def rows(out, s, hi_src, lo_src, tok, start=True):
            for t in range(KT):
                w = slice(t * P, (t + 1) * P)
                nc.tensor.matmul(out, hi_src[:, t, tok:tok + P], whi[:, s, w], start=start and t == 0, stop=False)
                nc.tensor.matmul(out, lo_src[:, t, tok:tok + P], whi[:, s, w], start=False, stop=False)
                mm = nc.tensor.matmul(out, hi_src[:, t, tok:tok + P], wlo[:, s, w], start=False, stop=t == KT - 1)
            return mm

        def pe_stat(pe, n, m, full):
            width = T if full else NX
            pe.wait_ge(sq_ready, KT * n + m + 1)
            if m == 0 and n:
                pe.wait_ge(norm_sd, n)
            nc.tensor.matmul(STAT[:, 0:width], ones[:, :], sq[:, m % 2, 0:width],
                             start=m == 0, stop=m == KT - 1).then_inc(stat_mm, 1)

        def act_prep(act, n, m, full, prep, par=None):
            par = m % 2 if par is None else par
            if not (isinstance(m, int) and KT * n + m < 2):
                act.wait_ge(stat_mm, m + (KT * n - 1))
            if prep:
                nc.scalar.activation(x_tile(xhi, m, full), res_tile(m, full), ACT.Copy,
                                     scale=gain(n, m)).then_inc(x_hi, 1)
            nc.scalar.activation(flat_or_two(sq[:, par, :], full), res_tile(m, full),
                                 ACT.Square).then_inc(sq_ready, 1)

        def dve_prep(dve, n, m, full):
            dve.wait_ge(x_hi, m + (KT * n + 1))
            nc.vector.scalar_tensor_tensor(x_tile(xlo, m, full), res_tile(m, full), gain(n, m),
                                           x_tile(xhi, m, full), ALU.mult, ALU.subtract).then_inc(x_lo, 1)

        def act_norm(act, n, full):
            width = T if full else NX
            act.wait_ge(stat_mm, KT * (n + 1))
            if n:
                act.wait_ge(norm_r, n)
            nc.scalar.activation(sd[:, 0:width], STAT[:, 0:width], ACT.Sqrt, bias=epsc[:, 0:1],
                                 scale=1.0 / D).then_inc(norm_sd, 1)

        def dve_norm(dve, n, full):
            width = T if full else NX
            dve.wait_ge(norm_sd, n + 1)
            nc.vector.reciprocal(rstd[:, 0:width], sd[:, 0:width]).then_inc(norm_r, 1)
            dve.wait_ge(norm_r, n + 1)

        def x_rhs(full_rows):
            if full_rows == "all":
                return (lambda t: xhi[:, t, 0:T]), (lambda t: xlo[:, t, 0:T])
            if full_rows == "x":
                return (lambda t: seg(xhi[:, t, :])), (lambda t: seg(xlo[:, t, :]))
            return (lambda t: xhi[:, t, 0:NX]), (lambda t: xlo[:, t, 0:NX])

        def wait_x(pe, n):
            return lambda t: pe.wait_ge(x_lo, KT * n + t + 1)

        def pe_ff_in(pe, name, n, width):
            c0, g0 = first[name]
            hi, lo = x_rhs("all" if width == T else "packed")

            def body(i, edge):
                for j in range(4):
                    pe.wait_ge(w_lo, c0 + 4 * i + j + 1)
                    out = start_group(pe, g0, 4, i, j)
                    head = edge and i == 0 and j == 0
                    strip(out[:, 0:width], (c0 + j) % RING, KT, hi, lo,
                          before=wait_x(pe, n) if head else None).then_inc(pe_done, 1)
                    if head:
                        pe_stat(pe, n, KT - 1, width == T)
            bodies(pe, counts[name], 4, body)

        def act_ff_in(act, name, n, width):
            c0, g0 = first[name]
            f = ffs[name[:2]]

            def body(i, edge):
                for j in range(4):
                    split_hi(act, c0, 4, i, j + LEAD)
                    if edge and i == 0 and j == 0:
                        act_norm(act, n, width == T)
                    u = 2 * i + j // 2
                    if j % 2 == 0:
                        act.wait_ge(acc_free, g0 + 4 * i + j + 1)
                        nc.scalar.activation(sg[:, 0:width], tg[:, 0:width], ACT.Silu).then_inc(f["silu"], 1)
                    else:
                        act.wait_ge(f["prod"], u + 1)
                        nc.scalar.activation(hid(hid_hi, u, width), hd[:, 0:width], ACT.Copy).then_inc(f["hhi"], 1)
            bodies(act, counts[name], 4, body)

        def dve_ff_in(dve, name, n, width):
            c0, g0 = first[name]
            f = ffs[name[:2]]

            def hidden_lo(u):
                dve.wait_ge(f["hhi"], u + 1)
                nc.vector.tensor_tensor(hid(hid_lo, u, width), hd[:, 0:width], hid(hid_hi, u, width),
                                        ALU.subtract).then_inc(f["hlo"], 1)

            def body(i, edge):
                for j in range(4):
                    head = edge and i == 0 and j == 0
                    if head:
                        split_lo(dve, c0, 4, i, j + LEAD)
                        dve_norm(dve, n, width == T)
                    out = ps[banks[g0 + j]][:, 0:width]
                    u = 2 * i + j // 2
                    dve.wait_ge(pe_done, c0 + 4 * i + j + 1)
                    if j % 2 == 0:
                        nc.vector.tensor_tensor(tg[:, 0:width], out, rstd[:, 0:width], ALU.mult).then_inc(acc_free, 1)
                        if not head:
                            hidden_lo(u - 1)
                    else:
                        nc.vector.tensor_tensor(tu[:, 0:width], out, rstd[:, 0:width], ALU.mult).then_inc(acc_free, 1)
                        dve.wait_ge(f["silu"], u + 1)
                        dve.wait_ge(acc_free, g0 + 4 * i + j + 1)
                        nc.vector.tensor_tensor(hd[:, 0:width], tu[:, 0:width], sg[:, 0:width],
                                                ALU.mult).then_inc(f["prod"], 1)
                    if not head:
                        split_lo(dve, c0, 4, i, j + LEAD)
            bodies(dve, counts[name], 4, body)
            hidden_lo(FT - 1)

        def pe_residual(pe, name, n, full, cpm, rhs, ready):
            c0, g0 = first[name]
            tiles = sizes[c0]
            width = T if full else NX
            per = 2 * cpm if cpm > 1 else 4
            mpb = per // cpm

            def body(i, edge):
                for j in range(per):
                    q, m = j % cpm, j // cpm
                    pe.wait_ge(w_lo, c0 + per * i + j + 1)
                    if q == 0:
                        out = start_group(pe, g0, mpb, i, m)
                    head = edge and i == 0 and m == 0
                    strip(out[:, 0:width], (c0 + j) % RING, tiles,
                          lambda t: rhs(q * tiles + t)[0], lambda t: rhs(q * tiles + t)[1],
                          start=q == 0, stop=q == cpm - 1,
                          before=(lambda t: ready(q * tiles + t)) if head else None).then_inc(pe_done, 1)
                    if q == cpm - 1 and not head:
                        stat(i, m)

            def stat(i, m):
                k = mpb * i + m - 1
                if isinstance(k, int):
                    pe_stat(pe, n, k, full)
                else:
                    pe.wait_ge(sq_ready, KT * n + 1 + k)
                    nc.tensor.matmul(STAT[:, 0:width], ones[:, :], sq[:, (m - 1) % 2, 0:width],
                                     start=False, stop=False).then_inc(stat_mm, 1)
            bodies(pe, counts[name], per, body)

        def act_residual(act, name, n, full, cpm, prep=True):
            c0, g0 = first[name]
            per = 2 * cpm if cpm > 1 else 4
            mpb = per // cpm

            def body(i, edge):
                for j in range(per):
                    split_hi(act, c0, per, i, j + LEAD)
                    if j % cpm == cpm - 1:
                        m = j // cpm
                        act.wait_ge(acc_free, g0 + mpb * i + m + 1)
                        act_prep(act, n, mpb * i + m, full, prep, par=m % 2)
            bodies(act, counts[name], per, body)

        def dve_residual(dve, name, n, full, cpm, scale, prep=True):
            c0, g0 = first[name]
            width = T if full else NX
            per = 2 * cpm if cpm > 1 else 4
            mpb = per // cpm

            def body(i, edge):
                for j in range(per):
                    if j % cpm == cpm - 1:
                        m = j // cpm
                        k = mpb * i + m
                        out = ps[banks[g0 + (mpb * i if isinstance(i, int) else mpb) + m]]
                        dve.wait_ge(pe_done, c0 + per * i + j + 1)
                        nc.vector.scalar_tensor_tensor(res_tile(k, full), flat_or_two(out, full), scale,
                                                       res_tile(k, full), ALU.mult, ALU.add).then_inc(acc_free, 1)
                        if prep and not (edge and i == 0 and m == 0):
                            dve_prep(dve, n, k - 1, full)
                    split_lo(dve, c0, per, i, j + LEAD)
            bodies(dve, counts[name], per, body)
            if prep:
                dve_prep(dve, n, KT - 1, full)

        mc, mg = first["mix"]
        QKT = 13
        V_FIRST, GATES = 14, 19
        UNITS = 16
        STEP0 = 17

        def qk_tile(t):
            if t < 4:
                return kn[:, t, :], T, V_FOXK
            if t < 8:
                return qn[:, t - 4, :], NX, V_FOXQ
            if t == 8:
                return kn[:, 4, :], T, V_SWAK
            return qn[:, t - 5, :], NX, V_SWAQ

        def unit(u):
            b = HD * (u % 2)
            return (u // 2, u // 2, b, u) if u < 8 else (u // 2, 4, b, (u - 8) // 2 + 4 * (u % 2))

        def pe_mix_chunk(pe, q):
            c, g = mc + q, mg + q
            pe.wait_ge(w_lo, c + 1)
            out = start_group(pe, mg, 1, q, 0)
            s = c % RING
            if V_FIRST <= q < GATES:
                for tt, tok in enumerate((0, P, SEG)):
                    mm = rows(out[:, tt * P:(tt + 1) * P], s, xhi, xlo, tok)
            else:
                wide = q < 5 or q == 9
                hi, lo = x_rhs("all" if wide else "x")
                mm = strip(out[:, 0:T if wide else NX], s, KT, hi, lo, before=wait_x(pe, N_MIX) if q == 0 else None)
            mm.then_inc(pe_done, 1)

        def pe_mix(pe):
            for q in range(STEP0):
                pe_mix_chunk(pe, q)
                if q == 0:
                    pe_stat(pe, N_MIX, KT - 1, True)
                if q == 4:
                    pe.wait_ge(norm_r, N_MIX + 1)
                    for tt, tok in enumerate((0, P, SEG)):
                        mm = nc.tensor.matmul(ps[5][:, tt:tt + 1], rstd[0:1, tok:tok + P], ones[0:1, 0:1],
                                              start=True, stop=True)
                    mm.then_inc(rt_mm, 1)
                if q == 6:
                    pe.wait_ge(rel_const, 32)
                    pe.wait_ge(table_set, 1)
                    pe.wait_ge(rt_copied, 1)
                    pe.wait_ge(norm_sd, N_MIX + 1)
                    nc.tensor.matmul(ps[4][0:HEADS, 0:REL_X], table[:, :], onehot[:, 0:REL_X], start=True, stop=True)
                    nc.tensor.matmul(ps[5][0:HEADS, 0:REL_M], table[:, :], onehot[:, REL_X:], start=True,
                                     stop=True).then_inc(rel_mm, 1)
                if q >= 3 and q - 3 < QKT:
                    pe_head_sums(pe, q - 3)
                if q == 13:
                    pe.wait_ge(f_dve, 6)
                    pe.wait_ge(rel_row, 2)
                    for tt, tok in enumerate((0, SEG)):
                        mm = nc.tensor.matmul(ps[5][:, tt * HEADS:(tt + 1) * HEADS], cum[:, tok:tok + P],
                                              ident[0:HEADS, 0:HEADS], start=True, stop=True)
                    mm.then_inc(cq_mm, 1)
                if q >= 14:
                    for h in range(3 * (q - 14), min(3 * (q - 14) + 3, HEADS)):
                        if h == 1:
                            pe.wait_ge(cq_copied, 1)
                        if h >= 2:
                            pe.wait_ge(ck_copied, h - 1)
                        nc.tensor.matmul(ps[4 + h % 2][:, 0:T], selneg[:, h * P:(h + 1) * P], cum[:, :],
                                         start=True, stop=True).then_inc(ck_mm, 1)
            for u in range(UNITS + 2):
                if u < UNITS:
                    pe_scores(pe, u)
                pe_mix_chunk(pe, STEP0 + u)
                if 1 <= u <= UNITS:
                    pe_turn(pe, u - 1)
                if u >= 2:
                    pe_values(pe, u - 2)

        def pe_head_sums(pe, t):
            width = qk_tile(t)[1]
            pe.wait_ge(qk_sq, t + 1)
            if t >= 2:
                pe.wait_ge(qk_sd, t - 1)
            nc.tensor.matmul(ps[6 + t % 2][:, 0:width], same[:, :], sq[:, t % 2, 0:width],
                             start=True, stop=True).then_inc(qk_ss, 1)

        def pe_scores(pe, u):
            qt, kt, b, _ = unit(u)
            if u == 0:
                pe.wait_ge(qk_n, 8)
                pe.wait_ge(ck_copied, HEADS)
            if u == 8:
                pe.wait_ge(qk_n, QKT)
            if u >= 2:
                pe.wait_ge(at_max, 2 * (u - 2) + 2)
            out = ps[4 + u % 2]
            nc.tensor.matmul(out[:, 0:SEG], qn[b:b + HD, qt, 0:P], kn[b:b + HD, kt, 0:SEG], start=True, stop=True)
            nc.tensor.matmul(out[:, SEG:SEG + T], qn[b:b + HD, qt, P:NX], kn[b:b + HD, kt, 0:T],
                             start=True, stop=True).then_inc(at_s, 1)

        def pe_turn(pe, u):
            p = att[:, u % 2, :]
            pe.wait_ge(at_norm, 2 * u + 2)
            if u >= 1:
                pe.wait_ge(at_pt, 2 * u)
            if u == 0:
                pe.wait_ge(qk_sd, QKT)
            for n, lo in enumerate((0, SEG, 2 * SEG)):
                nc.tensor.transpose(ps[6][:, n * P:(n + 1) * P], p[:, lo:lo + P], ident[:, :])
            for n, lo in enumerate((P, SEG + P)):
                mm = nc.tensor.transpose(ps[3][:, n * P:(n + 1) * P], p[:, lo:lo + P], ident[:, :])
            mm.then_inc(at_tr, 1)

        def pe_values(pe, u):
            b = HD * (u % 2)
            h = unit(u)[3]
            col = h * HD if u < 8 else 512 + (u % 2) * HD
            pe.wait_ge(at_pt, 2 * u + 2)
            if u == 0:
                pe.wait_ge(acc_free, mg + GATES)
            if u >= 2 and u % 2 == 0:
                pe.wait_ge(o_lo, u // 2)
            o = ps[7][b:b + HD, 0:NX]
            keys, meta = pts[:, u % 2, :], ptm[:, u % 2, :]
            nc.tensor.matmul(o, v0[:, col:col + HD], keys[:, 0:NX], start=True, stop=False)
            nc.tensor.matmul(ps[7][b:b + HD, P:NX], v1[:, col:col + HD], keys[:, NX:NX + P], start=False, stop=False)
            nc.tensor.matmul(o, vm[:, col:col + HD], meta, start=False, stop=True).then_inc(at_pv, 1)

        def act_mix(act):
            act.wait_ge(angle_step, ANGLE_STEPS)
            for q in range(STEP0):
                split_hi(act, mc, 1, q, LEAD)
                if q == 0:
                    act_norm(act, N_MIX, True)
                if 1 <= q <= QKT:
                    t = q - 1
                    dst, width, _ = qk_tile(t)
                    act.wait_ge(acc_free, mg + q + 1)
                    if t >= 2:
                        act.wait_ge(qk_ss, t - 1)
                    nc.scalar.activation(sq[:, t % 2, 0:width], dst, ACT.Square).then_inc(qk_sq, 1)
                if q == 3:
                    nc.scalar.activation(fabs[:, :], fa[:, :], ACT.Abs,
                                         bias=vecs[0:HEADS, V_FBIAS:V_FBIAS + 1]).then_inc(f_act, 1)
                    act.wait_ge(f_act, 1)
                    nc.scalar.activation(fexp[:, :], fabs[:, :], ACT.Exp, scale=-1.0).then_inc(f_act, 1)
                    act.wait_ge(f_act, 2)
                    nc.scalar.activation(flog[:, :], fexp[:, :], ACT.Ln, bias=ones[0:HEADS, 0:1]).then_inc(f_act, 1)
                if q == 7:
                    act.wait_ge(rel_mm, 1)
                    nc.scalar.activation(relrow[:, 0:REL_X], ps[4][0:HEADS, 0:REL_X], ACT.Copy).then_inc(rel_row, 1)
                    nc.scalar.activation(relrow[:, REL_X:], ps[5][0:HEADS, 0:REL_M], ACT.Copy).then_inc(rel_row, 1)
                if q >= 3 and q - 3 < QKT:
                    t = q - 3
                    width = qk_tile(t)[1]
                    is_q = qk_tile(t)[2] in (V_FOXQ, V_SWAQ)
                    act.wait_ge(qk_ss, t + 1)
                    if t >= 2:
                        act.wait_ge(qk_r, t - 1)
                    root = sg if t % 2 else tu
                    nc.scalar.activation(root[:, 0:width], ps[6 + t % 2][:, 0:width], ACT.Sqrt,
                                         bias=epsc[:, 1:2] if is_q else epsc[:, 0:1],
                                         scale=1.0 if is_q else 1.0 / HD).then_inc(qk_sd, 1)
                if q >= 14:
                    for h in range(3 * (q - 14), min(3 * (q - 14) + 3, HEADS)):
                        act.wait_ge(ck_mm, h + 1)
                        nc.scalar.activation(ckb[:, h, :], ps[4 + h % 2][:, 0:T], ACT.Copy).then_inc(ck_copied, 1)
            for u in range(UNITS + 2):
                split_hi(act, mc, 1, STEP0 + u, LEAD)
                if u < UNITS:
                    act_softmax(act, u)
                if 1 <= u <= UNITS:
                    v = u - 1
                    act.wait_ge(at_tr, v + 1)
                    if v >= 2:
                        act.wait_ge(at_pv, v - 1)
                    nc.scalar.activation(pts[:, v % 2, :], ps[6][:, 0:384], ACT.Copy).then_inc(at_pt, 1)
                    nc.scalar.activation(ptm[:, v % 2, :], ps[3][0:META, 0:NX], ACT.Copy).then_inc(at_pt, 1)
                if u >= 2 and u % 2 == 1:
                    act_heads_out(act, (u - 2) // 2)

        def act_softmax(act, u):
            s = small[:, u % 2, :]
            a = att[:, u % 2, :]
            act.wait_ge(at_neg, u + 1)
            if u >= 2:
                act.wait_ge(at_inv, u - 1)
            nc.scalar.activation(a[:, 0:SEG], a[:, 0:SEG], ACT.Exp, bias=s[:, 2:3], accum_out=s[:, 4:5]).then_inc(at_exp, 1)
            if u >= 8:
                h = unit(u)[3]
                nc.scalar.activation(s[:, 8:10], s[:, 2:4], ACT.Exp,
                                     bias=vecs[:, V_SINK + h:V_SINK + h + 1]).then_inc(at_exp, 1)
            nc.scalar.activation(a[:, SEG:], a[:, SEG:], ACT.Exp, bias=s[:, 3:4], accum_out=s[:, 5:6]).then_inc(at_exp, 1)

        def exps(u):
            return 2 * (u + 1) + max(u - 7, 0)

        def act_heads_out(act, t):
            act.wait_ge(at_pv, 2 * t + 2)
            nc.scalar.activation(oy_hi[:, t, :], ps[7][:, 0:NX], ACT.Copy).then_inc(o_hi, 1)

        def dve_mix(dve):
            dve.wait_ge(angle_step, ANGLE_STEPS)
            for q in range(STEP0):
                if q == 0:
                    split_lo(dve, mc, 1, q, LEAD)
                    dve_norm(dve, N_MIX, True)
                dve_mix_read(dve, q)
                if q == 2:
                    dve_forget_min(dve)
                if q == 4:
                    dve_forget_scan(dve)
                if q == 5:
                    dve.wait_ge(rt_mm, 1)
                    nc.vector.tensor_copy(rtok[:, 0:3], ps[5][:, 0:3]).then_inc(rt_copied, 1)
                if q:
                    split_lo(dve, mc, 1, q, LEAD)
                if q >= 4:
                    dve_head_norm(dve, q - 4)
                if q == 14:
                    dve.wait_ge(cq_mm, 1)
                    nc.vector.tensor_copy(cq[:, :], ps[5][:, 0:16]).then_inc(cq_copied, 1)
            for u in range(UNITS + 2):
                if u < UNITS:
                    dve_scores(dve, u)
                split_lo(dve, mc, 1, STEP0 + u, LEAD)
                if u < UNITS:
                    dve_probs(dve, u)
                dve_mix_read(dve, STEP0 + u)
                if u >= 2 and u % 2 == 1:
                    t = (u - 2) // 2
                    dve.wait_ge(o_hi, t + 1)
                    nc.vector.tensor_tensor(oy_lo[:, t, :], ps[7][:, 0:NX], oy_hi[:, t, :],
                                            ALU.subtract).then_inc(o_lo, 1)

        def dve_mix_read(dve, q):
            out = ps[banks[mg + q]]
            dve.wait_ge(pe_done, mc + q + 1)
            if q == 0:
                nc.vector.tensor_tensor(fa[:, :], out[0:HEADS, 0:T], rstd[0:HEADS, 0:T], ALU.mult).then_inc(acc_free, 1)
            elif q <= QKT:
                dst, width, _ = qk_tile(q - 1)
                if width == T:
                    nc.vector.tensor_tensor(dst, out[:, 0:T], rstd[:, 0:T], ALU.mult).then_inc(acc_free, 1)
                else:
                    nc.vector.tensor_tensor(two(dst), two(out[:, 0:NX]), seg(rstd[:, :]), ALU.mult).then_inc(acc_free, 1)
            elif q < GATES:
                col = slice((q - V_FIRST) * P, (q - V_FIRST + 1) * P)
                if q == V_FIRST:
                    dve.wait_ge(rt_copied, 1)
                nc.vector.tensor_scalar(v0[:, col], out[:, 0:P], rtok[:, 0:1], None, ALU.mult)
                nc.vector.tensor_scalar(vm[:, col], out[0:META, P:2 * P], rtok[0:META, 1:2], None, ALU.mult)
                nc.vector.tensor_scalar(v1[:, col], out[:, 2 * P:3 * P], rtok[:, 2:3], None, ALU.mult).then_inc(acc_free, 1)
            else:
                if q == GATES:
                    dve.wait_ge(rel_out, 16)
                    dve.wait_ge(ck_copied, HEADS)
                nc.vector.tensor_tensor(two(gate[:, q - GATES, :]), two(out[:, 0:NX]), seg(rstd[:, :]),
                                        ALU.mult).then_inc(acc_free, 1)

        def dve_forget_min(dve):
            dve.wait_ge(acc_free, mg + 1)
            nc.vector.tensor_scalar(fmin[:, :], fa[:, :], vecs[0:HEADS, V_FBIAS:V_FBIAS + 1], 0.0, ALU.add,
                                    ALU.min).then_inc(f_dve, 1)
            nc.vector.memset(fones[:, :], 1.0).then_inc(f_dve, 1)

        def dve_forget_scan(dve):
            dve.wait_ge(f_act, 3)
            dve.wait_ge(f_dve, 2)
            nc.vector.tensor_tensor(fa[:, :], fmin[:, :], flog[:, :], ALU.subtract).then_inc(f_dve, 1)
            dve.wait_ge(f_dve, 3)
            nc.vector.tensor_tensor_scan(cum[:, P:SEG], fones[:, P:SEG], fa[:, P:SEG], 0.0, ALU.mult,
                                         ALU.add).then_inc(f_dve, 1)
            dve.wait_ge(f_dve, 4)
            nc.vector.tensor_tensor_scan(cum[:, 0:P], fones[:, 0:P], fa[:, 0:P], cum[:, SEG - 1:SEG], ALU.mult,
                                         ALU.add).then_inc(f_dve, 1)
            dve.wait_ge(f_dve, 5)
            nc.vector.tensor_tensor_scan(cum[:, SEG:T], fones[:, SEG:T], fa[:, SEG:T], cum[:, P - 1:P], ALU.mult,
                                         ALU.add).then_inc(f_dve, 1)

        def dve_head_norm(dve, t):
            dst, width, col = qk_tile(t)
            root = sg if t % 2 else tu
            dve.wait_ge(qk_sd, t + 1)
            if t:
                dve.wait_ge(qk_n, t)
            nc.vector.reciprocal(hd[:, 0:width], root[:, 0:width]).then_inc(qk_r, 1)
            dve.wait_ge(qk_r, t + 1)
            nc.vector.scalar_tensor_tensor(dst, dst, vecs[:, col:col + 1], hd[:, 0:width], ALU.mult,
                                           ALU.mult).then_inc(qk_n, 1)

        def dve_scores(dve, u):
            h = unit(u)[3]
            s, a, out = small[:, u % 2, :], att[:, u % 2, :], ps[4 + u % 2]
            if u < 8:
                if u == 0:
                    dve.wait_ge(cq_copied, 1)
                    dve.wait_ge(ck_copied, HEADS)
                    dve.wait_ge(mask_set, 4)
                    dve.wait_ge(qk_n, QKT)
                nc.vector.scalar_tensor_tensor(bm[:, 0:SEG], ckb[:, h, 0:SEG], cq[:, h:h + 1], mask[:, 0:SEG],
                                               ALU.add, ALU.add).then_inc(at_bias, 1)
                nc.vector.scalar_tensor_tensor(bm[:, SEG:], ckb[:, h, :], cq[:, HEADS + h:HEADS + h + 1],
                                               mask[:, SEG:], ALU.add, ALU.add).then_inc(at_bias, 1)
                dve.wait_ge(at_bias, 2 * u + 2)
                bias, least = bm[:, :], (-3.0e38, -3.0e38)
            else:
                if u == 8:
                    dve.wait_ge(rel_in, 80)
                bias, least = rel[:, h, :], (vecs[:, V_SINK + h:V_SINK + h + 1],) * 2
            dve.wait_ge(at_s, u + 1)
            if u >= 2:
                dve.wait_ge(at_tr, u - 1)
            nc.vector.tensor_tensor_reduce(a[:, 0:SEG], out[:, 0:SEG], bias[:, 0:SEG], 1.0, least[0], ALU.add,
                                           ALU.max, s[:, 0:1]).then_inc(at_max, 1)
            nc.vector.tensor_tensor_reduce(a[:, SEG:], out[:, SEG:SEG + T], bias[:, SEG:], 1.0, least[1], ALU.add,
                                           ALU.max, s[:, 1:2]).then_inc(at_max, 1)
            dve.wait_ge(at_max, 2 * u + 2)
            nc.vector.tensor_scalar(s[:, 2:4], s[:, 0:2], -1.0, None, ALU.mult).then_inc(at_neg, 1)

        def dve_probs(dve, u):
            s, a = small[:, u % 2, :], att[:, u % 2, :]
            dve.wait_ge(at_exp, exps(u))
            if u >= 8:
                nc.vector.tensor_tensor(s[:, 4:6], s[:, 4:6], s[:, 8:10], ALU.add).then_inc(at_sum, 1)
                dve.wait_ge(at_sum, u - 7)
            nc.vector.reciprocal(s[:, 6:8], s[:, 4:6]).then_inc(at_inv, 1)
            dve.wait_ge(at_inv, u + 1)
            nc.vector.tensor_scalar(a[:, 0:SEG], a[:, 0:SEG], s[:, 6:7], None, ALU.mult).then_inc(at_norm, 1)
            nc.vector.tensor_scalar(a[:, SEG:], a[:, SEG:], s[:, 7:8], None, ALU.mult).then_inc(at_norm, 1)

        bc, bg = first["branch"]

        def pe_branch(pe):
            for m in range(KT):
                pe.wait_ge(w_lo, bc + m + 1)
                for br in range(2):
                    out = start_group(pe, bg, 2, m, br)
                    if m == 0:
                        pe.wait_ge(o_lo, 4 * br + 4)
                    mm = strip(out[:, 0:NX], (bc + m) % RING, 4, lambda t: oy_hi[:, 4 * br + t, :],
                               lambda t: oy_lo[:, 4 * br + t, :], at=4 * br)
                mm.then_inc(pe_done, 1)

        def act_branch(act):
            for m in range(KT):
                split_hi(act, bc, 1, m, LEAD)
                if m == 0:
                    act.wait_ge(acc_free, mg + counts["mix"])
                for br in range(2):
                    nc.scalar.activation(gate[:, 2 * m + br, :], gate[:, 2 * m + br, :], ACT.Sigmoid).then_inc(sig_done, 1)
                act.wait_ge(y_step, m + 1)
                nc.scalar.activation(oy_hi[:, 8 + m, :], hd[:, 0:NX], ACT.Copy).then_inc(y_hi, 1)

        def dve_branch(dve):
            def low(m):
                dve.wait_ge(y_hi, m + 1)
                nc.vector.tensor_tensor(oy_lo[:, 8 + m, :], hd[:, 0:NX], oy_hi[:, 8 + m, :], ALU.subtract).then_inc(y_lo, 1)

            for m in range(KT):
                dve.wait_ge(pe_done, bc + m + 1)
                dve.wait_ge(sig_done, 2 * m + 2)
                if m:
                    dve.wait_ge(y_step, m)
                for br, dst in enumerate((tg, tu)):
                    nc.vector.tensor_tensor(dst[:, 0:NX], ps[banks[bg + 2 * m + br]][:, 0:NX], gate[:, 2 * m + br, :],
                                            ALU.mult).then_inc(acc_free, 1)
                if m:
                    low(m - 1)
                dve.wait_ge(acc_free, bg + 2 * m + 2)
                if m:
                    dve.wait_ge(y_lo, m)
                nc.vector.tensor_tensor(hd[:, 0:NX], tg[:, 0:NX], tu[:, 0:NX], ALU.add).then_inc(y_step, 1)
                split_lo(dve, bc, 1, m, LEAD)
            low(KT - 1)

        sc, sgrp = first["mixb"]
        STEPS = 36
        TAPS_PER_STEP = 5
        RET0 = 20
        MEM0 = 4

        def pe_mixb(pe):
            for q in range(STEPS):
                c, g = sc + q, sgrp + q
                pe.wait_ge(w_lo, c + 1)
                out = start_group(pe, sgrp, 1, q, 0)
                s = c % RING
                if 12 <= q < 16 or q >= 28:
                    src = (xhi, xlo) if q < 16 else (mem_hi, mem_lo)
                    for tt in range(2):
                        mm = rows(out[:, tt * P:(tt + 1) * P], s, *src, tt * P)
                elif q < 20:
                    hi, lo = x_rhs("packed")
                    mm = strip(out[:, 0:NX], s, KT, hi, lo, before=wait_x(pe, N_MIXB) if q == 0 else None)
                else:
                    if q == 20:
                        pe.wait_ge(m_lo, KT)
                    mm = strip(out[:, 0:NX], s, KT, lambda t: mem_hi[:, t, :], lambda t: mem_lo[:, t, :])
                mm.then_inc(pe_done, 1)
                if q == 0:
                    pe_stat(pe, N_MIXB, KT - 1, False)
                if q == 2:
                    pe.wait_ge(norm_r, N_MIXB + 1)
                    for tt in range(2):
                        mm = nc.tensor.matmul(ps[5][:, tt:tt + 1], rstd[0:1, tt * P:(tt + 1) * P], ones[0:1, 0:1],
                                              start=True, stop=True)
                    mm.then_inc(rt_mm, 1)
                if MEM0 < q <= MEM0 + KT:
                    e = q - MEM0 - 1
                    pe.wait_ge(m_sq, e + 1)
                    if e == 0:
                        pe.wait_ge(norm_sd, N_MIXB + 1)
                    nc.tensor.matmul(ps[4][:, 0:NX], ones[:, :], msq[:, e % 2, :], start=e == 0,
                                     stop=e == KT - 1).then_inc(m_stat, 1)
                if 9 <= q < 13:
                    e = q - 9
                    pe.wait_ge(acc_free, sgrp + 8 + e + 1)
                    if e >= 2:
                        pe.wait_ge(rot_step, 3 * (e - 2) + 2)
                    nc.tensor.matmul(ps[6 + e % 2][:, 0:NX], swap[:, :], qr[:, e, :], start=True, stop=True).then_inc(rot_mm, 1)
                if q == 16:
                    pe.wait_ge(m_r, 1)
                    pe.wait_ge(rt_copied, 2)
                    for tt in range(2):
                        mm = nc.tensor.matmul(ps[5][:, tt:tt + 1], memr[0:1, tt * P:(tt + 1) * P], ones[0:1, 0:1],
                                              start=True, stop=True)
                    mm.then_inc(rt_mm, 1)
                if q >= RET0:
                    pe_retention(pe, q - RET0)
            pe_conv_sums(pe)

        def pe_retention(pe, r):
            if r < HEADS:
                b = RDK * (r % 4)
                if r == 0:
                    pe.wait_ge(rot_step, 12)
                    pe.wait_ge(m_sd, 1)
                    pe.wait_ge(rt_copied, 3)
                if r >= 2:
                    pe.wait_ge(ra_dec, r - 1)
                out = ps[4 + r % 2]
                qh, kh = qr[b:b + RDK, r // 4, :], qr[b:b + RDK, 2 + r // 4, :]
                nc.tensor.matmul(out[:, 0:NX], kh[:, 0:P], qh[:, :], start=True, stop=True)
                nc.tensor.matmul(out[:, NX:NX + P], kh[:, P:NX], qh[:, P:NX], start=True, stop=True).then_inc(ra_mm, 1)
            if 1 <= r <= HEADS:
                h = r - 1
                b = HD * (h % 2)
                pe.wait_ge(ra_dec, h + 1)
                if h >= 2 and h % 2 == 0:
                    pe.wait_ge(ry_copied, h // 2)
                a = amat[:, h % 2, :]
                nc.tensor.matmul(ps[6][b:b + HD, 0:NX], v2[:, 0, h * HD:(h + 1) * HD], a[:, 0:NX], start=True, stop=False)
                nc.tensor.matmul(ps[6][b:b + HD, P:NX], v2[:, 1, h * HD:(h + 1) * HD], a[:, NX:NX + P], start=False,
                                 stop=True).then_inc(ry_mm, 1)
            if r >= 3 and r % 2 == 1 and (r - 3) // 2 < 4:
                t = (r - 3) // 2
                pe.wait_ge(ry_copied, t + 1)
                if t:
                    pe.wait_ge(gn_sd, t)
                nc.tensor.matmul(ps[7][:, 0:NX], same[:, :], yr[:, t % 2, :], start=True, stop=True).then_inc(gn_mu, 1)
            if r >= 4 and r % 2 == 0 and (r - 4) // 2 < 4:
                t = (r - 4) // 2
                pe.wait_ge(gn_sq, t + 1)
                nc.tensor.matmul(ps[7][:, NX:512], same[:, :], msq[:, t % 2, :], start=True, stop=True).then_inc(gn_var, 1)

        def pe_conv_sums(pe):
            pe.wait_ge(conv_step, 4 * TAPS)
            pe.wait_ge(gn_sd, 4)
            pe.wait_ge(gn_cen, 4)
            for t in range(4):
                mm = nc.tensor.matmul(ps[7][:, 0:NX], ones[:, :], cy[:, t, :], start=t == 0, stop=t == 3)
            mm.then_inc(ln_mu, 1)
            for t in range(4):
                pe.wait_ge(ln_sq, t + 1)
                nc.tensor.matmul(ps[6][:, 0:NX], ones[:, :], msq[:, t % 2, :], start=t == 0, stop=t == 3).then_inc(ln_var, 1)

        def act_mixb(act):
            for q in range(STEPS):
                split_hi(act, sc, 1, q, LEAD)
                if q == 0:
                    act_norm(act, N_MIXB, False)
                if q == 1:
                    act.wait_ge(angle_step, ANGLE_STEPS)
                    nc.scalar.activation(sinv[:, :], angle[:, :], ACT.Sin).then_inc(cs_act, 1)
                    nc.scalar.activation(cosv[:, :], angle[:, :], ACT.Sin, scale=0.5).then_inc(cs_act, 1)
                if q < 8 and q % 2 == 0:
                    act.wait_ge(acc_free, sgrp + q + 1)
                    nc.scalar.activation(sg[:, 0:NX], tg[:, 0:NX], ACT.Sigmoid).then_inc(cb_sig, 1)
                if MEM0 <= q < MEM0 + KT:
                    e = q - MEM0
                    if e == 0:
                        act.wait_ge(mem_in, 16)
                    nc.scalar.activation(mem_hi[:, e, :], mem[:, e, :], ACT.Copy, scale=gain(N_MEM, e)).then_inc(m_hi, 1)
                    if e >= 2:
                        act.wait_ge(m_stat, e - 1)
                    nc.scalar.activation(msq[:, e % 2, :], mem[:, e, :], ACT.Square).then_inc(m_sq, 1)
                if q == 14:
                    act.wait_ge(m_stat, KT)
                    nc.scalar.activation(memsd[:, :], ps[4][:, 0:NX], ACT.Sqrt, bias=epsc[:, 0:1],
                                         scale=1.0 / D).then_inc(m_sd, 1)
                if 16 <= q < 20:
                    act.wait_ge(acc_free, sgrp + q + 1)
                    src = tu if q % 2 else tg
                    nc.scalar.activation(rg[:, q - 16, :], src[:, 0:NX], ACT.Silu).then_inc(rg_done, 1)
                if q >= RET0:
                    act_retention(act, q - RET0)
            for t in range(4):
                act.wait_ge(ln_cen, t + 1)
                if t >= 2:
                    act.wait_ge(ln_var, t - 1)
                nc.scalar.activation(msq[:, t % 2, :], cy[:, t, :], ACT.Square).then_inc(ln_sq, 1)
            act.wait_ge(ln_var, 4)
            nc.scalar.activation(memsd[:, :], ps[6][:, 0:NX], ACT.Sqrt, bias=epsc[:, 0:1], scale=1.0 / CONV).then_inc(ln_sd, 1)
            for t in range(4):
                act.wait_ge(ln_n, t + 1)
                if t >= 2:
                    act.wait_ge(z_lo, 4 + t - 1)
                nc.scalar.activation(zt[:, t % 2, :], cy[:, t, :], ACT.Silu,
                                     bias=vecs[:, V_LNB + t:V_LNB + t + 1]).then_inc(ln_z, 1)
                act.wait_ge(ln_z, t + 1)
                nc.scalar.activation(oz_hi[:, t, :], zt[:, t % 2, :], ACT.Copy).then_inc(z_hi, 1)

        def act_retention(act, r):
            if r >= 4 and r % 2 == 0 and (r - 4) // 2 < 4:
                t = (r - 4) // 2
                act.wait_ge(gn_cen, t + 1)
                if t >= 2:
                    act.wait_ge(gn_var, t - 1)
                nc.scalar.activation(msq[:, t % 2, :], yr[:, t % 2, :], ACT.Square).then_inc(gn_sq, 1)
            if r >= 5 and r % 2 == 1 and (r - 5) // 2 < 4:
                t = (r - 5) // 2
                act.wait_ge(gn_var, t + 1)
                if t:
                    act.wait_ge(gn_r, t)
                nc.scalar.activation(memsd[:, :], ps[7][:, NX:512], ACT.Sqrt, bias=epsc[:, 0:1],
                                     scale=1.0 / HD).then_inc(gn_sd, 1)
            if r >= 6 and r % 2 == 0 and (r - 6) // 2 < 4:
                t = (r - 6) // 2
                act.wait_ge(gn_z, t + 1)
                nc.scalar.activation(oz_hi[:, 4 + t, :], zt[:, t % 2, :], ACT.Copy).then_inc(z_hi, 1)

        def conv_taps(dve, a, b):
            for n in range(a, min(b, 4 * TAPS)):
                t, j = n // TAPS, n % TAPS
                src = glu[:, t, j:j + NX]
                w = convw[:, t * TAPS + j:t * TAPS + j + 1]
                if j == 0:
                    dve.wait_ge(glu_done, t + 1)
                    nc.vector.tensor_scalar(cy[:, t, :], src, w, vecs[:, V_CONVB + t:V_CONVB + t + 1], ALU.mult,
                                            ALU.add).then_inc(conv_step, 1)
                else:
                    dve.wait_ge(conv_step, n)
                    nc.vector.scalar_tensor_tensor(cy[:, t, :], src, w, cy[:, t, :], ALU.mult, ALU.add).then_inc(conv_step, 1)

        def dve_mixb(dve):
            for q in range(STEPS):
                split_lo(dve, sc, 1, q, LEAD)
                if q == 0:
                    dve_norm(dve, N_MIXB, False)
                out = ps[banks[sgrp + q]]
                dve.wait_ge(pe_done, sc + q + 1)
                if q < 8:
                    dst = tu if q % 2 else tg
                    if q % 2 and q > 1:
                        dve.wait_ge(glu_done, q // 2)
                    nc.vector.tensor_tensor(dst[:, 0:NX], out[:, 0:NX], rstd[:, 0:NX], ALU.mult).then_inc(acc_free, 1)
                    if q % 2:
                        dve.wait_ge(cb_sig, q // 2 + 1)
                        dve.wait_ge(acc_free, sgrp + q + 1)
                        nc.vector.tensor_tensor(glu[:, q // 2, TAPS - 1:], tu[:, 0:NX], sg[:, 0:NX],
                                                ALU.mult).then_inc(glu_done, 1)
                elif q < 12:
                    nc.vector.tensor_tensor(qr[:, q - 8, :], out[:, 0:NX], rstd[:, 0:NX], ALU.mult).then_inc(acc_free, 1)
                elif q < 16:
                    col = slice((q - 12) * P, (q - 11) * P)
                    if q == 12:
                        dve.wait_ge(rt_copied, 2)
                    nc.vector.tensor_scalar(v2[:, 0, col], out[:, 0:P], rtok[:, 0:1], None, ALU.mult)
                    nc.vector.tensor_scalar(v2[:, 1, col], out[:, P:NX], rtok[:, 1:2], None, ALU.mult).then_inc(acc_free, 1)
                elif q < 20:
                    dst = tu if q % 2 else tg
                    if q == 17:
                        dve.wait_ge(glu_done, 4)
                    if q >= 18:
                        dve.wait_ge(rg_done, q - 17)
                    nc.vector.tensor_tensor(dst[:, 0:NX], out[:, 0:NX], rstd[:, 0:NX], ALU.mult).then_inc(acc_free, 1)
                elif q < 28:
                    nc.vector.tensor_tensor(km[:, q - 20, :], out[:, 0:NX], memr[:, :], ALU.mult).then_inc(acc_free, 1)
                else:
                    col = slice((q - 28) * P, (q - 27) * P)
                    nc.vector.tensor_scalar(vmem[:, 0, col], out[:, 0:P], rtok[:, 2:3], None, ALU.mult)
                    nc.vector.tensor_scalar(vmem[:, 1, col], out[:, P:NX], rtok[:, 3:4], None, ALU.mult).then_inc(acc_free, 1)
                if q == 2:
                    dve.wait_ge(cs_act, 2)
                    nc.vector.tensor_tensor(cosv[:, :], cosv[:, :], cosv[:, :], ALU.mult).then_inc(cs_dve, 1)
                    dve.wait_ge(cs_dve, 1)
                    nc.vector.tensor_scalar(cosv[:, :], cosv[:, :], -2.0, 1.0, ALU.mult, ALU.add).then_inc(cs_dve, 1)
                if q == 3:
                    dve.wait_ge(rt_mm, 2)
                    nc.vector.tensor_copy(rtok[:, 0:2], ps[5][:, 0:2]).then_inc(rt_copied, 1)
                if MEM0 <= q < MEM0 + KT:
                    e = q - MEM0
                    dve.wait_ge(m_hi, e + 1)
                    nc.vector.scalar_tensor_tensor(mem_lo[:, e, :], mem[:, e, :], gain(N_MEM, e), mem_hi[:, e, :],
                                                   ALU.mult, ALU.subtract).then_inc(m_lo, 1)
                if 10 <= q < 14:
                    e = q - 10
                    dve.wait_ge(rot_mm, e + 1)
                    dve.wait_ge(cs_dve, 2)
                    if e:
                        dve.wait_ge(rot_step, 3 * e)
                    nc.vector.tensor_tensor(qr[:, e, :], qr[:, e, :], cosv[:, :], ALU.mult).then_inc(rot_step, 1)
                    nc.vector.tensor_tensor(hd[:, 0:NX], ps[6 + e % 2][:, 0:NX], sinv[:, :], ALU.mult).then_inc(rot_step, 1)
                    dve.wait_ge(rot_step, 3 * e + 2)
                    nc.vector.tensor_tensor(qr[:, e, :], qr[:, e, :], hd[:, 0:NX], ALU.add).then_inc(rot_step, 1)
                if q == 15:
                    dve.wait_ge(m_sd, 1)
                    nc.vector.reciprocal(memr[:, :], memsd[:, :]).then_inc(m_r, 1)
                if q == 17:
                    dve.wait_ge(rt_mm, 3)
                    nc.vector.tensor_copy(rtok[:, 2:4], ps[5][:, 0:2]).then_inc(rt_copied, 1)
                    dve.wait_ge(rt_copied, 3)
                    dve.wait_ge(m_r, 1)
                if q >= RET0:
                    dve_retention(dve, q - RET0)
                if q >= 2:
                    conv_taps(dve, (q - 2) * TAPS_PER_STEP, (q - 1) * TAPS_PER_STEP)
            dve.wait_ge(ln_mu, 1)
            for t in range(4):
                nc.vector.scalar_tensor_tensor(cy[:, t, :], ps[7][:, 0:NX], -1.0 / CONV, cy[:, t, :], ALU.mult,
                                               ALU.add).then_inc(ln_cen, 1)
            dve.wait_ge(ln_sd, 1)
            nc.vector.reciprocal(hd[:, 0:NX], memsd[:, :]).then_inc(ln_r, 1)
            dve.wait_ge(ln_r, 1)
            for t in range(4):
                nc.vector.scalar_tensor_tensor(cy[:, t, :], cy[:, t, :], vecs[:, V_LNW + t:V_LNW + t + 1], hd[:, 0:NX],
                                               ALU.mult, ALU.mult).then_inc(ln_n, 1)
            for t in range(4):
                dve.wait_ge(z_hi, 4 + t + 1)
                nc.vector.tensor_tensor(oz_lo[:, t, :], zt[:, t % 2, :], oz_hi[:, t, :], ALU.subtract).then_inc(z_lo, 1)

        def dve_retention(dve, r):
            if r < HEADS:
                if r == 0:
                    dve.wait_ge(decay_in, 16)
                dve.wait_ge(ra_mm, r + 1)
                if r >= 2:
                    dve.wait_ge(ry_mm, r - 1)
                nc.vector.tensor_tensor(amat[:, r % 2, :], ps[4 + r % 2][:, 0:384], decay[:, r, :], ALU.mult).then_inc(ra_dec, 1)
            if r >= 2 and r % 2 == 0 and (r - 2) // 2 < 4:
                t = (r - 2) // 2
                dve.wait_ge(ry_mm, 2 * t + 2)
                if t >= 2:
                    dve.wait_ge(gn_z, t - 1)
                nc.vector.tensor_copy(yr[:, t % 2, :], ps[6][:, 0:NX]).then_inc(ry_copied, 1)
            if r >= 3 and r % 2 == 1 and (r - 3) // 2 < 4:
                t = (r - 3) // 2
                dve.wait_ge(gn_mu, t + 1)
                nc.vector.scalar_tensor_tensor(yr[:, t % 2, :], ps[7][:, 0:NX], -1.0 / HD, yr[:, t % 2, :], ALU.mult,
                                               ALU.add).then_inc(gn_cen, 1)
            if r >= 5 and r % 2 == 1 and (r - 5) // 2 < 4:
                t = (r - 5) // 2
                dve.wait_ge(gn_sd, t + 1)
                nc.vector.reciprocal(hd[:, 0:NX], memsd[:, :]).then_inc(gn_r, 1)
                dve.wait_ge(gn_r, t + 1)
                nc.vector.scalar_tensor_tensor(yr[:, t % 2, :], yr[:, t % 2, :], vecs[:, V_GNW + t:V_GNW + t + 1],
                                               hd[:, 0:NX], ALU.mult, ALU.mult).then_inc(gn_n, 1)
                dve.wait_ge(gn_n, t + 1)
                dve.wait_ge(rg_done, t + 1)
                if t >= 2:
                    dve.wait_ge(z_lo, t - 1)
                nc.vector.tensor_tensor(zt[:, t % 2, :], yr[:, t % 2, :], rg[:, t, :], ALU.mult).then_inc(gn_z, 1)
            if r >= 6 and r % 2 == 0 and (r - 6) // 2 < 4:
                t = (r - 6) // 2
                dve.wait_ge(z_hi, t + 1)
                nc.vector.tensor_tensor(oz_lo[:, 4 + t, :], zt[:, t % 2, :], oz_hi[:, 4 + t, :],
                                        ALU.subtract).then_inc(z_lo, 1)

        qc, qg = first["xq"]

        def pe_xattn(pe):
            hi, lo = x_rhs("packed")
            for m in range(KT):
                pe.wait_ge(w_lo, qc + m + 1)
                out = start_group(pe, qg, 1, m, 0)
                strip(out[:, 0:NX], (qc + m) % RING, KT, hi, lo,
                      before=wait_x(pe, N_XATT) if m == 0 else None).then_inc(pe_done, 1)
                if m == 0:
                    pe_stat(pe, N_XATT, KT - 1, False)
                if m >= 3 and m % 2 == 1:
                    pe_xscores(pe, m // 2 - 1)
                if m >= 5 and m % 2 == 1:
                    pe_xturn(pe, m // 2 - 2)
                if m == 7:
                    pe_xvalues(pe, 0)
            pe_xscores(pe, 3)
            pe_xturn(pe, 2)
            pe_xvalues(pe, 1)
            pe_xturn(pe, 3)
            pe_xvalues(pe, 2)
            pe_xvalues(pe, 3)

        def pe_xscores(pe, h):
            pe.wait_ge(acc_free, qg + 2 * h + 2)
            if h == 0:
                pe.wait_ge(norm_sd, N_XATT + 1)
            if h >= 2:
                pe.wait_ge(xs_exp, 2 * (h - 2) + 2)
            out = ps[4 + h % 2]
            for qt in range(2):
                for t in range(2):
                    mm = nc.tensor.matmul(out[:, qt * NX:(qt + 1) * NX], qx[:, 2 * h + t, qt * P:(qt + 1) * P],
                                          km[:, 2 * h + t, :], start=t == 0, stop=t == 1)
            mm.then_inc(xs_s, 1)

        def pe_xturn(pe, h):
            pe.wait_ge(xs_norm, 2 * h + 2)
            if h:
                pe.wait_ge(xs_pt, h)
            p = xatt[:, h % 2, :]
            for t in range(2):
                for qt in range(2):
                    mm = nc.tensor.transpose(ps[6][:, t * NX + qt * P:t * NX + (qt + 1) * P],
                                             p[:, qt * NX + t * P:qt * NX + (t + 1) * P], ident[:, :])
            mm.then_inc(xs_tr, 1)

        def pe_xvalues(pe, h):
            pe.wait_ge(xs_pt, h + 1)
            if h:
                pe.wait_ge(xo_lo, h)
            for dt in range(2):
                col = h * XH_DIM + dt * P
                for t in range(2):
                    mm = nc.tensor.matmul(ps[7][:, dt * NX:(dt + 1) * NX], vmem[:, t, col:col + P],
                                          xpt[:, h % 2, t * NX:(t + 1) * NX], start=t == 0, stop=t == 1)
            mm.then_inc(xs_pv, 1)

        def act_xattn(act):
            for m in range(KT):
                split_hi(act, qc, 1, m, LEAD)
                if m == 0:
                    act_norm(act, N_XATT, False)
                if m >= 3 and m % 2 == 1:
                    act_xexp(act, m // 2 - 1)
                if m >= 5 and m % 2 == 1:
                    act_xcopy(act, m // 2 - 2)
                if m == 7:
                    act_xout(act, 0)
            act_xexp(act, 3)
            act_xcopy(act, 2)
            act_xout(act, 1)
            act_xcopy(act, 3)
            act_xout(act, 2)
            act_xout(act, 3)

        def act_xexp(act, h):
            s = xsmall[:, h % 2, :]
            act.wait_ge(xs_neg, h + 1)
            if h >= 2:
                act.wait_ge(xs_tr, h - 1)
                act.wait_ge(xs_inv, h - 1)
            for qt in range(2):
                nc.scalar.activation(xatt[:, h % 2, qt * NX:(qt + 1) * NX], ps[4 + h % 2][:, qt * NX:(qt + 1) * NX],
                                     ACT.Exp, bias=s[:, 2 + qt:3 + qt], scale=XH_DIM ** -0.5,
                                     accum_out=s[:, 4 + qt:5 + qt]).then_inc(xs_exp, 1)

        def act_xcopy(act, h):
            act.wait_ge(xs_tr, h + 1)
            if h >= 2:
                act.wait_ge(xs_pv, h - 1)
            nc.scalar.activation(xpt[:, h % 2, :], ps[6][:, :], ACT.Copy).then_inc(xs_pt, 1)

        def act_xout(act, h):
            act.wait_ge(xs_pv, h + 1)
            nc.scalar.activation(oz_hi[:, 2 * h:2 * h + 2, :], two(ps[7][:, :]), ACT.Copy).then_inc(xo_hi, 1)

        def dve_xattn(dve):
            for m in range(KT):
                split_lo(dve, qc, 1, m, LEAD)
                if m == 0:
                    dve_norm(dve, N_XATT, False)
                dve.wait_ge(pe_done, qc + m + 1)
                nc.vector.tensor_tensor(qx[:, m, :], ps[banks[qg + m]][:, 0:NX], rstd[:, 0:NX], ALU.mult).then_inc(acc_free, 1)
                if m >= 3 and m % 2 == 1:
                    dve_xmax(dve, m // 2 - 1)
                    dve_xprobs(dve, m // 2 - 1)
                if m == 7:
                    dve_xlow(dve, 0)
            dve_xmax(dve, 3)
            dve_xprobs(dve, 3)
            for h in range(1, 4):
                dve_xlow(dve, h)

        def dve_xmax(dve, h):
            s = xsmall[:, h % 2, :]
            dve.wait_ge(xs_s, h + 1)
            nc.vector.tensor_reduce(s[:, 0:2], two(ps[4 + h % 2][:, :]), AX.X, ALU.max).then_inc(xs_max, 1)
            dve.wait_ge(xs_max, h + 1)
            nc.vector.tensor_scalar(s[:, 2:4], s[:, 0:2], -(XH_DIM ** -0.5), None, ALU.mult).then_inc(xs_neg, 1)

        def dve_xprobs(dve, h):
            s = xsmall[:, h % 2, :]
            dve.wait_ge(xs_exp, 2 * h + 2)
            nc.vector.reciprocal(s[:, 6:8], s[:, 4:6]).then_inc(xs_inv, 1)
            dve.wait_ge(xs_inv, h + 1)
            for qt in range(2):
                a = xatt[:, h % 2, qt * NX:(qt + 1) * NX]
                nc.vector.tensor_scalar(a, a, s[:, 6 + qt:7 + qt], None, ALU.mult).then_inc(xs_norm, 1)

        def dve_xlow(dve, h):
            dve.wait_ge(xo_hi, h + 1)
            nc.vector.tensor_tensor(oz_lo[:, 2 * h:2 * h + 2, :], two(ps[7][:, :]), oz_hi[:, 2 * h:2 * h + 2, :],
                                    ALU.subtract).then_inc(xo_lo, 1)

        uc, ug = first["up"]

        def pe_up(pe):
            hi, lo = x_rhs("packed")

            def body(i, edge):
                for j in range(4):
                    pe.wait_ge(w_lo, uc + 4 * i + j + 1)
                    out = start_group(pe, ug, 4, i, j)
                    head = edge and i == 0 and j == 0
                    strip(out[:, 0:NX], (uc + j) % RING, KT, hi, lo,
                          before=wait_x(pe, N_MLP) if head else None).then_inc(pe_done, 1)
                    if head:
                        pe_stat(pe, N_MLP, KT - 1, False)
            bodies(pe, F2T, 4, body)

        def act_up(act):
            def body(i, edge):
                for j in range(4):
                    split_hi(act, uc, 4, i, j + LEAD)
                    if edge and i == 0 and j == 0:
                        act_norm(act, N_MLP, False)
                    act.wait_ge(up_prod, 4 * i + j + 1)
                    nc.scalar.activation(hid(hid_hi, 4 * i + j, NX), hd[:, 0:NX], ACT.Copy).then_inc(up_hhi, 1)
            bodies(act, F2T, 4, body)

        def dve_up(dve):
            def low(u):
                dve.wait_ge(up_hhi, u + 1)
                nc.vector.tensor_tensor(hid(hid_lo, u, NX), hd[:, 0:NX], hid(hid_hi, u, NX), ALU.subtract).then_inc(up_hlo, 1)

            def body(i, edge):
                for j in range(4):
                    split_lo(dve, uc, 4, i, j + LEAD)
                    head = edge and i == 0 and j == 0
                    if head:
                        dve_norm(dve, N_MLP, False)
                    u = 4 * i + j
                    dve.wait_ge(pe_done, uc + 4 * i + j + 1)
                    if not head:
                        dve.wait_ge(up_prod, u)
                    nc.vector.tensor_tensor(tg[:, 0:NX], ps[banks[ug + j]][:, 0:NX], rstd[:, 0:NX], ALU.mult).then_inc(acc_free, 1)
                    if not head:
                        low(u - 1)
                    dve.wait_ge(acc_free, ug + 4 * i + j + 1)
                    if not head:
                        dve.wait_ge(up_hlo, u)
                    nc.vector.scalar_tensor_tensor(hd[:, 0:NX], tg[:, 0:NX], 0.0, tg[:, 0:NX], ALU.max,
                                                   ALU.mult).then_inc(up_prod, 1)
            bodies(dve, F2T, 4, body)
            low(F2T - 1)

        ffn_rhs = {w: (lambda t, w=w: (hid(hid_hi, t, w), hid(hid_lo, t, w))) for w in (T, NX)}
        block = ctx.enter_context(nc.Block())

        @block.sync
        def _(sp):
            sp.dma_start(raw[:, 0, 0:KT * P], io["w_f1in"][0]).then_inc(w_in[0], 16)
            sp.dma_start(res[:, :, 0:T], io["res"]).then_inc(res_in, 16)
            for name, n, tiles, *_ in PHASES:
                c0 = first[name][0]
                w = io[f"w_{name}"]

                def load(j, i, sp=sp, c0=c0, tiles=tiles, w=w):
                    c = c0 + 4 * i + j
                    if not (isinstance(i, int) and c < RING):
                        sp.wait_ge(w_lo, c - (RING - 1))
                    sp.dma_start(raw[:, (c0 + j) % RING, 0:tiles * P], w[4 * i + j]).then_inc(w_in[(c0 + j) % RING], 16)

                for j in range(4):
                    if c0 + j:
                        load(j, 0)
                if n // 4 > 1:
                    with sp.Fori(1, n // 4) as i:
                        for j in range(4):
                            load(j, i)
                for j in range(n % 4):
                    load(j, n // 4)
            for m in range(KT):
                sp.wait_ge(out_tile, m + 1)
                sp.dma_start(io["out"][:, m, :], outb[:, m, :]).then_inc(out_done, 16)
            sp.wait_ge(out_done, 16 * KT)

        @block.gpsimd
        def _(pool):
            nc.gpsimd.memset(ones[:, :], 1.0).then_inc(ones_set, 1)
            nc.gpsimd.memset(epsc[:, 0:1], EPS).then_inc(ones_set, 1)
            nc.gpsimd.memset(epsc[:, 1:2], HD * EPS).then_inc(ones_set, 1)
            for dst, name in ((same, "same"), (ident, "ident"), (swap, "swap"), (selneg, "selneg"), (convw, "convw")):
                pool.dma_start(dst[:, :], io[name]).then_inc(const_in, 16)
            pool.dma_start(posi[:, :], io["positions"]).then_inc(pos_in, 16)

            step = [0]

            def done(ins):
                step[0] += 1
                ins.then_inc(angle_step, 1)
                pool.wait_ge(angle_step, step[0])

            pool.wait_ge(pos_in, 16)
            pool.wait_ge(gain_in, 32)
            done(nc.gpsimd.tensor_copy(posf[:, :], posi[:, :]))
            done(nc.gpsimd.tensor_scalar(angle[:, :], posf[:, :], vecs[:, V_FREQ:V_FREQ + 1], None, ALU.mult))
            magic = 1.5 * 2.0 ** 23
            for period, bits in ((512 * np.pi, 10), (2 * np.pi, 15)):
                done(nc.gpsimd.tensor_scalar(turns[:, :], angle[:, :], float(1.0 / period), magic, ALU.mult, ALU.add))
                done(nc.gpsimd.tensor_scalar(turns[:, :], turns[:, :], -magic, None, ALU.add))
                rest = float(period)
                for p in range(3):
                    scale = 2.0 ** (np.floor(np.log2(abs(rest))) + 1 - bits)
                    piece = float(np.floor(rest / scale) * scale) if p < 2 else rest
                    rest -= piece
                    done(nc.gpsimd.tensor_scalar(part[:, :], turns[:, :], piece, None, ALU.mult))
                    done(nc.gpsimd.tensor_tensor(angle[:, :], angle[:, :], part[:, :], ALU.subtract))
            done(nc.gpsimd.tensor_scalar(angle[:, :], angle[:, :], 3.1415925, -3.1415925, ALU.min, ALU.max))
            assert step[0] == ANGLE_STEPS

            pool.wait_ge(pe_done, mc)
            nc.gpsimd.memset(table[:, :], NEG).then_inc(table_set, 1)
            pool.wait_ge(table_set, 1)
            pool.dma_start(table[0:BUCKETS, :], io["rel_table"]).then_inc(rel_const, 16)
            pool.dma_start(onehot[:, :], io["onehot"]).then_inc(rel_const, 16)
            nc.gpsimd.memset(mask[:, :], 0.0).then_inc(mask_set, 1)
            pool.wait_ge(mask_set, 1)
            for n, lo in enumerate((0, 2 * SEG)):
                nc.gpsimd.affine_select(out=mask[:, lo:lo + P], in_=mask[:, lo:lo + P], compare_op=ALU.is_ge, fill=NEG,
                                        base=0, pattern=[[-1, P]], channel_multiplier=1).then_inc(mask_set, 1)
                pool.wait_ge(mask_set, n + 2)
            nc.gpsimd.memset(small[:, :, :], 0.0).then_inc(mask_set, 1)
            pool.wait_ge(rel_row, 2)
            pool.dma_start(rel_dram.ap(), relrow[:, :]).then_inc(rel_out, 16)
            pool.wait_ge(rel_out, 16)
            rel_row_size = REL_X + REL_M
            copies = bass.AP(rel_dram, 0, [[0, P], [rel_row_size, HEADS], [1, rel_row_size]])
            pool.dma_start(rel_wide.ap(), copies).then_inc(rel_out, 16)
            pool.wait_ge(rel_out, 32)
            for col, n, start in ((0, P, 255), (P, META, REL_X + 255), (SEG, P, 127), (SEG + P, META, REL_X + 127),
                                  (2 * SEG, P, 255)):
                src = bass.AP(rel_wide, start, [[HEADS * rel_row_size - 1, P], [rel_row_size, HEADS], [1, n]])
                pool.dma_start(rel[:, :, col:col + n], src).then_inc(rel_in, 16)

            pool.wait_ge(pe_done, sc)
            nc.gpsimd.memset(glu[:, :, 0:TAPS - 1], 0.0).then_inc(glu_zero, 1)
            pool.dma_start(mem[:, :, :], io["mem"]).then_inc(mem_in, 16)
            pool.dma_start(decay[:, :, :], io["decay"]).then_inc(decay_in, 16)

        @block.scalar
        def _(act):
            act.dma_start(gains[:, :], io["gains"]).then_inc(gain_in, 16)
            act.dma_start(vecs[:, :], io["vecs"]).then_inc(gain_in, 16)
            act.wait_ge(gain_in, 32)
            act.wait_ge(ones_set, 3)
            split_hi(act, 0, 1, 0, 0)
            act.wait_ge(res_in, 16)
            for m in range(KT):
                act_prep(act, N_F1, m, True, True)
                if m in (3, 6):
                    split_hi(act, 0, 1, m // 3, 0)
            act_ff_in(act, "f1in", N_F1, T)
            act_residual(act, "f1out", N_MIX, True, 2)
            act_mix(act)
            act_branch(act)
            act_residual(act, "wo", N_F2, False, 1)
            act_ff_in(act, "f2in", N_F2, NX)
            act_residual(act, "f2out", N_MIXB, False, 2)
            act_mixb(act)
            act_residual(act, "wo2", N_XATT, False, 1)
            act_xattn(act)
            act_residual(act, "xo", N_MLP, False, 1)
            act_up(act)
            act_residual(act, "down", N_FINAL, False, 4, prep=False)
            act_norm(act, N_FINAL, False)

        @block.vector
        def _(dve):
            split_lo(dve, 0, 1, 0, 0)
            dve.wait_ge(gain_in, 32)
            for m in range(KT):
                dve_prep(dve, N_F1, m, True)
                if m in (3, 6):
                    split_lo(dve, 0, 1, m // 3, 0)
            dve_ff_in(dve, "f1in", N_F1, T)
            dve_residual(dve, "f1out", N_MIX, True, 2, 0.5)
            dve_mix(dve)
            dve_branch(dve)
            dve_residual(dve, "wo", N_F2, False, 1, 1.0)
            dve_ff_in(dve, "f2in", N_F2, NX)
            dve_residual(dve, "f2out", N_MIXB, False, 2, 0.5)
            dve.wait_ge(glu_zero, 1)
            dve.wait_ge(const_in, 80)
            dve_mixb(dve)
            dve_residual(dve, "wo2", N_XATT, False, 1, 1.0)
            dve_xattn(dve)
            dve_residual(dve, "xo", N_MLP, False, 1, 1.0)
            dve_up(dve)
            dve_residual(dve, "down", N_FINAL, False, 4, 1.0, prep=False)
            dve_norm(dve, N_FINAL, False)
            for m in range(KT):
                nc.vector.scalar_tensor_tensor(two(outb[:, m, :]), res_tile(m, False), gain(N_FINAL, m),
                                               two(rstd[:, 0:NX]), ALU.mult, ALU.mult).then_inc(out_tile, 1)

        @block.tensor
        def _(pe):
            pe.wait_ge(ones_set, 3)
            for m in range(KT - 1):
                pe_stat(pe, N_F1, m, True)
            pe_ff_in(pe, "f1in", N_F1, T)
            pe_residual(pe, "f1out", N_MIX, True, 2, ffn_rhs[T], lambda k: pe.wait_ge(ffs["f1"]["hlo"], k + 1))
            pe.wait_ge(const_in, 80)
            pe_mix(pe)
            pe_branch(pe)
            pe_residual(pe, "wo", N_F2, False, 1, lambda t: (oy_hi[:, 8 + t, :], oy_lo[:, 8 + t, :]),
                        lambda k: pe.wait_ge(y_lo, k + 1))
            pe_ff_in(pe, "f2in", N_F2, NX)
            pe_residual(pe, "f2out", N_MIXB, False, 2, ffn_rhs[NX], lambda k: pe.wait_ge(ffs["f2"]["hlo"], k + 1))
            pe_mixb(pe)
            pe_residual(pe, "wo2", N_XATT, False, 1, lambda t: (oz_hi[:, t, :], oz_lo[:, t, :]),
                        lambda k: pe.wait_ge(z_lo, 8 if k < 4 else 4))
            pe_xattn(pe)
            pe_residual(pe, "xo", N_MLP, False, 1, lambda t: (oz_hi[:, t, :], oz_lo[:, t, :]),
                        lambda k: pe.wait_ge(xo_lo, k // 2 + 1))
            pe_up(pe)
            pe_residual(pe, "down", N_FINAL, False, 4, ffn_rhs[NX], lambda k: pe.wait_ge(up_hlo, k + 1))
            pe_stat(pe, N_FINAL, KT - 1, False)


def shape_constants():
    eye = np.eye(P, dtype=np.float32)
    block = np.kron(np.eye(2), np.ones((HD, HD))).astype(np.float32)
    half = RDK // 2
    swap = np.zeros((P, P), np.float32)
    for h in range(P // RDK):
        for i in range(half):
            swap[h * RDK + half + i, h * RDK + i] = -1.0
            swap[h * RDK + i, h * RDK + half + i] = 1.0
    selneg = np.zeros((HEADS, HEADS, P), np.float32)
    for h in range(HEADS):
        selneg[h, h, :] = -1.0
    freq = np.float32(10000.0) ** (-np.arange(half, dtype=np.float32) / np.float32(half))
    freq = np.tile(freq, P // half).astype(np.float32).reshape(P, 1)

    def bucket(d):
        small = BUCKETS // 2
        large = small + int(np.log(max(d, 1) / small) / np.log(128 / small) * (BUCKETS - small) + 1e-9)
        return max(d, 0) if d < small else min(large, BUCKETS - 1)

    onehot = np.zeros((BUCKETS + 1, REL_X + REL_M), np.float32)
    for v in range(REL_X):
        d = 255 - v
        onehot[bucket(d) if 0 <= d < WINDOW else BUCKETS, v] = 1.0
    for v in range(REL_M):
        onehot[bucket(271 - v), REL_X + v] = 1.0
    log_g = np.log1p(-np.exp2(-5.0 - np.arange(HEADS)))
    j, i = np.arange(P)[:, None], np.arange(NX)[None, :]
    seen = j // HD <= i // HD
    full = np.exp(log_g[:, None, None] * np.abs(i - j)) * seen * RDK ** -0.5
    decay = np.concatenate([full, full[:, :, 0:P]], axis=2).transpose(1, 0, 2)
    return {"ident": eye, "same": block, "swap": swap, "selneg": selneg.reshape(HEADS, HEADS * P), "freq": freq,
            "onehot": onehot, "decay": np.ascontiguousarray(decay.astype(np.float32))}


def strips(w, tiles=KT):
    k, m = w.shape
    a = w.reshape(k // P // tiles, tiles, P, m // P, P).transpose(3, 0, 2, 1, 4)
    return a.reshape(-1, P, tiles * P)


def kernel(**inputs):
    import concourse.bacc as bacc
    from concourse.bass_utils import run_bass_kernel_spmd as run

    a = {k: np.asarray(v) for k, v in inputs.items()}
    const = shape_constants()

    def turns(x, y):
        return np.stack([strips(x), strips(y)], axis=1).reshape(-1, P, KT * P)

    def columns(v):
        return v.reshape(-1, P).T

    arrays = {}
    for f, name in (("f1", "ffn1"), ("f2", "ffn2")):
        w_in, w_out = a[f"{name}_w_in"][0], a[f"{name}_w_out"][0]
        arrays[f"w_{f}in"] = turns(w_in[:, :FF], w_in[:, FF:])
        arrays[f"w_{f}out"] = strips(w_out, WIDE)
    w = a["w_in"][0]
    cut = np.cumsum([512, 512, 512, HEADS, 512, 128, 128, D])
    fq, fk, fv, ff, sq_, sk, sv, ga, gb = np.split(w, cut, axis=1)
    forget = np.zeros((D, P), w.dtype)
    forget[:, :HEADS] = ff
    order = np.concatenate([np.arange(HD) + HD * h for t in range(4) for h in (t, t + 4)])
    arrays["w_mix"] = np.concatenate([strips(x) for x in (forget, fk, fq, sk, sq_[:, order], fv, sv)] + [turns(ga, gb)])
    arrays["w_branch"] = np.concatenate([strips(a["w_branch_fox"][0], 4), strips(a["w_branch_swa"][0][order], 4)], axis=2)
    arrays["w_wo"] = strips(a["w_out"][0])
    w = a["w_in_2"]
    ca, cb, rq, rk, rv, rg = np.split(w, np.cumsum([512, 512, 256, 256, 512]), axis=1)
    arrays["w_mixb"] = np.concatenate([turns(cb, ca)] + [strips(x) for x in (rq, rk, rv, rg)])
    arrays["w_xkv"] = strips(a["xkv_w_2"])
    arrays["w_wo2"], arrays["w_xq"], arrays["w_xo"] = (strips(a[k]) for k in ("w_out_2", "xq_w_2", "xo_w_2"))
    arrays["w_up"], arrays["w_down"] = strips(a["mlp_up_w_2"]), strips(a["mlp_down_w_2"])

    x, meta = a["x"][0], a["meta_tokens"]
    tokens = np.concatenate([x[:P], meta, x[P:]])
    arrays["res"] = tokens.T.reshape(KT, P, T).transpose(1, 0, 2)
    arrays["mem"] = a["mem_2"][0].T.reshape(KT, P, NX).transpose(1, 0, 2)
    arrays["gains"] = np.concatenate([columns(a[k].reshape(-1)) for k in (
        "ffn1_norm", "mix_norm", "ffn2_norm", "norm_mix_w_2", "norm_xattn_w_2", "norm_mlp_w_2", "norm_f_w_2",
        "norm_mem_w_2")], axis=1)
    twice = [np.tile(a[k][0], 2).reshape(P, 1) for k in ("fox_q_norm", "fox_k_norm", "swa_q_norm", "swa_k_norm")]
    fbias = np.zeros((P, 1), np.float32)
    fbias[:HEADS, 0] = a["forget_bias"][0]
    arrays["vecs"] = np.concatenate(twice + [fbias, const["freq"]] + [
        columns(a[k]) for k in ("conv_b_2", "conv_ln_w_2", "conv_ln_b_2", "ret_gn_w_2")
    ] + [np.broadcast_to(a["swa_sinks"][0], (P, HEADS))], axis=1)
    arrays["convw"] = a["conv_w_2"].T.reshape(4, P, TAPS).transpose(1, 0, 2).reshape(P, 4 * TAPS)
    arrays["positions"] = np.broadcast_to(a["positions_2"].reshape(1, NX), (P, NX))
    arrays["rel_table"] = a["rel_bias_table"]
    for k in ("ident", "same", "swap", "selneg", "onehot", "decay"):
        arrays[k] = const[k]

    nc = bacc.Bacc("TRN2", target_bir_lowering=False, num_devices=1)
    arrays = {f"in_{k}": np.ascontiguousarray(v) for k, v in arrays.items()}
    io = {k[3:]: nc.dram_tensor(k, v.shape, mybir.dt.from_np(v.dtype), kind="ExternalInput").ap()
          for k, v in arrays.items()}
    io["out"] = nc.dram_tensor("out", (P, KT, NX), F32, kind="ExternalOutput").ap()
    build(nc, io)
    got = run(nc, [arrays], core_ids=[0]).results[0]["out"]
    return np.ascontiguousarray(got.transpose(2, 1, 0).reshape(1, NX, D))
```

```python
from contextlib import ExitStack

import numpy as np

import concourse.bass as bass
from concourse import mybir

F32 = mybir.dt.float32
F32R = mybir.dt.float32r
I32 = mybir.dt.int32
ALU = mybir.AluOpType
ACT = mybir.ActivationFunctionType
AX = mybir.AxisListType

P = 128
D = 1024
KT = D // P
NX = 256
META = 16
T = NX + META
SEG = P + META
W2 = 2 * SEG
FF = 2816
FT = FF // P
FF2 = 4096
F2T = FF2 // P
HEADS = 8
HD = 64
EPS = 1e-6
NEG = -1e30
WINDOW = 128
BUCKETS = 32
CONV = 512
TAPS = 31
XH_DIM = 256
XHEADS = 4
RDK = 32
RING = 4
LEAD = 3
WIDE = 11

PHASES = [
    ("f1in", 2 * FT, KT, 2 * FT, 4), ("f1out", 2 * KT, WIDE, KT, 2),
    ("mix", 35, KT, 35, 3), ("branch", KT, KT, 2 * KT, 4), ("wo", KT, KT, KT, 4),
    ("f2in", 2 * FT, KT, 2 * FT, 4), ("f2out", 2 * KT, WIDE, KT, 2),
    ("mixb", 20, KT, 20, 3), ("memk", KT, KT, KT, 3), ("wo2", KT, KT, KT, 4),
    ("xq", KT, KT, KT, 3), ("memv", KT, KT, KT, 3), ("xo", KT, KT, KT, 4),
    ("up", F2T, KT, F2T, 4), ("down", 4 * KT, KT, KT, 2),
]
V_FOXQ, V_FOXK, V_SWAQ, V_SWAK, V_FBIAS, V_FREQ, V_CONVB, V_LNW, V_LNB, V_GNW, V_SINK = (
    0, 1, 2, 3, 4, 5, 6, 10, 14, 18, 22)
V_COLS = V_SINK + HEADS
N_F1, N_MIX, N_F2, N_MIXB, N_XATT, N_MLP, N_FINAL, N_MEM = range(8)

ANGLE_STEPS = 19
REL_X = 384
REL_M = 272


def plan():
    first, sizes, banks = {}, [], []
    for name, n, tiles, groups, ring in PHASES:
        first[name] = (len(sizes), len(banks))
        sizes += [tiles] * n
        banks += [(len(banks) + i) % ring for i in range(groups)]
    need = [max([p + 1 for p in range(g) if banks[p] == b], default=0) for g, b in enumerate(banks)]
    return first, sizes, banks, need


def build(nc, io):
    first, sizes, banks, need = plan()
    C = len(sizes)
    counts = {name: n for name, n, *_ in PHASES}

    ctx = ExitStack()
    with ctx:
        def sem(name):
            return ctx.enter_context(nc.semaphore(name))

        top = [((nc.sbuf_base + 63) // 64) * 64]

        def place(name, shape, dt=F32, at=None):
            size = int(np.prod(shape[1:])) * 4
            size = (size + 31) // 32 * 32
            where = top[0] if at is None else at[0]
            t = nc.alloc_sbuf_tensor_at(name, shape, dt, offset=where)
            if at is None:
                top[0] += size
            else:
                at[0] += size
                assert at[0] <= nc.sbuf_usable_end, (name, at[0])
            return t

        raw = place("raw", [P, RING, WIDE * P])
        whi = place("whi", [P, RING, WIDE * P], F32R)
        wlo = place("wlo", [P, RING, WIDE * P], F32R)
        xhi = place("xhi", [P, KT, W2], F32R)
        xlo = place("xlo", [P, KT, W2], F32R)
        res = place("res", [P, KT, W2])
        ones = place("ones", [P, P])
        same = place("same_head", [P, P])
        ident = place("ident", [P, P])
        swap = place("swap", [P, P])
        selneg = place("selneg", [HEADS, HEADS * P])
        gains = place("gains", [P, 8 * KT])
        vecs = place("vecs", [P, V_COLS])
        convw = place("convw", [P, 4 * TAPS])
        epsc = place("epsc", [P, 2])
        rstd = place("rstd", [P, W2])
        root = place("root", [P, 4])
        inv = place("inv", [P, 4])
        work_at = top[0]
        sq = place("sq", [P, 2, W2])
        tg = place("tg", [P, W2])
        tu = place("tu", [P, W2])
        sg = place("sg", [P, W2])
        hd = place("hd", [P, W2])
        qk_root = place("qk_root", [P, 2, 6])
        qk_inv = place("qk_inv", [P, 2, 6])
        angle = place("angle", [P, NX])
        area = top[0]

        at = [area]
        hid_hi = place("hid_hi", [P, F2T * NX], F32R, at)
        hid_lo = place("hid_lo", [P, F2T * NX], F32R, at)

        at = [area]
        oy_hi = place("oy_hi", [P, 16, NX], F32R, at)
        oy_lo = place("oy_lo", [P, 16, NX], F32R, at)
        qn = place("qn", [P, 8, NX], F32, at)
        kn = place("kn", [P, 5, T], F32, at)
        v0 = place("v0", [P, 640], F32, at)
        v1 = place("v1", [P, 640], F32, at)
        vm = place("vm", [META, 640], F32, at)
        gate_at = at[0]
        gate = place("gate", [P, 16, NX], F32, at)
        ckb = place("ckb", [P, HEADS, T], F32, at)
        rel = place("rel", [P, HEADS, SEG + T], F32, at)
        att = place("att", [P, 2, SEG + T], F32, at)
        mask = place("mask", [P, SEG + T], F32, at)
        cq = place("cq", [P, 16], F32, at)
        qk_wide = place("qk_wide", [P, 2, 6 * HD], F32, at)
        small = place("small", [P, 2, 12], F32, at)
        at = [work_at]
        bm = place("bm", [P, SEG + T], F32, at)
        pts = place("pts", [P, 2, 384], F32, at)
        ptm = place("ptm", [META, 2, NX], F32, at)
        at = [gate_at]
        fa = place("fa", [HEADS, T], F32, at)
        fabs = place("fabs", [HEADS, T], F32, at)
        fexp = place("fexp", [HEADS, T], F32, at)
        fmin = place("fmin", [HEADS, T], F32, at)
        flog = place("flog", [HEADS, T], F32, at)
        fones = place("fones", [HEADS, T], F32, at)
        cum = place("cum", [HEADS, T], F32, at)
        table = place("table", [BUCKETS + 1, HEADS], F32, at)
        onehot = place("onehot", [BUCKETS + 1, REL_X + REL_M], F32, at)
        relrow = place("relrow", [HEADS, REL_X + REL_M], F32, at)
        vt = place("vt", [P, 2, T], F32, at)
        assert at[0] <= gate_at + 16 * NX * 4

        at = [area]
        oz_hi = place("oz_hi", [P, 8, NX], F32R, at)
        oz_lo = place("oz_lo", [P, 8, NX], F32R, at)
        mem_hi = place("mem_hi", [P, KT, NX], F32R, at)
        mem_lo = place("mem_lo", [P, KT, NX], F32R, at)
        mem_at = at[0]
        mem = place("mem", [P, KT, NX], F32, at)
        glu_at = at[0]
        glu = place("glu", [P, 4, TAPS - 1 + NX], F32, at)
        cy = place("cy", [P, 4, NX], F32, at)
        qr = place("qr", [P, 4, NX], F32, at)
        v2 = place("v2", [P, 2, 512], F32, at)
        rg = place("rg", [P, 4, NX], F32, at)
        cosv = place("cosv", [P, NX], F32, at)
        sinv = place("sinv", [P, NX], F32, at)
        vmem = place("vmem", [P, 2, D], F32, at)
        amat = place("amat", [P, 2, 384], F32, at)
        yr = place("yr", [P, 2, NX], F32, at)
        zt = place("zt", [P, 2, NX], F32, at)
        csq = place("csq", [P, 4, NX], F32, at)
        memr = place("memr", [P, NX], F32, at)
        col_root = place("col_root", [P, 3, 4], F32, at)
        col_inv = place("col_inv", [P, 3, 4], F32, at)
        msq = place("msq", [P, 2, NX], F32, at)
        decay_at = at[0]
        decay = place("decay", [P, HEADS, 384], F32, at)
        at = [mem_at]
        km = place("km", [P, KT, NX], F32, at)
        at = [glu_at]
        qx = place("qx", [P, KT, NX], F32, at)
        at = [decay_at]
        xatt = place("xatt", [P, XHEADS, 512], F32, at)
        xpt = place("xpt", [P, 2, 512], F32, at)
        xsmall = place("xsmall", [P, XHEADS, 8], F32, at)

        at = [area + 2 * F2T * NX * 4]
        posi = place("posi", [P, NX], I32, at)
        posf = place("posf", [P, NX], F32, at)
        turns = place("turns", [P, NX], F32, at)
        part = place("part", [P, NX], F32, at)
        at = [area]
        outb = place("outb", [P, KT, NX], F32, at)

        ps = [ctx.enter_context(nc.psum_tensor(f"bank{i}", [P, 512], F32)) for i in range(8)]
        STAT = ps[4]

        rel_dram = nc.dram_tensor("rel_rows", (HEADS, REL_X + REL_M), F32, kind="Internal")
        rel_wide = nc.dram_tensor("rel_copies", (P, HEADS, REL_X + REL_M), F32, kind="Internal")

        w_in = [sem(f"w_in{s}") for s in range(RING)]
        w_hi = sem("w_hi")
        w_lo = sem("w_lo")
        pe_done = sem("pe_done")
        acc_free = sem("acc_free")
        x_hi, x_lo = sem("x_hi"), sem("x_lo")
        sq_ready = sem("sq_ready")
        stat_mm = sem("stat_mm")
        norm_sd, norm_inv, norm_bc, norm_r = (sem(s) for s in ("norm_sd", "norm_inv", "norm_bc", "norm_r"))
        res_even, res_odd = sem("res_even"), sem("res_odd")
        gain_in, ident_in = sem("gain_in"), sem("ident_in")
        const_in, pos_in = sem("const_in"), sem("pos_in")
        ones_set, mask_set = sem("ones_set"), sem("mask_set")
        angle_step = sem("angle_step")
        ffs = {f: {s: sem(f"{f}_{s}") for s in ("silu", "prod", "hhi", "hlo")} for f in ("f1", "f2")}
        up_prod, up_hhi, up_hlo = sem("up_prod"), sem("up_hhi"), sem("up_hlo")
        out_tile, out_done = sem("out_tile"), sem("out_done")
        qk_sq, qk_ss, qk_sd, qk_r, qk_bc, qk_n = (
            sem(s) for s in ("qk_sq", "qk_ss", "qk_sd", "qk_r", "qk_bc", "qk_n"))
        qk_inv_set = sem("qk_inv_set")
        v_tr, v_copied = sem("v_tr"), sem("v_copied")
        f_act, f_dve = sem("f_act"), sem("f_dve")
        cq_mm, cq_copied, ck_mm, ck_copied = (sem(s) for s in ("cq_mm", "cq_copied", "ck_mm", "ck_copied"))
        table_set, rel_const, rel_mm, rel_row, rel_out, rel_in = (
            sem(s) for s in ("table_set", "rel_const", "rel_mm", "rel_row", "rel_out", "rel_in"))
        at_s, at_bias, at_max, at_neg, at_exp, at_sum, at_inv, at_norm = (
            sem(s) for s in ("at_s", "at_bias", "at_max", "at_neg", "at_exp", "at_sum", "at_inv", "at_norm"))
        at_tr, at_pt, at_pv, o_hi, o_lo = (sem(s) for s in ("at_tr", "at_pt", "at_pv", "o_hi", "o_lo"))
        sig_done, y_step, y_hi, y_lo = (sem(s) for s in ("sig_done", "y_step", "y_hi", "y_lo"))
        decay_in, mem_in, glu_zero = sem("decay_in"), sem("mem_in"), sem("glu_zero")
        cs_act, cs_dve = sem("cs_act"), sem("cs_dve")
        cb_sig, glu_done, conv_step = sem("cb_sig"), sem("glu_done"), sem("conv_step")
        rot_mm, rot_step, rg_done = sem("rot_mm"), sem("rot_step"), sem("rg_done")
        m_hi, m_lo, m_sq, m_stat, m_sd, m_inv, m_bc, m_r = (
            sem(s) for s in ("m_hi", "m_lo", "m_sq", "m_stat", "m_sd", "m_inv", "m_bc", "m_r"))
        rv_tr, rv_copied = sem("rv_tr"), sem("rv_copied")
        ra_mm, ra_dec, ry_mm, ry_copied = (sem(s) for s in ("ra_mm", "ra_dec", "ry_mm", "ry_copied"))
        gn_mu, gn_cen, gn_sq, gn_var, gn_sd, gn_r, gn_bc, gn_n, gn_z = (
            sem(s) for s in ("gn_mu", "gn_cen", "gn_sq", "gn_var", "gn_sd", "gn_r", "gn_bc", "gn_n", "gn_z"))
        ln_mu, ln_cen, ln_sq, ln_var, ln_sd, ln_r, ln_bc, ln_n, ln_z = (
            sem(s) for s in ("ln_mu", "ln_cen", "ln_sq", "ln_var", "ln_sd", "ln_r", "ln_bc", "ln_n", "ln_z"))
        z_hi, z_lo = sem("z_hi"), sem("z_lo")
        c_hi, c_lo = sem("c_hi"), sem("c_lo")
        xv_tr, xv_copied = sem("xv_tr"), sem("xv_copied")
        xs_s, xs_max, xs_neg, xs_exp, xs_inv, xs_norm, xs_tr, xs_pt, xs_pv, xo_hi, xo_lo = (
            sem(s) for s in ("xs_s", "xs_max", "xs_neg", "xs_exp", "xs_inv", "xs_norm", "xs_tr", "xs_pt",
                             "xs_pv", "xo_hi", "xo_lo"))

        def seg(ap):
            return ap.rearrange("p (s t) -> p s t", s=2)[:, :, 0:P]

        def two(ap):
            return ap.rearrange("p (s t) -> p s t", s=2)

        def res_tile(m, full):
            return res[:, m, 0:T] if full else seg(res[:, m, :])

        def x_tile(t, m, full):
            return t[:, m, 0:T] if full else two(t[:, m, 0:NX])

        def flat_or_two(ap, full):
            return ap[:, 0:T] if full else two(ap[:, 0:NX])

        def gain(n, m):
            return gains[:, n * KT + m:n * KT + m + 1] if isinstance(m, int) else gains[:, bass.ds(m + n * KT, 1)]

        def hid(t, j, n):
            return t[:, 0:FT * T].rearrange("p (j t) -> p j t", t=n)[:, j, :] if n == T else \
                t[:, 0:F2T * NX].rearrange("p (j t) -> p j t", t=n)[:, j, :]

        def bodies(eng, n, per, body):
            count = n // per
            body(0, True)
            if count > 3:
                with eng.Fori(1, count - 1) as i:
                    body(i, False)
            else:
                for i in range(1, count - 1):
                    body(i, False)
            if count > 1:
                body(count - 1, True)

        def split_hi(act, c0, per, i, j):
            static = isinstance(i, int)
            c = c0 + per * i + j
            if static and c >= C:
                return
            s = (c if static else c0 + j) % RING
            tiles = sizes[c] if static else sizes[c0 + per + j]
            act.wait_ge(w_in[s], (c // RING + 1) * 16 if static else (per // RING * i + ((c0 + j) // RING + 1)) * 16)
            if not (static and c < RING):
                act.wait_ge(pe_done, c - (RING - 1))
            nc.scalar.activation(whi[:, s, 0:tiles * P], raw[:, s, 0:tiles * P], ACT.Copy).then_inc(w_hi, 1)

        def split_lo(dve, c0, per, i, j):
            static = isinstance(i, int)
            c = c0 + per * i + j
            if static and c >= C:
                return
            s = (c if static else c0 + j) % RING
            tiles = sizes[c] if static else sizes[c0 + per + j]
            dve.wait_ge(w_hi, c + 1)
            nc.vector.tensor_tensor(wlo[:, s, 0:tiles * P], raw[:, s, 0:tiles * P], whi[:, s, 0:tiles * P],
                                    ALU.subtract).then_inc(w_lo, 1)

        def start_group(pe, g0, per, i, j):
            if isinstance(i, int):
                if need[g0 + per * i + j]:
                    pe.wait_ge(acc_free, need[g0 + per * i + j])
            else:
                pe.wait_ge(acc_free, need[g0 + per + j] + per * (i - 1))
            return ps[banks[g0 + (per if not isinstance(i, int) else per * i) + j]]

        def strip(out, s, tiles, rhs_hi, rhs_lo, start=True, stop=True, at=0, before=None):
            for t in range(tiles):
                if before is not None:
                    before(t)
                w = slice((at + t) * P, (at + t + 1) * P)
                nc.tensor.matmul(out, whi[:, s, w], rhs_hi(t), start=start and t == 0, stop=False)
                nc.tensor.matmul(out, whi[:, s, w], rhs_lo(t), start=False, stop=False)
                mm = nc.tensor.matmul(out, wlo[:, s, w], rhs_hi(t), start=False, stop=stop and t == tiles - 1)
            return mm

        def token_sums(out, src, toks, cols, start, stop):
            n = cols.shape[-1]
            for b, tok in enumerate(toks):
                mm = nc.tensor.matmul(out[:, b * n:(b + 1) * n], src[:, tok:tok + P], cols, start=start and b == 0,
                                      stop=stop and b == len(toks) - 1)
            return mm

        def spread(out, values, toks):
            for b, tok in enumerate(toks):
                mm = nc.tensor.matmul(out[:, tok:tok + P], values[:, b:b + 1].to_broadcast([P, P]), ident[:, :],
                                      start=True, stop=True)
            return mm

        def blocks(width):
            return (0, P, SEG) if width == T else (0, P)

        one_col = ones[:, 0:1]
        head_cols = same[:, :].rearrange("p (h d) -> p h d", h=2)[:, :, 0]

        def pe_stat(pe, n, m, full, par=None):
            par = m % 2 if par is None else par
            width = T if full else NX
            pe.wait_ge(sq_ready, m + (KT * n + 1))
            static = isinstance(m, int)
            if static and m == 0 and n:
                pe.wait_ge(norm_r, n)
            token_sums(STAT, sq[:, par, :], blocks(width), one_col, start=static and m == 0,
                       stop=static and m == KT - 1).then_inc(stat_mm, 1)

        def pe_norm(pe, n, full):
            pe.wait_ge(norm_inv, n + 1)
            if n == 0:
                pe.wait_ge(ident_in, 16)
            spread(STAT[:, P:], inv, blocks(T if full else NX)).then_inc(norm_bc, 1)

        def act_prep(act, n, m, full, prep, par=None):
            par = m % 2 if par is None else par
            if not (isinstance(m, int) and KT * n + m < 2):
                act.wait_ge(stat_mm, m + (KT * n - 1))
            if prep:
                nc.scalar.activation(x_tile(xhi, m, full), res_tile(m, full), ACT.Copy,
                                     scale=gain(n, m)).then_inc(x_hi, 1)
            nc.scalar.activation(flat_or_two(sq[:, par, :], full), res_tile(m, full),
                                 ACT.Square).then_inc(sq_ready, 1)

        def dve_prep(dve, n, m, full):
            dve.wait_ge(x_hi, m + (KT * n + 1))
            nc.vector.scalar_tensor_tensor(x_tile(xlo, m, full), res_tile(m, full), gain(n, m),
                                           x_tile(xhi, m, full), ALU.mult, ALU.subtract).then_inc(x_lo, 1)

        def act_norm(act, n, full):
            width = T if full else NX
            nb = len(blocks(width))
            act.wait_ge(stat_mm, KT * (n + 1))
            nc.scalar.activation(root[:, 0:nb], STAT[:, 0:nb], ACT.Sqrt, bias=epsc[:, 0:1],
                                 scale=1.0 / D).then_inc(norm_sd, 1)
            act.wait_ge(norm_bc, n + 1)
            nc.scalar.activation(rstd[:, 0:width], STAT[:, P:P + width], ACT.Copy).then_inc(norm_r, 1)

        def dve_norm(dve, n, full):
            nb = len(blocks(T if full else NX))
            dve.wait_ge(norm_sd, n + 1)
            nc.vector.reciprocal(inv[:, 0:nb], root[:, 0:nb]).then_inc(norm_inv, 1)
            dve.wait_ge(norm_r, n + 1)

        def x_rhs(full_rows):
            if full_rows == "all":
                return (lambda t: xhi[:, t, 0:T]), (lambda t: xlo[:, t, 0:T])
            if full_rows == "x":
                return (lambda t: seg(xhi[:, t, :])), (lambda t: seg(xlo[:, t, :]))
            return (lambda t: xhi[:, t, 0:NX]), (lambda t: xlo[:, t, 0:NX])

        def wait_x(pe, n):
            def wait(t):
                if n == N_F1 and t:
                    pe_stat(pe, n, t - 1, True)
                pe.wait_ge(x_lo, KT * n + t + 1)
            return wait

        def pe_ff_in(pe, name, n, width):
            c0, g0 = first[name]
            hi, lo = x_rhs("all" if width == T else "packed")

            def body(i, edge):
                for j in range(4):
                    pe.wait_ge(w_lo, c0 + 4 * i + j + 1)
                    out = start_group(pe, g0, 4, i, j)
                    head = edge and i == 0 and j == 0
                    strip(out[:, 0:width], (c0 + j) % RING, KT, hi, lo,
                          before=wait_x(pe, n) if head else None).then_inc(pe_done, 1)
                    if head:
                        pe_stat(pe, n, KT - 1, width == T)
                    if edge and i == 0 and j == 1:
                        pe_norm(pe, n, width == T)
            bodies(pe, counts[name], 4, body)

        def act_ff_in(act, name, n, width):
            c0, g0 = first[name]
            f = ffs[name[:2]]

            def body(i, edge):
                for j in range(4):
                    split_hi(act, c0, 4, i, j + LEAD)
                    if edge and i == 0 and j == 0:
                        act_norm(act, n, width == T)
                    u = 2 * i + j // 2
                    if j % 2 == 0:
                        act.wait_ge(acc_free, g0 + 4 * i + j + 1)
                        nc.scalar.activation(sg[:, 0:width], tg[:, 0:width], ACT.Silu).then_inc(f["silu"], 1)
                    else:
                        act.wait_ge(f["prod"], u + 1)
                        nc.scalar.activation(hid(hid_hi, u, width), hd[:, 0:width], ACT.Copy).then_inc(f["hhi"], 1)
            bodies(act, counts[name], 4, body)

        def dve_ff_in(dve, name, n, width):
            c0, g0 = first[name]
            f = ffs[name[:2]]

            def hidden_lo(u):
                dve.wait_ge(f["hhi"], u + 1)
                nc.vector.tensor_tensor(hid(hid_lo, u, width), hd[:, 0:width], hid(hid_hi, u, width),
                                        ALU.subtract).then_inc(f["hlo"], 1)

            def body(i, edge):
                for j in range(4):
                    head = edge and i == 0 and j == 0
                    if head:
                        split_lo(dve, c0, 4, i, j + LEAD)
                        dve_norm(dve, n, width == T)
                    out = ps[banks[g0 + j]][:, 0:width]
                    u = 2 * i + j // 2
                    dve.wait_ge(pe_done, c0 + 4 * i + j + 1)
                    if j % 2 == 0:
                        nc.vector.tensor_tensor(tg[:, 0:width], out, rstd[:, 0:width], ALU.mult).then_inc(acc_free, 1)
                        if not head:
                            hidden_lo(u - 1)
                    else:
                        nc.vector.tensor_tensor(tu[:, 0:width], out, rstd[:, 0:width], ALU.mult).then_inc(acc_free, 1)
                        dve.wait_ge(f["silu"], u + 1)
                        dve.wait_ge(acc_free, g0 + 4 * i + j + 1)
                        nc.vector.tensor_tensor(hd[:, 0:width], tu[:, 0:width], sg[:, 0:width],
                                                ALU.mult).then_inc(f["prod"], 1)
                    if not head:
                        split_lo(dve, c0, 4, i, j + LEAD)
            bodies(dve, counts[name], 4, body)
            hidden_lo(FT - 1)

        def pe_residual(pe, name, n, full, cpm, rhs, ready):
            c0, g0 = first[name]
            tiles = sizes[c0]
            width = T if full else NX
            per = 2 * cpm if cpm > 1 else 4
            mpb = per // cpm

            def body(i, edge):
                for j in range(per):
                    q, m = j % cpm, j // cpm
                    pe.wait_ge(w_lo, c0 + per * i + j + 1)
                    if q == 0:
                        out = start_group(pe, g0, mpb, i, m)
                    head = edge and i == 0 and m == 0
                    strip(out[:, 0:width], (c0 + j) % RING, tiles,
                          lambda t: rhs(q * tiles + t)[0], lambda t: rhs(q * tiles + t)[1],
                          start=q == 0, stop=q == cpm - 1,
                          before=(lambda t: ready(q * tiles + t)) if head else None).then_inc(pe_done, 1)
                    if q == cpm - 1 and not head:
                        stat(i, m)

            def stat(i, m):
                pe_stat(pe, n, mpb * i + m - 1, full, par=(m - 1) % 2)
            bodies(pe, counts[name], per, body)

        def act_residual(act, name, n, full, cpm, prep=True):
            c0, g0 = first[name]
            per = 2 * cpm if cpm > 1 else 4
            mpb = per // cpm

            def body(i, edge):
                for j in range(per):
                    split_hi(act, c0, per, i, j + LEAD)
                    if j % cpm == cpm - 1:
                        m = j // cpm
                        act.wait_ge(acc_free, g0 + mpb * i + m + 1)
                        act_prep(act, n, mpb * i + m, full, prep, par=m % 2)
            bodies(act, counts[name], per, body)

        def dve_residual(dve, name, n, full, cpm, scale, prep=True):
            c0, g0 = first[name]
            width = T if full else NX
            per = 2 * cpm if cpm > 1 else 4
            mpb = per // cpm

            def body(i, edge):
                for j in range(per):
                    if j % cpm == cpm - 1:
                        m = j // cpm
                        k = mpb * i + m
                        out = ps[banks[g0 + (mpb * i if isinstance(i, int) else mpb) + m]]
                        dve.wait_ge(pe_done, c0 + per * i + j + 1)
                        nc.vector.scalar_tensor_tensor(res_tile(k, full), flat_or_two(out, full), scale,
                                                       res_tile(k, full), ALU.mult, ALU.add).then_inc(acc_free, 1)
                        last = edge and isinstance(k, int) and k == KT - 1
                        if prep and last:
                            dve_prep(dve, n, k, full)
                    split_lo(dve, c0, per, i, j + LEAD)
                    if prep and j % cpm == cpm - 1 and not last:
                        dve_prep(dve, n, k, full)
            bodies(dve, counts[name], per, body)

        mc, mg = first["mix"]
        QKT = 13
        V_FIRST, GATES = 14, 19
        UNITS = 16
        STEP0 = 18

        def qk_tile(t):
            if t < 4:
                return kn[:, t, :], T, V_FOXK
            if t < 8:
                return qn[:, t - 4, :], NX, V_FOXQ
            if t == 8:
                return kn[:, 4, :], T, V_SWAK
            return qn[:, t - 5, :], NX, V_SWAQ

        def unit(u):
            b = HD * (u % 2)
            return (u // 2, u // 2, b, u) if u < 8 else (u // 2, 4, b, (u - 8) // 2 + 4 * (u % 2))

        def pe_mix_chunk(pe, q):
            pe.wait_ge(w_lo, mc + q + 1)
            out = start_group(pe, mg, 1, q, 0)
            wide = q < 5 or q == 9 or V_FIRST <= q < GATES
            hi, lo = x_rhs("all" if wide else "x")
            strip(out[:, 0:T if wide else NX], (mc + q) % RING, KT, hi, lo,
                  before=wait_x(pe, N_MIX) if q == 0 else None).then_inc(pe_done, 1)

        def pe_mix(pe):
            for q in range(STEP0):
                pe_mix_chunk(pe, q)
                pe_mix_extra(pe, q)
            for u in range(UNITS + 2):
                q = STEP0 + u
                if u < UNITS:
                    pe_scores(pe, u)
                if q < counts["mix"]:
                    pe_mix_chunk(pe, q)
                if 1 <= u <= UNITS:
                    pe_turn(pe, u - 1)
                pe_mix_extra(pe, q)
                if u >= 2:
                    pe_values(pe, u - 2)

        def pe_mix_extra(pe, q):
            if q == 0:
                pe_stat(pe, N_MIX, KT - 1, True)
            if q == 1:
                pe_norm(pe, N_MIX, True)
            if 3 <= q < 3 + QKT:
                t = q - 3
                pe.wait_ge(qk_r, t + 1)
                if t:
                    pe.wait_ge(qk_n, t)
                for b, tok in enumerate(blocks(qk_tile(t)[1])):
                    mm = nc.tensor.matmul(ps[6][:, tok:tok + P], qk_wide[:, t % 2, b * P:(b + 1) * P], ident[:, :],
                                          start=True, stop=True)
                mm.then_inc(qk_bc, 1)
            if 2 <= q < 2 + QKT:
                t = q - 2
                pe.wait_ge(qk_sq, t + 1)
                if t:
                    pe.wait_ge(qk_sd, t)
                token_sums(ps[7], sq[:, t % 2, :], blocks(qk_tile(t)[1]), head_cols, True, True).then_inc(qk_ss, 1)
            if q == 6:
                pe.wait_ge(rel_const, 32)
                pe.wait_ge(table_set, 1)
                pe.wait_ge(norm_r, N_MIX + 1)
                nc.tensor.matmul(ps[4][0:HEADS, 0:REL_X], table[:, :], onehot[:, 0:REL_X], start=True, stop=True)
                nc.tensor.matmul(ps[5][0:HEADS, 0:REL_M], table[:, :], onehot[:, REL_X:], start=True,
                                 stop=True).then_inc(rel_mm, 1)
            if q == 8:
                pe.wait_ge(f_dve, 6)
                pe.wait_ge(rel_row, 2)
                for tt, tok in enumerate((0, SEG)):
                    mm = nc.tensor.matmul(ps[5][:, tt * HEADS:(tt + 1) * HEADS], cum[:, tok:tok + P],
                                          ident[0:HEADS, 0:HEADS], start=True, stop=True)
                mm.then_inc(cq_mm, 1)
            if 9 <= q < 13:
                for h in (2 * (q - 9), 2 * (q - 9) + 1):
                    if h == 1:
                        pe.wait_ge(cq_copied, 1)
                    if h >= 2:
                        pe.wait_ge(ck_copied, h - 1)
                    nc.tensor.matmul(ps[4 + h % 2][:, 0:T], selneg[:, h * P:(h + 1) * P], cum[:, :],
                                     start=True, stop=True).then_inc(ck_mm, 1)
            if V_FIRST < q <= GATES:
                t = q - 1 - V_FIRST
                pe.wait_ge(acc_free, mg + q)
                pe.wait_ge(qk_sd, QKT)
                if t:
                    pe.wait_ge(v_copied, 3 * t)
                for b, tok in enumerate((0, P, SEG)):
                    mm = nc.tensor.transpose(ps[7][:, b * P:(b + 1) * P], vt[:, t % 2, tok:tok + P], ident[:, :])
                mm.then_inc(v_tr, 1)

        def pe_scores(pe, u):
            qt, kt, b, _ = unit(u)
            if u == 0:
                pe.wait_ge(qk_n, QKT)
                pe.wait_ge(ck_copied, HEADS)
            if u >= 2:
                pe.wait_ge(at_max, 2 * (u - 2) + 2)
            out = ps[4 + u % 2]
            nc.tensor.matmul(out[:, 0:SEG], qn[b:b + HD, qt, 0:P], kn[b:b + HD, kt, 0:SEG], start=True, stop=True)
            nc.tensor.matmul(out[:, SEG:SEG + T], qn[b:b + HD, qt, P:NX], kn[b:b + HD, kt, 0:T],
                             start=True, stop=True).then_inc(at_s, 1)

        def pe_turn(pe, u):
            p = att[:, u % 2, :]
            pe.wait_ge(at_norm, 2 * u + 2)
            if u >= 1:
                pe.wait_ge(at_pt, 2 * u)
            for n, lo in enumerate((0, SEG, 2 * SEG)):
                nc.tensor.transpose(ps[6][:, n * P:(n + 1) * P], p[:, lo:lo + P], ident[:, :])
            for n, lo in enumerate((P, SEG + P)):
                mm = nc.tensor.transpose(ps[3][:, n * P:(n + 1) * P], p[:, lo:lo + P], ident[:, :])
            mm.then_inc(at_tr, 1)

        def pe_values(pe, u):
            b = HD * (u % 2)
            h = unit(u)[3]
            col = h * HD if u < 8 else 512 + (u % 2) * HD
            pe.wait_ge(at_pt, 2 * u + 2)
            if u == 0:
                pe.wait_ge(v_copied, 3 * (GATES - V_FIRST))
            if u >= 2 and u % 2 == 0:
                pe.wait_ge(o_lo, u // 2)
            o = ps[7][b:b + HD, 0:NX]
            keys, meta = pts[:, u % 2, :], ptm[:, u % 2, :]
            nc.tensor.matmul(o, v0[:, col:col + HD], keys[:, 0:NX], start=True, stop=False)
            nc.tensor.matmul(ps[7][b:b + HD, P:NX], v1[:, col:col + HD], keys[:, NX:NX + P], start=False, stop=False)
            nc.tensor.matmul(o, vm[:, col:col + HD], meta, start=False, stop=True).then_inc(at_pv, 1)

        def act_mix(act):
            act.wait_ge(angle_step, ANGLE_STEPS)
            for q in range(STEP0):
                split_hi(act, mc, 1, q, LEAD)
                act_mix_extra(act, q)
            for u in range(UNITS + 2):
                q = STEP0 + u
                if q < counts["mix"]:
                    split_hi(act, mc, 1, q, LEAD)
                if u < UNITS:
                    act_softmax(act, u)
                act_mix_extra(act, q)
                if 1 <= u <= UNITS:
                    v = u - 1
                    act.wait_ge(at_tr, v + 1)
                    if v >= 2:
                        act.wait_ge(at_pv, v - 1)
                    nc.scalar.activation(pts[:, v % 2, :], ps[6][:, 0:384], ACT.Copy).then_inc(at_pt, 1)
                    nc.scalar.activation(ptm[:, v % 2, :], ps[3][0:META, 0:NX], ACT.Copy).then_inc(at_pt, 1)
                if u >= 2 and u % 2 == 1:
                    act_heads_out(act, (u - 2) // 2)

        def act_mix_extra(act, q):
            if q == 0:
                act_norm(act, N_MIX, True)
            if q == 2:
                act.wait_ge(acc_free, mg + 1)
                nc.scalar.activation(fabs[:, :], fa[:, :], ACT.Abs,
                                     bias=vecs[0:HEADS, V_FBIAS:V_FBIAS + 1]).then_inc(f_act, 1)
                act.wait_ge(f_act, 1)
                nc.scalar.activation(fexp[:, :], fabs[:, :], ACT.Exp, scale=-1.0).then_inc(f_act, 1)
                act.wait_ge(f_act, 2)
                nc.scalar.activation(flog[:, :], fexp[:, :], ACT.Ln, bias=ones[0:HEADS, 0:1]).then_inc(f_act, 1)
            if 2 <= q < 2 + QKT:
                t = q - 2
                dst, width, _ = qk_tile(t)
                act.wait_ge(acc_free, mg + t + 2)
                if t >= 2:
                    act.wait_ge(qk_ss, t - 1)
                nc.scalar.activation(sq[:, t % 2, 0:width], dst, ACT.Square).then_inc(qk_sq, 1)
            if 3 <= q < 3 + QKT:
                t = q - 3
                n = 2 * len(blocks(qk_tile(t)[1]))
                is_q = qk_tile(t)[2] in (V_FOXQ, V_SWAQ)
                act.wait_ge(qk_ss, t + 1)
                if t >= 2:
                    act.wait_ge(qk_r, t - 1)
                nc.scalar.activation(qk_root[:, t % 2, 0:n], ps[7][:, 0:n], ACT.Sqrt,
                                     bias=epsc[:, 1:2] if is_q else epsc[:, 0:1],
                                     scale=1.0 if is_q else 1.0 / HD).then_inc(qk_sd, 1)
            if q == 7:
                act.wait_ge(rel_mm, 1)
                nc.scalar.activation(relrow[:, 0:REL_X], ps[4][0:HEADS, 0:REL_X], ACT.Copy).then_inc(rel_row, 1)
                nc.scalar.activation(relrow[:, REL_X:], ps[5][0:HEADS, 0:REL_M], ACT.Copy).then_inc(rel_row, 1)
            if 10 <= q < 14:
                for h in (2 * (q - 10), 2 * (q - 10) + 1):
                    act.wait_ge(ck_mm, h + 1)
                    nc.scalar.activation(ckb[:, h, :], ps[4 + h % 2][:, 0:T], ACT.Copy).then_inc(ck_copied, 1)
            if V_FIRST + 2 <= q <= GATES + 1:
                t = q - 2 - V_FIRST
                col = slice(t * P, (t + 1) * P)
                act.wait_ge(v_tr, t + 1)
                nc.scalar.activation(v0[:, col], ps[7][:, 0:P], ACT.Copy).then_inc(v_copied, 1)
                nc.scalar.activation(vm[:, col], ps[7][0:META, P:2 * P], ACT.Copy).then_inc(v_copied, 1)
                nc.scalar.activation(v1[:, col], ps[7][:, 2 * P:3 * P], ACT.Copy).then_inc(v_copied, 1)

        def act_softmax(act, u):
            s = small[:, u % 2, :]
            a = att[:, u % 2, :]
            act.wait_ge(at_neg, u + 1)
            if u >= 2:
                act.wait_ge(at_inv, u - 1)
            nc.scalar.activation(a[:, 0:SEG], a[:, 0:SEG], ACT.Exp, bias=s[:, 2:3], accum_out=s[:, 4:5]).then_inc(at_exp, 1)
            if u >= 8:
                h = unit(u)[3]
                nc.scalar.activation(s[:, 8:10], s[:, 2:4], ACT.Exp,
                                     bias=vecs[:, V_SINK + h:V_SINK + h + 1]).then_inc(at_exp, 1)
            nc.scalar.activation(a[:, SEG:], a[:, SEG:], ACT.Exp, bias=s[:, 3:4], accum_out=s[:, 5:6]).then_inc(at_exp, 1)

        def exps(u):
            return 2 * (u + 1) + max(u - 7, 0)

        def act_heads_out(act, t):
            act.wait_ge(at_pv, 2 * t + 2)
            nc.scalar.activation(oy_hi[:, t, :], ps[7][:, 0:NX], ACT.Copy).then_inc(o_hi, 1)

        def dve_mix(dve):
            dve.wait_ge(angle_step, ANGLE_STEPS)
            for q in range(STEP0):
                if q == 0:
                    split_lo(dve, mc, 1, q, LEAD)
                    dve_norm(dve, N_MIX, True)
                if 3 <= q < 3 + QKT:
                    t = q - 3
                    n = 2 * len(blocks(qk_tile(t)[1]))
                    dve.wait_ge(qk_sd, t + 1)
                    if t >= 2:
                        dve.wait_ge(qk_bc, t - 1)
                    nc.vector.reciprocal(qk_inv[:, t % 2, 0:n], qk_root[:, t % 2, 0:n]).then_inc(qk_inv_set, 1)
                    dve.wait_ge(qk_inv_set, t + 1)
                    nc.vector.tensor_copy(qk_wide[:, t % 2, 0:n * HD].rearrange("p (n d) -> p n d", d=HD),
                                          qk_inv[:, t % 2, 0:n].unsqueeze(2).to_broadcast([P, n, HD])).then_inc(qk_r, 1)
                if 4 <= q < 4 + QKT:
                    t = q - 4
                    dst, width, col = qk_tile(t)
                    dve.wait_ge(qk_bc, t + 1)
                    nc.vector.scalar_tensor_tensor(dst, dst, vecs[:, col:col + 1], ps[6][:, 0:width], ALU.mult,
                                                   ALU.mult).then_inc(qk_n, 1)
                dve_mix_read(dve, q)
                if q == 1:
                    dve_forget_min(dve)
                if q == 3:
                    dve_forget_scan(dve)
                if q == 9:
                    dve.wait_ge(cq_mm, 1)
                    nc.vector.tensor_copy(cq[:, :], ps[5][:, 0:16]).then_inc(cq_copied, 1)
                if q:
                    split_lo(dve, mc, 1, q, LEAD)
            for u in range(UNITS + 2):
                q = STEP0 + u
                if u < UNITS:
                    dve_scores(dve, u)
                if q < counts["mix"]:
                    split_lo(dve, mc, 1, q, LEAD)
                if u < UNITS:
                    dve_probs(dve, u)
                if q < counts["mix"]:
                    dve_mix_read(dve, q)
                if u >= 2 and u % 2 == 1:
                    t = (u - 2) // 2
                    dve.wait_ge(o_hi, t + 1)
                    nc.vector.tensor_tensor(oy_lo[:, t, :], ps[7][:, 0:NX], oy_hi[:, t, :],
                                            ALU.subtract).then_inc(o_lo, 1)

        def dve_mix_read(dve, q):
            out = ps[banks[mg + q]]
            dve.wait_ge(pe_done, mc + q + 1)
            if q == 0:
                nc.vector.tensor_tensor(fa[:, :], out[0:HEADS, 0:T], rstd[0:HEADS, 0:T], ALU.mult).then_inc(acc_free, 1)
            elif q <= QKT:
                dst, width, _ = qk_tile(q - 1)
                if width == T:
                    nc.vector.tensor_tensor(dst, out[:, 0:T], rstd[:, 0:T], ALU.mult).then_inc(acc_free, 1)
                else:
                    nc.vector.tensor_tensor(two(dst), two(out[:, 0:NX]), seg(rstd[:, :]), ALU.mult).then_inc(acc_free, 1)
            elif q < GATES:
                t = q - V_FIRST
                if t >= 2:
                    dve.wait_ge(v_tr, t - 1)
                nc.vector.tensor_tensor(vt[:, t % 2, :], out[:, 0:T], rstd[:, 0:T], ALU.mult).then_inc(acc_free, 1)
            else:
                if q == GATES:
                    dve.wait_ge(rel_out, 16)
                    dve.wait_ge(ck_copied, HEADS)
                nc.vector.tensor_tensor(two(gate[:, q - GATES, :]), two(out[:, 0:NX]), seg(rstd[:, :]),
                                        ALU.mult).then_inc(acc_free, 1)

        def dve_forget_min(dve):
            dve.wait_ge(acc_free, mg + 1)
            nc.vector.tensor_scalar(fmin[:, :], fa[:, :], vecs[0:HEADS, V_FBIAS:V_FBIAS + 1], 0.0, ALU.add,
                                    ALU.min).then_inc(f_dve, 1)
            nc.vector.memset(fones[:, :], 1.0).then_inc(f_dve, 1)

        def dve_forget_scan(dve):
            dve.wait_ge(f_act, 3)
            dve.wait_ge(f_dve, 2)
            nc.vector.tensor_tensor(fa[:, :], fmin[:, :], flog[:, :], ALU.subtract).then_inc(f_dve, 1)
            dve.wait_ge(f_dve, 3)
            nc.vector.tensor_tensor_scan(cum[:, P:SEG], fones[:, P:SEG], fa[:, P:SEG], 0.0, ALU.mult,
                                         ALU.add).then_inc(f_dve, 1)
            dve.wait_ge(f_dve, 4)
            nc.vector.tensor_tensor_scan(cum[:, 0:P], fones[:, 0:P], fa[:, 0:P], cum[:, SEG - 1:SEG], ALU.mult,
                                         ALU.add).then_inc(f_dve, 1)
            dve.wait_ge(f_dve, 5)
            nc.vector.tensor_tensor_scan(cum[:, SEG:T], fones[:, SEG:T], fa[:, SEG:T], cum[:, P - 1:P], ALU.mult,
                                         ALU.add).then_inc(f_dve, 1)

        def dve_scores(dve, u):
            h = unit(u)[3]
            s, a, out = small[:, u % 2, :], att[:, u % 2, :], ps[4 + u % 2]
            if u < 8:
                if u == 0:
                    dve.wait_ge(cq_copied, 1)
                    dve.wait_ge(ck_copied, HEADS)
                    dve.wait_ge(mask_set, 4)
                    dve.wait_ge(qk_n, QKT)
                nc.vector.scalar_tensor_tensor(bm[:, 0:SEG], ckb[:, h, 0:SEG], cq[:, h:h + 1], mask[:, 0:SEG],
                                               ALU.add, ALU.add).then_inc(at_bias, 1)
                nc.vector.scalar_tensor_tensor(bm[:, SEG:], ckb[:, h, :], cq[:, HEADS + h:HEADS + h + 1],
                                               mask[:, SEG:], ALU.add, ALU.add).then_inc(at_bias, 1)
                dve.wait_ge(at_bias, 2 * u + 2)
                bias, least = bm[:, :], (-3.0e38, -3.0e38)
            else:
                if u == 8:
                    dve.wait_ge(rel_in, 80)
                bias, least = rel[:, h, :], (vecs[:, V_SINK + h:V_SINK + h + 1],) * 2
            dve.wait_ge(at_s, u + 1)
            if u >= 2:
                dve.wait_ge(at_tr, u - 1)
            nc.vector.tensor_tensor_reduce(a[:, 0:SEG], out[:, 0:SEG], bias[:, 0:SEG], 1.0, least[0], ALU.add,
                                           ALU.max, s[:, 0:1]).then_inc(at_max, 1)
            nc.vector.tensor_tensor_reduce(a[:, SEG:], out[:, SEG:SEG + T], bias[:, SEG:], 1.0, least[1], ALU.add,
                                           ALU.max, s[:, 1:2]).then_inc(at_max, 1)
            dve.wait_ge(at_max, 2 * u + 2)
            nc.vector.tensor_scalar(s[:, 2:4], s[:, 0:2], -1.0, None, ALU.mult).then_inc(at_neg, 1)

        def dve_probs(dve, u):
            s, a = small[:, u % 2, :], att[:, u % 2, :]
            dve.wait_ge(at_exp, exps(u))
            if u >= 8:
                nc.vector.tensor_tensor(s[:, 4:6], s[:, 4:6], s[:, 8:10], ALU.add).then_inc(at_sum, 1)
                dve.wait_ge(at_sum, u - 7)
            nc.vector.reciprocal(s[:, 6:8], s[:, 4:6]).then_inc(at_inv, 1)
            dve.wait_ge(at_inv, u + 1)
            nc.vector.tensor_scalar(a[:, 0:SEG], a[:, 0:SEG], s[:, 6:7], None, ALU.mult).then_inc(at_norm, 1)
            nc.vector.tensor_scalar(a[:, SEG:], a[:, SEG:], s[:, 7:8], None, ALU.mult).then_inc(at_norm, 1)

        bc, bg = first["branch"]

        def pe_branch(pe):
            for m in range(KT):
                pe.wait_ge(w_lo, bc + m + 1)
                for br in range(2):
                    out = start_group(pe, bg, 2, m, br)
                    if m == 0:
                        pe.wait_ge(o_lo, 4 * br + 4)
                    mm = strip(out[:, 0:NX], (bc + m) % RING, 4, lambda t: oy_hi[:, 4 * br + t, :],
                               lambda t: oy_lo[:, 4 * br + t, :], at=4 * br)
                mm.then_inc(pe_done, 1)

        def act_branch(act):
            for m in range(KT):
                split_hi(act, bc, 1, m, LEAD)
                if m == 0:
                    act.wait_ge(acc_free, mg + counts["mix"])
                for br in range(2):
                    nc.scalar.activation(gate[:, 2 * m + br, :], gate[:, 2 * m + br, :], ACT.Sigmoid).then_inc(sig_done, 1)
                act.wait_ge(y_step, m + 1)
                nc.scalar.activation(oy_hi[:, 8 + m, :], hd[:, 0:NX], ACT.Copy).then_inc(y_hi, 1)

        def dve_branch(dve):
            def low(m):
                dve.wait_ge(y_hi, m + 1)
                nc.vector.tensor_tensor(oy_lo[:, 8 + m, :], hd[:, 0:NX], oy_hi[:, 8 + m, :], ALU.subtract).then_inc(y_lo, 1)

            for m in range(KT):
                dve.wait_ge(pe_done, bc + m + 1)
                dve.wait_ge(sig_done, 2 * m + 2)
                if m:
                    dve.wait_ge(y_step, m)
                for br, dst in enumerate((tg, tu)):
                    nc.vector.tensor_tensor(dst[:, 0:NX], ps[banks[bg + 2 * m + br]][:, 0:NX], gate[:, 2 * m + br, :],
                                            ALU.mult).then_inc(acc_free, 1)
                dve.wait_ge(acc_free, bg + 2 * m + 2)
                if m:
                    dve.wait_ge(y_lo, m)
                nc.vector.tensor_tensor(hd[:, 0:NX], tg[:, 0:NX], tu[:, 0:NX], ALU.add).then_inc(y_step, 1)
                if m == KT - 1:
                    low(m)
                split_lo(dve, bc, 1, m, LEAD)
                if m < KT - 1:
                    low(m)

        sc, sgrp = first["mixb"]
        STEPS = counts["mixb"] + counts["memk"]
        TAP0 = 4
        TAPS_PER_STEP = 7
        RET0 = 13
        MEM0 = 4
        LN0 = TAP0 + -(-4 * TAPS // TAPS_PER_STEP)
        RV = 12

        def pe_mixb(pe):
            for q in range(STEPS):
                pe.wait_ge(w_lo, sc + q + 1)
                out = start_group(pe, sgrp, 1, q, 0)
                s = (sc + q) % RING
                if q < 20:
                    hi, lo = x_rhs("packed")
                    mm = strip(out[:, 0:NX], s, KT, hi, lo, before=wait_x(pe, N_MIXB) if q == 0 else None)
                else:
                    if q == 20:
                        pe.wait_ge(m_lo, KT)
                    mm = strip(out[:, 0:NX], s, KT, lambda t: mem_hi[:, t, :], lambda t: mem_lo[:, t, :])
                mm.then_inc(pe_done, 1)
                if q == 0:
                    pe_stat(pe, N_MIXB, KT - 1, False)
                if q == 1:
                    pe_norm(pe, N_MIXB, False)
                if MEM0 < q <= MEM0 + KT:
                    e = q - MEM0 - 1
                    pe.wait_ge(m_sq, e + 1)
                    token_sums(ps[3], msq[:, e % 2, :], blocks(NX), one_col, e == 0, e == KT - 1).then_inc(m_stat, 1)
                if q == 14:
                    pe.wait_ge(m_inv, 1)
                    pe.wait_ge(rv_copied, 1)
                    spread(ps[3], col_inv[:, 0, :], blocks(NX)).then_inc(m_bc, 1)
                if 9 <= q < 13:
                    e = q - 9
                    pe.wait_ge(acc_free, sgrp + 8 + e + 1)
                    if e >= 2:
                        pe.wait_ge(rot_step, 3 * (e - 2) + 2)
                    nc.tensor.matmul(ps[6 + e % 2][:, 0:NX], swap[:, :], qr[:, e, :], start=True, stop=True).then_inc(rot_mm, 1)
                if RV < q <= RV + 4:
                    t = q - 1 - RV
                    pe.wait_ge(acc_free, sgrp + q)
                    pe.wait_ge(m_sd, 1)
                    if t:
                        pe.wait_ge(rv_copied, t)
                    if t == 2:
                        pe.wait_ge(m_r, 1)
                    src = tu if t % 2 else tg
                    for tt in range(2):
                        mm = nc.tensor.transpose(ps[3][:, NX + tt * P:NX + (tt + 1) * P], src[:, tt * P:(tt + 1) * P],
                                                 ident[:, :])
                    mm.then_inc(rv_tr, 1)
                if q >= RET0:
                    pe_retention(pe, q - RET0)
                if q == LN0 + 1:
                    pe.wait_ge(conv_step, 4 * TAPS)
                    pe.wait_ge(ra_dec, HEADS)
                    for t in range(4):
                        mm = nc.tensor.matmul(ps[4][:, 0:NX], ones[:, :], cy[:, t, :], start=t == 0, stop=t == 3)
                    mm.then_inc(ln_mu, 1)
                if q == LN0 + 2:
                    for t in range(4):
                        pe.wait_ge(ln_sq, t + 1)
                        mm = token_sums(ps[5], csq[:, t, :], blocks(NX), one_col, t == 0, t == 3)
                    mm.then_inc(ln_var, 1)
                if q == LN0 + 3:
                    pe.wait_ge(ln_r, 1)
                    spread(ps[5][:, P:], col_inv[:, 2, :], blocks(NX)).then_inc(ln_bc, 1)

        def pe_retention(pe, r):
            if r < HEADS:
                b = RDK * (r % 4)
                pe.wait_ge(rot_step, 9 if r < 4 else 12)
                if r == 0:
                    pe.wait_ge(norm_r, N_MIXB + 1)
                if r >= 2:
                    pe.wait_ge(ra_dec, r - 1)
                out = ps[4 + r % 2]
                qh, kh = qr[b:b + RDK, r // 4, :], qr[b:b + RDK, 2 + r // 4, :]
                nc.tensor.matmul(out[:, 0:NX], kh[:, 0:P], qh[:, :], start=True, stop=True)
                nc.tensor.matmul(out[:, NX:NX + P], kh[:, P:NX], qh[:, P:NX], start=True, stop=True).then_inc(ra_mm, 1)
            if 1 <= r <= HEADS:
                h = r - 1
                b = HD * (h % 2)
                pe.wait_ge(ra_dec, h + 1)
                pe.wait_ge(rv_copied, h // 2 + 1)
                if h == 0:
                    pe.wait_ge(rot_step, 8)
                if h >= 2 and h % 2 == 0:
                    pe.wait_ge(ry_copied, h // 2)
                a = amat[:, h % 2, :]
                nc.tensor.matmul(ps[6][b:b + HD, 0:NX], v2[:, 0, h * HD:(h + 1) * HD], a[:, 0:NX], start=True, stop=False)
                nc.tensor.matmul(ps[6][b:b + HD, P:NX], v2[:, 1, h * HD:(h + 1) * HD], a[:, NX:NX + P], start=False,
                                 stop=True).then_inc(ry_mm, 1)
            if r >= 6 and r % 2 == 0 and (r - 6) // 2 < 4:
                t = (r - 6) // 2
                pe.wait_ge(gn_r, t + 1)
                pe.wait_ge(gn_cen, min(t + 2, 4))
                for b, tok in enumerate(blocks(NX)):
                    for h in range(2):
                        v = col_inv[:, 1, 2 * b + h:2 * b + h + 1].to_broadcast([P, HD])
                        mm = nc.tensor.matmul(ps[7][h * HD:(h + 1) * HD, NX + tok:NX + tok + P], v, ident[:, :],
                                              start=True, stop=True)
                mm.then_inc(gn_bc, 1)
            if r >= 3 and r % 2 == 1 and (r - 3) // 2 < 4:
                t = (r - 3) // 2
                pe.wait_ge(ry_copied, t + 1)
                if t == 0:
                    pe.wait_ge(rot_step, 12)
                if t >= 2:
                    pe.wait_ge(gn_n, t - 1)
                nc.tensor.matmul(ps[7][:, 0:NX], same[:, :], yr[:, t % 2, :], start=True, stop=True).then_inc(gn_mu, 1)
            if r >= 4 and r % 2 == 0 and (r - 4) // 2 < 4:
                t = (r - 4) // 2
                pe.wait_ge(gn_sq, t + 1)
                if t == 0:
                    pe.wait_ge(rv_copied, 4)
                if t:
                    pe.wait_ge(gn_sd, t)
                token_sums(ps[3], msq[:, t % 2, :], blocks(NX), head_cols, True, True).then_inc(gn_var, 1)

        def act_mixb(act):
            for q in range(STEPS):
                split_hi(act, sc, 1, q, LEAD)
                if q == 0:
                    act_norm(act, N_MIXB, False)
                if q == 1:
                    act.wait_ge(angle_step, ANGLE_STEPS)
                    nc.scalar.activation(sinv[:, :], angle[:, :], ACT.Sin).then_inc(cs_act, 1)
                    nc.scalar.activation(cosv[:, :], angle[:, :], ACT.Sin, scale=0.5).then_inc(cs_act, 1)
                if q < 8 and q % 2 == 0:
                    act.wait_ge(acc_free, sgrp + q + 1)
                    nc.scalar.activation(sg[:, 0:NX], tg[:, 0:NX], ACT.Sigmoid).then_inc(cb_sig, 1)
                if MEM0 <= q < MEM0 + KT:
                    e = q - MEM0
                    if e == 0:
                        act.wait_ge(mem_in, 16)
                    nc.scalar.activation(mem_hi[:, e, :], mem[:, e, :], ACT.Copy, scale=gain(N_MEM, e)).then_inc(m_hi, 1)
                    if e >= 2:
                        act.wait_ge(m_stat, e - 1)
                    nc.scalar.activation(msq[:, e % 2, :], mem[:, e, :], ACT.Square).then_inc(m_sq, 1)
                if q == MEM0 + KT + 1:
                    act.wait_ge(m_stat, KT)
                    nc.scalar.activation(col_root[:, 0, 0:2], ps[3][:, 0:2], ACT.Sqrt, bias=epsc[:, 0:1],
                                         scale=1.0 / D).then_inc(m_sd, 1)
                if q == 15:
                    act.wait_ge(m_bc, 1)
                    act.wait_ge(rv_tr, 2)
                    nc.scalar.activation(memr[:, :], ps[3][:, 0:NX], ACT.Copy).then_inc(m_r, 1)
                if RV + 2 <= q < RV + 6:
                    t = q - 2 - RV
                    act.wait_ge(rv_tr, t + 1)
                    nc.scalar.activation(v2[:, :, t * P:(t + 1) * P], two(ps[3][:, NX:512]), ACT.Copy).then_inc(rv_copied, 1)
                if 17 <= q < 21:
                    act.wait_ge(acc_free, sgrp + q)
                    src = tg if q % 2 else tu
                    nc.scalar.activation(rg[:, q - 17, :], src[:, 0:NX], ACT.Silu).then_inc(rg_done, 1)
                if q >= RET0:
                    act_retention(act, q - RET0)
                if q == LN0 + 2:
                    for t in range(4):
                        act.wait_ge(ln_cen, t + 1)
                        nc.scalar.activation(csq[:, t, :], cy[:, t, :], ACT.Square).then_inc(ln_sq, 1)
                if q == LN0 + 3:
                    act.wait_ge(ln_var, 1)
                    nc.scalar.activation(col_root[:, 2, 0:2], ps[5][:, 0:2], ACT.Sqrt, bias=epsc[:, 0:1],
                                         scale=1.0 / CONV).then_inc(ln_sd, 1)
            act_conv_out(act)

        def act_conv_out(act):
            for t in range(4):
                act.wait_ge(ln_n, t + 1)
                nc.scalar.activation(cy[:, t, :], cy[:, t, :], ACT.Silu,
                                     bias=vecs[:, V_LNB + t:V_LNB + t + 1]).then_inc(ln_z, 1)
            for t in range(4):
                act.wait_ge(ln_z, t + 1)
                nc.scalar.activation(oz_hi[:, 4 + t, :], cy[:, t, :], ACT.Copy).then_inc(c_hi, 1)

        def act_retention(act, r):
            if r >= 4 and r % 2 == 0 and (r - 4) // 2 < 4:
                t = (r - 4) // 2
                act.wait_ge(gn_cen, t + 1)
                if t >= 2:
                    act.wait_ge(gn_var, t - 1)
                nc.scalar.activation(msq[:, t % 2, :], yr[:, t % 2, :], ACT.Square).then_inc(gn_sq, 1)
            if r >= 5 and r % 2 == 1 and (r - 5) // 2 < 4:
                t = (r - 5) // 2
                act.wait_ge(gn_var, t + 1)
                if t:
                    act.wait_ge(gn_r, t)
                nc.scalar.activation(col_root[:, 1, :], ps[3][:, 0:4], ACT.Sqrt, bias=epsc[:, 0:1],
                                     scale=1.0 / HD).then_inc(gn_sd, 1)
            if r >= 7 and r % 2 == 1 and (r - 7) // 2 < 4:
                t = (r - 7) // 2
                act.wait_ge(gn_z, t + 1)
                nc.scalar.activation(oz_hi[:, t, :], zt[:, t % 2, :], ACT.Copy).then_inc(z_hi, 1)

        def conv_taps(dve, a, b):
            for n in range(a, min(b, 4 * TAPS)):
                t, j = n // (2 * TAPS) * 2 + n % 2, n % (2 * TAPS) // 2
                src = glu[:, t, j:j + NX]
                w = convw[:, t * TAPS + j:t * TAPS + j + 1]
                if j == 0:
                    dve.wait_ge(glu_done, t + 1)
                    nc.vector.tensor_scalar(cy[:, t, :], src, w, vecs[:, V_CONVB + t:V_CONVB + t + 1], ALU.mult,
                                            ALU.add).then_inc(conv_step, 1)
                else:
                    dve.wait_ge(conv_step, n - 1)
                    nc.vector.scalar_tensor_tensor(cy[:, t, :], src, w, cy[:, t, :], ALU.mult, ALU.add).then_inc(conv_step, 1)

        def dve_mixb(dve):
            for q in range(STEPS):
                if q == 0:
                    split_lo(dve, sc, 1, q, LEAD)
                    dve_norm(dve, N_MIXB, False)
                if q == 3:
                    dve.wait_ge(cs_act, 2)
                    nc.vector.tensor_tensor(cosv[:, :], cosv[:, :], cosv[:, :], ALU.mult).then_inc(cs_dve, 1)
                    dve.wait_ge(cs_dve, 1)
                    nc.vector.tensor_scalar(cosv[:, :], cosv[:, :], -2.0, 1.0, ALU.mult, ALU.add).then_inc(cs_dve, 1)
                if 10 <= q < 14:
                    e = q - 10
                    dve.wait_ge(rot_mm, e + 1)
                    dve.wait_ge(cs_dve, 2)
                    if e:
                        dve.wait_ge(rot_step, 3 * e)
                    nc.vector.tensor_tensor(qr[:, e, :], qr[:, e, :], cosv[:, :], ALU.mult).then_inc(rot_step, 1)
                    nc.vector.tensor_tensor(hd[:, 0:NX], ps[6 + e % 2][:, 0:NX], sinv[:, :], ALU.mult).then_inc(rot_step, 1)
                    dve.wait_ge(rot_step, 3 * e + 2)
                    nc.vector.tensor_tensor(qr[:, e, :], qr[:, e, :], hd[:, 0:NX], ALU.add).then_inc(rot_step, 1)
                if q == 14:
                    dve.wait_ge(m_sd, 1)
                    nc.vector.reciprocal(col_inv[:, 0, 0:2], col_root[:, 0, 0:2]).then_inc(m_inv, 1)
                if q == LN0 + 3:
                    dve.wait_ge(ln_sd, 1)
                    nc.vector.reciprocal(col_inv[:, 2, 0:2], col_root[:, 2, 0:2]).then_inc(ln_r, 1)
                dve_mixb_read(dve, q)
                if q >= RET0:
                    dve_retention(dve, q - RET0)
                if q:
                    split_lo(dve, sc, 1, q, LEAD)
                if MEM0 <= q < MEM0 + KT:
                    e = q - MEM0
                    dve.wait_ge(m_hi, e + 1)
                    nc.vector.scalar_tensor_tensor(mem_lo[:, e, :], mem[:, e, :], gain(N_MEM, e), mem_hi[:, e, :],
                                                   ALU.mult, ALU.subtract).then_inc(m_lo, 1)
                if q >= TAP0:
                    conv_taps(dve, (q - TAP0) * TAPS_PER_STEP, (q - TAP0 + 1) * TAPS_PER_STEP)
                if q == LN0 + 1:
                    dve.wait_ge(ln_mu, 1)
                    for t in range(4):
                        nc.vector.scalar_tensor_tensor(cy[:, t, :], ps[4][:, 0:NX], -1.0 / CONV, cy[:, t, :], ALU.mult,
                                                       ALU.add).then_inc(ln_cen, 1)
            dve.wait_ge(ln_bc, 1)
            for t in range(4):
                nc.vector.scalar_tensor_tensor(cy[:, t, :], cy[:, t, :], vecs[:, V_LNW + t:V_LNW + t + 1],
                                               ps[5][:, P:P + NX], ALU.mult, ALU.mult).then_inc(ln_n, 1)
            for t in range(4):
                dve.wait_ge(c_hi, t + 1)
                nc.vector.tensor_tensor(oz_lo[:, 4 + t, :], cy[:, t, :], oz_hi[:, 4 + t, :], ALU.subtract).then_inc(c_lo, 1)

        def dve_mixb_read(dve, q):
            out = ps[banks[sgrp + q]][:, 0:NX]
            dve.wait_ge(pe_done, sc + q + 1)
            if 8 <= q < RV:
                nc.vector.tensor_tensor(qr[:, q - 8, :], out, rstd[:, 0:NX], ALU.mult).then_inc(acc_free, 1)
            elif q < 20:
                dst = tu if q % 2 else tg
                if q < 8 and q % 2 and q > 1:
                    dve.wait_ge(glu_done, q // 2)
                if q == RV + 1:
                    dve.wait_ge(glu_done, 4)
                if RV + 2 <= q < RV + 6:
                    dve.wait_ge(rv_tr, q - RV - 1)
                if q >= RV + 6:
                    dve.wait_ge(rg_done, q - RV - 5)
                nc.vector.tensor_tensor(dst[:, 0:NX], out, rstd[:, 0:NX], ALU.mult).then_inc(acc_free, 1)
                if q < 8 and q % 2:
                    dve.wait_ge(cb_sig, q // 2 + 1)
                    dve.wait_ge(acc_free, sgrp + q + 1)
                    nc.vector.tensor_tensor(glu[:, q // 2, TAPS - 1:], tu[:, 0:NX], sg[:, 0:NX],
                                            ALU.mult).then_inc(glu_done, 1)
            else:
                if q == 20:
                    dve.wait_ge(m_r, 1)
                nc.vector.tensor_tensor(km[:, q - 20, :], out, memr[:, :], ALU.mult).then_inc(acc_free, 1)

        def dve_retention(dve, r):
            if r < HEADS:
                if r == 0:
                    dve.wait_ge(decay_in, 16)
                dve.wait_ge(ra_mm, r + 1)
                if r >= 2:
                    dve.wait_ge(ry_mm, r - 1)
                nc.vector.tensor_tensor(amat[:, r % 2, :], ps[4 + r % 2][:, 0:384], decay[:, r, :], ALU.mult).then_inc(ra_dec, 1)
            if r >= 3 and r % 2 == 1 and (r - 3) // 2 < 4:
                t = (r - 3) // 2
                dve.wait_ge(gn_mu, t + 1)
                nc.vector.scalar_tensor_tensor(yr[:, t % 2, :], ps[7][:, 0:NX], -1.0 / HD, yr[:, t % 2, :], ALU.mult,
                                               ALU.add).then_inc(gn_cen, 1)
            if r >= 5 and r % 2 == 1 and (r - 5) // 2 < 4:
                t = (r - 5) // 2
                dve.wait_ge(gn_sd, t + 1)
                if t:
                    dve.wait_ge(gn_bc, t)
                nc.vector.reciprocal(col_inv[:, 1, :], col_root[:, 1, :]).then_inc(gn_r, 1)
            if r >= 6 and r % 2 == 0 and (r - 6) // 2 < 4:
                t = (r - 6) // 2
                dve.wait_ge(gn_bc, t + 1)
                nc.vector.scalar_tensor_tensor(yr[:, t % 2, :], yr[:, t % 2, :], vecs[:, V_GNW + t:V_GNW + t + 1],
                                               ps[7][:, NX:512], ALU.mult, ALU.mult).then_inc(gn_n, 1)
                dve.wait_ge(gn_n, t + 1)
                dve.wait_ge(rg_done, t + 1)
                if t >= 2:
                    dve.wait_ge(z_lo, t - 1)
                nc.vector.tensor_tensor(zt[:, t % 2, :], yr[:, t % 2, :], rg[:, t, :], ALU.mult).then_inc(gn_z, 1)
            if r >= 2 and r % 2 == 0 and (r - 2) // 2 < 4:
                t = (r - 2) // 2
                dve.wait_ge(ry_mm, 2 * t + 2)
                if t >= 2:
                    dve.wait_ge(gn_z, t - 1)
                nc.vector.tensor_copy(yr[:, t % 2, :], ps[6][:, 0:NX]).then_inc(ry_copied, 1)
            if r >= 7 and r % 2 == 1 and (r - 7) // 2 < 4:
                t = (r - 7) // 2
                dve.wait_ge(z_hi, t + 1)
                nc.vector.tensor_tensor(oz_lo[:, t, :], zt[:, t % 2, :], oz_hi[:, t, :], ALU.subtract).then_inc(z_lo, 1)

        qc, qg = first["xq"]
        XSTEPS = counts["xq"] + counts["memv"]

        def pe_xattn(pe):
            hi, lo = x_rhs("packed")
            for m in range(XSTEPS + 2):
                if m < XSTEPS:
                    pe.wait_ge(w_lo, qc + m + 1)
                    out = start_group(pe, qg, 1, m, 0)[:, 0:NX]
                    s = (qc + m) % RING
                    if m < KT:
                        mm = strip(out, s, KT, hi, lo, before=wait_x(pe, N_XATT) if m == 0 else None)
                    else:
                        mm = strip(out, s, KT, lambda t: mem_hi[:, t, :], lambda t: mem_lo[:, t, :])
                    mm.then_inc(pe_done, 1)
                if m == 0:
                    pe_stat(pe, N_XATT, KT - 1, False)
                if m == 1:
                    pe_norm(pe, N_XATT, False)
                if KT < m <= XSTEPS:
                    e = m - 1 - KT
                    pe.wait_ge(acc_free, qg + m)
                    if e:
                        pe.wait_ge(xv_copied, e)
                    src = tu if e % 2 else tg
                    for tt in range(2):
                        mm = nc.tensor.transpose(ps[3][:, tt * P:(tt + 1) * P], src[:, tt * P:(tt + 1) * P], ident[:, :])
                    mm.then_inc(xv_tr, 1)
                if m % 2 == 0 and 0 <= (m - 2) // 2 < XHEADS:
                    pe_xscores(pe, (m - 2) // 2)
                if m % 2 == 0 and 0 <= (m - 8) // 2 < XHEADS:
                    pe_xturn(pe, (m - 8) // 2)
                if m % 2 == 1 and 0 <= (m - 11) // 2 < XHEADS:
                    pe_xvalues(pe, (m - 11) // 2)

        def pe_xscores(pe, h):
            pe.wait_ge(acc_free, qg + 2 * h + 2)
            if h == 0:
                pe.wait_ge(norm_r, N_XATT + 1)
            if h >= 2:
                pe.wait_ge(xs_exp, 2 * (h - 2) + 2)
            out = ps[4 + h % 2]
            for qt in range(2):
                for t in range(2):
                    mm = nc.tensor.matmul(out[:, qt * NX:(qt + 1) * NX], qx[:, 2 * h + t, qt * P:(qt + 1) * P],
                                          km[:, 2 * h + t, :], start=t == 0, stop=t == 1)
            mm.then_inc(xs_s, 1)

        def pe_xturn(pe, h):
            pe.wait_ge(xs_norm, 2 * h + 2)
            if h:
                pe.wait_ge(xs_pt, h)
            p = xatt[:, h, :]
            for t in range(2):
                for qt in range(2):
                    mm = nc.tensor.transpose(ps[6][:, t * NX + qt * P:t * NX + (qt + 1) * P],
                                             p[:, qt * NX + t * P:qt * NX + (t + 1) * P], ident[:, :])
            mm.then_inc(xs_tr, 1)

        def pe_xvalues(pe, h):
            pe.wait_ge(xs_pt, h + 1)
            pe.wait_ge(xv_copied, 2 * h + 2)
            if h:
                pe.wait_ge(xo_lo, h)
            for dt in range(2):
                col = h * XH_DIM + dt * P
                for t in range(2):
                    mm = nc.tensor.matmul(ps[7][:, dt * NX:(dt + 1) * NX], vmem[:, t, col:col + P],
                                          xpt[:, h % 2, t * NX:(t + 1) * NX], start=t == 0, stop=t == 1)
            mm.then_inc(xs_pv, 1)

        def act_xattn(act):
            for m in range(XSTEPS + 3):
                if m < XSTEPS:
                    split_hi(act, qc, 1, m, LEAD)
                if m == 0:
                    act_norm(act, N_XATT, False)
                if m % 2 == 1 and 0 <= (m - 3) // 2 < XHEADS:
                    act_xexp(act, (m - 3) // 2)
                if KT + 2 <= m < XSTEPS + 2:
                    e = m - 2 - KT
                    act.wait_ge(xv_tr, e + 1)
                    nc.scalar.activation(vmem[:, :, e * P:(e + 1) * P], two(ps[3][:, 0:NX]), ACT.Copy).then_inc(xv_copied, 1)
                if m % 2 == 1 and 0 <= (m - 9) // 2 < XHEADS:
                    act_xcopy(act, (m - 9) // 2)
                if m % 2 == 0 and 0 <= (m - 12) // 2 < XHEADS:
                    act_xout(act, (m - 12) // 2)

        def act_xexp(act, h):
            s = xsmall[:, h, :]
            act.wait_ge(xs_neg, h + 1)
            for qt in range(2):
                nc.scalar.activation(xatt[:, h, qt * NX:(qt + 1) * NX], ps[4 + h % 2][:, qt * NX:(qt + 1) * NX],
                                     ACT.Exp, bias=s[:, 2 + qt:3 + qt], scale=XH_DIM ** -0.5,
                                     accum_out=s[:, 4 + qt:5 + qt]).then_inc(xs_exp, 1)

        def act_xcopy(act, h):
            act.wait_ge(xs_tr, h + 1)
            if h >= 2:
                act.wait_ge(xs_pv, h - 1)
            nc.scalar.activation(xpt[:, h % 2, :], ps[6][:, :], ACT.Copy).then_inc(xs_pt, 1)

        def act_xout(act, h):
            act.wait_ge(xs_pv, h + 1)
            nc.scalar.activation(oz_hi[:, 2 * h:2 * h + 2, :], two(ps[7][:, :]), ACT.Copy).then_inc(xo_hi, 1)

        def dve_xattn(dve):
            for m in range(XSTEPS + 3):
                if m == 0:
                    split_lo(dve, qc, 1, m, LEAD)
                    dve_norm(dve, N_XATT, False)
                if m < XSTEPS:
                    out = ps[banks[qg + m]][:, 0:NX]
                    dve.wait_ge(pe_done, qc + m + 1)
                    if m < KT:
                        nc.vector.tensor_tensor(qx[:, m, :], out, rstd[:, 0:NX], ALU.mult).then_inc(acc_free, 1)
                    else:
                        e = m - KT
                        if e >= 2:
                            dve.wait_ge(xv_tr, e - 1)
                        dst = tu if e % 2 else tg
                        nc.vector.tensor_tensor(dst[:, 0:NX], out, memr[:, :], ALU.mult).then_inc(acc_free, 1)
                if m % 2 == 0 and 0 <= (m - 2) // 2 < XHEADS:
                    dve_xmax(dve, (m - 2) // 2)
                if 0 < m < XSTEPS:
                    split_lo(dve, qc, 1, m, LEAD)
                if m % 2 == 1 and 0 <= (m - 3) // 2 < XHEADS:
                    dve_xprobs(dve, (m - 3) // 2)
                if m % 2 == 0 and 0 <= (m - 12) // 2 < XHEADS:
                    dve_xlow(dve, (m - 12) // 2)

        def dve_xmax(dve, h):
            s = xsmall[:, h, :]
            dve.wait_ge(xs_s, h + 1)
            nc.vector.tensor_reduce(s[:, 0:2], two(ps[4 + h % 2][:, :]), AX.X, ALU.max).then_inc(xs_max, 1)
            dve.wait_ge(xs_max, h + 1)
            nc.vector.tensor_scalar(s[:, 2:4], s[:, 0:2], -(XH_DIM ** -0.5), None, ALU.mult).then_inc(xs_neg, 1)

        def dve_xprobs(dve, h):
            s = xsmall[:, h, :]
            dve.wait_ge(xs_exp, 2 * h + 2)
            nc.vector.reciprocal(s[:, 6:8], s[:, 4:6]).then_inc(xs_inv, 1)
            dve.wait_ge(xs_inv, h + 1)
            for qt in range(2):
                a = xatt[:, h, qt * NX:(qt + 1) * NX]
                nc.vector.tensor_scalar(a, a, s[:, 6 + qt:7 + qt], None, ALU.mult).then_inc(xs_norm, 1)

        def dve_xlow(dve, h):
            dve.wait_ge(xo_hi, h + 1)
            nc.vector.tensor_tensor(oz_lo[:, 2 * h:2 * h + 2, :], two(ps[7][:, :]), oz_hi[:, 2 * h:2 * h + 2, :],
                                    ALU.subtract).then_inc(xo_lo, 1)

        uc, ug = first["up"]

        def pe_up(pe):
            hi, lo = x_rhs("packed")

            def body(i, edge):
                for j in range(4):
                    pe.wait_ge(w_lo, uc + 4 * i + j + 1)
                    out = start_group(pe, ug, 4, i, j)
                    head = edge and i == 0 and j == 0
                    strip(out[:, 0:NX], (uc + j) % RING, KT, hi, lo,
                          before=wait_x(pe, N_MLP) if head else None).then_inc(pe_done, 1)
                    if head:
                        pe_stat(pe, N_MLP, KT - 1, False)
                    if edge and i == 0 and j == 1:
                        pe_norm(pe, N_MLP, False)
            bodies(pe, F2T, 4, body)

        def act_up(act):
            def body(i, edge):
                for j in range(4):
                    split_hi(act, uc, 4, i, j + LEAD)
                    if edge and i == 0 and j == 0:
                        act_norm(act, N_MLP, False)
                    act.wait_ge(up_prod, 4 * i + j + 1)
                    nc.scalar.activation(hid(hid_hi, 4 * i + j, NX), hd[:, 0:NX], ACT.Copy).then_inc(up_hhi, 1)
            bodies(act, F2T, 4, body)

        def dve_up(dve):
            def low(u):
                dve.wait_ge(up_hhi, u + 1)
                nc.vector.tensor_tensor(hid(hid_lo, u, NX), hd[:, 0:NX], hid(hid_hi, u, NX), ALU.subtract).then_inc(up_hlo, 1)

            def body(i, edge):
                for j in range(4):
                    head = edge and i == 0 and j == 0
                    u = 4 * i + j
                    if head:
                        split_lo(dve, uc, 4, i, j + LEAD)
                        dve_norm(dve, N_MLP, False)
                    dve.wait_ge(pe_done, uc + 4 * i + j + 1)
                    if not head:
                        dve.wait_ge(up_prod, u)
                    nc.vector.tensor_tensor(tg[:, 0:NX], ps[banks[ug + j]][:, 0:NX], rstd[:, 0:NX], ALU.mult).then_inc(acc_free, 1)
                    dve.wait_ge(acc_free, ug + 4 * i + j + 1)
                    if not head:
                        dve.wait_ge(up_hlo, u)
                    nc.vector.scalar_tensor_tensor(hd[:, 0:NX], tg[:, 0:NX], 0.0, tg[:, 0:NX], ALU.max,
                                                   ALU.mult).then_inc(up_prod, 1)
                    if not head:
                        split_lo(dve, uc, 4, i, j + LEAD)
                    low(u)
            bodies(dve, F2T, 4, body)

        ffn_rhs = {w: (lambda t, w=w: (hid(hid_hi, t, w), hid(hid_lo, t, w))) for w in (T, NX)}
        block = ctx.enter_context(nc.Block())

        @block.sync
        def _(sp):
            sp.dma_start(raw[:, 0, 0:KT * P], io["w_f1in"][0]).then_inc(w_in[0], 16)
            for m in range(0, KT, 2):
                sp.dma_start(res[:, m, 0:T], io["res"][:, m, :]).then_inc(res_even, 16)
            for name, n, tiles, *_ in PHASES:
                c0 = first[name][0]
                w = io[f"w_{name}"]

                def load(j, i, sp=sp, c0=c0, tiles=tiles, w=w):
                    c = c0 + 4 * i + j
                    if not (isinstance(i, int) and c < RING):
                        sp.wait_ge(w_lo, c - (RING - 1))
                    sp.dma_start(raw[:, (c0 + j) % RING, 0:tiles * P], w[4 * i + j]).then_inc(w_in[(c0 + j) % RING], 16)

                for j in range(4):
                    if c0 + j:
                        load(j, 0)
                if n // 4 > 1:
                    with sp.Fori(1, n // 4) as i:
                        for j in range(4):
                            load(j, i)
                for j in range(n % 4):
                    load(j, n // 4)
            for m in range(KT):
                sp.wait_ge(out_tile, m + 1)
                sp.dma_start(io["out"][:, m, :], outb[:, m, :]).then_inc(out_done, 16)
            sp.wait_ge(out_done, 16 * KT)

        @block.gpsimd
        def _(pool):
            nc.gpsimd.memset(ones[:, :], 1.0).then_inc(ones_set, 1)
            nc.gpsimd.memset(epsc[:, 0:1], EPS).then_inc(ones_set, 1)
            nc.gpsimd.memset(epsc[:, 1:2], HD * EPS).then_inc(ones_set, 1)
            for dst, name in ((same, "same"), (swap, "swap"), (selneg, "selneg"), (convw, "convw")):
                pool.dma_start(dst[:, :], io[name]).then_inc(const_in, 16)
            pool.dma_start(posi[:, :], io["positions"]).then_inc(pos_in, 16)

            step = [0]

            def done(ins):
                step[0] += 1
                ins.then_inc(angle_step, 1)
                pool.wait_ge(angle_step, step[0])

            pool.wait_ge(pos_in, 16)
            pool.wait_ge(gain_in, 32)
            done(nc.gpsimd.tensor_copy(posf[:, :], posi[:, :]))
            done(nc.gpsimd.tensor_scalar(angle[:, :], posf[:, :], vecs[:, V_FREQ:V_FREQ + 1], None, ALU.mult))
            magic = 1.5 * 2.0 ** 23
            for period, bits in ((512 * np.pi, 10), (2 * np.pi, 15)):
                done(nc.gpsimd.tensor_scalar(turns[:, :], angle[:, :], float(1.0 / period), magic, ALU.mult, ALU.add))
                done(nc.gpsimd.tensor_scalar(turns[:, :], turns[:, :], -magic, None, ALU.add))
                rest = float(period)
                for p in range(3):
                    scale = 2.0 ** (np.floor(np.log2(abs(rest))) + 1 - bits)
                    piece = float(np.floor(rest / scale) * scale) if p < 2 else rest
                    rest -= piece
                    done(nc.gpsimd.tensor_scalar(part[:, :], turns[:, :], piece, None, ALU.mult))
                    done(nc.gpsimd.tensor_tensor(angle[:, :], angle[:, :], part[:, :], ALU.subtract))
            done(nc.gpsimd.tensor_scalar(angle[:, :], angle[:, :], 3.1415925, -3.1415925, ALU.min, ALU.max))
            assert step[0] == ANGLE_STEPS

            pool.wait_ge(pe_done, mc)
            nc.gpsimd.memset(table[:, :], NEG).then_inc(table_set, 1)
            pool.wait_ge(table_set, 1)
            pool.dma_start(table[0:BUCKETS, :], io["rel_table"]).then_inc(rel_const, 16)
            pool.dma_start(onehot[:, :], io["onehot"]).then_inc(rel_const, 16)
            nc.gpsimd.memset(mask[:, :], 0.0).then_inc(mask_set, 1)
            pool.wait_ge(mask_set, 1)
            for n, lo in enumerate((0, 2 * SEG)):
                nc.gpsimd.affine_select(out=mask[:, lo:lo + P], in_=mask[:, lo:lo + P], compare_op=ALU.is_ge, fill=NEG,
                                        base=0, pattern=[[-1, P]], channel_multiplier=1).then_inc(mask_set, 1)
                pool.wait_ge(mask_set, n + 2)
            nc.gpsimd.memset(small[:, :, :], 0.0).then_inc(mask_set, 1)
            pool.wait_ge(rel_row, 2)
            pool.dma_start(rel_dram.ap(), relrow[:, :]).then_inc(rel_out, 16)
            pool.wait_ge(rel_out, 16)
            rel_row_size = REL_X + REL_M
            copies = bass.AP(rel_dram, 0, [[0, P], [rel_row_size, HEADS], [1, rel_row_size]])
            pool.dma_start(rel_wide.ap(), copies).then_inc(rel_out, 16)
            pool.wait_ge(rel_out, 32)
            for col, n, start in ((0, P, 255), (P, META, REL_X + 255), (SEG, P, 127), (SEG + P, META, REL_X + 127),
                                  (2 * SEG, P, 255)):
                src = bass.AP(rel_wide, start, [[HEADS * rel_row_size - 1, P], [rel_row_size, HEADS], [1, n]])
                pool.dma_start(rel[:, :, col:col + n], src).then_inc(rel_in, 16)

            pool.wait_ge(pe_done, sc)
            nc.gpsimd.memset(glu[:, :, 0:TAPS - 1], 0.0).then_inc(glu_zero, 1)
            pool.dma_start(mem[:, :, :], io["mem"]).then_inc(mem_in, 16)
            pool.dma_start(decay[:, :, :], io["decay"]).then_inc(decay_in, 16)

        @block.scalar
        def _(act):
            act.dma_start(gains[:, :], io["gains"]).then_inc(gain_in, 16)
            act.dma_start(vecs[:, :], io["vecs"]).then_inc(gain_in, 16)
            for m in range(1, KT, 2):
                act.dma_start(res[:, m, 0:T], io["res"][:, m, :]).then_inc(res_odd, 16)
            act.dma_start(ident[:, :], io["ident"]).then_inc(ident_in, 16)
            act.wait_ge(gain_in, 32)
            act.wait_ge(ones_set, 3)
            split_hi(act, 0, 1, 0, 0)
            act.wait_ge(res_even, 16 * KT // 2)
            act.wait_ge(res_odd, 16 * KT // 2)
            for m in range(KT):
                act_prep(act, N_F1, m, True, True)
                if m in (3, 6):
                    split_hi(act, 0, 1, m // 3, 0)
            act_ff_in(act, "f1in", N_F1, T)
            act_residual(act, "f1out", N_MIX, True, 2)
            act_mix(act)
            act_branch(act)
            act_residual(act, "wo", N_F2, False, 1)
            act_ff_in(act, "f2in", N_F2, NX)
            act_residual(act, "f2out", N_MIXB, False, 2)
            act_mixb(act)
            act_residual(act, "wo2", N_XATT, False, 1)
            act_xattn(act)
            act_residual(act, "xo", N_MLP, False, 1)
            act_up(act)
            act_residual(act, "down", N_FINAL, False, 4, prep=False)
            act_norm(act, N_FINAL, False)

        @block.vector
        def _(dve):
            split_lo(dve, 0, 1, 0, 0)
            dve.wait_ge(gain_in, 32)
            for m in range(KT):
                dve_prep(dve, N_F1, m, True)
                if m in (3, 6):
                    split_lo(dve, 0, 1, m // 3, 0)
            dve_ff_in(dve, "f1in", N_F1, T)
            dve_residual(dve, "f1out", N_MIX, True, 2, 0.5)
            dve_mix(dve)
            dve_branch(dve)
            dve_residual(dve, "wo", N_F2, False, 1, 1.0)
            dve_ff_in(dve, "f2in", N_F2, NX)
            dve_residual(dve, "f2out", N_MIXB, False, 2, 0.5)
            dve.wait_ge(glu_zero, 1)
            dve.wait_ge(const_in, 64)
            dve_mixb(dve)
            dve_residual(dve, "wo2", N_XATT, False, 1, 1.0)
            dve_xattn(dve)
            dve_residual(dve, "xo", N_MLP, False, 1, 1.0)
            dve_up(dve)
            dve_residual(dve, "down", N_FINAL, False, 4, 1.0, prep=False)
            dve_norm(dve, N_FINAL, False)
            for m in range(KT):
                nc.vector.scalar_tensor_tensor(two(outb[:, m, :]), res_tile(m, False), gain(N_FINAL, m),
                                               two(rstd[:, 0:NX]), ALU.mult, ALU.mult).then_inc(out_tile, 1)

        @block.tensor
        def _(pe):
            pe.wait_ge(ones_set, 3)
            pe_ff_in(pe, "f1in", N_F1, T)
            pe_residual(pe, "f1out", N_MIX, True, 2, ffn_rhs[T], lambda k: pe.wait_ge(ffs["f1"]["hlo"], k + 1))
            pe.wait_ge(const_in, 64)
            pe_mix(pe)
            pe_branch(pe)
            pe_residual(pe, "wo", N_F2, False, 1, lambda t: (oy_hi[:, 8 + t, :], oy_lo[:, 8 + t, :]),
                        lambda k: pe.wait_ge(y_lo, k + 1))
            pe_ff_in(pe, "f2in", N_F2, NX)
            pe_residual(pe, "f2out", N_MIXB, False, 2, ffn_rhs[NX], lambda k: pe.wait_ge(ffs["f2"]["hlo"], k + 1))
            pe_mixb(pe)
            pe_residual(pe, "wo2", N_XATT, False, 1, lambda t: (oz_hi[:, t, :], oz_lo[:, t, :]),
                        lambda k: pe.wait_ge(z_lo, k + 1) if k < 4 else pe.wait_ge(c_lo, k - 3))
            pe_xattn(pe)
            pe_residual(pe, "xo", N_MLP, False, 1, lambda t: (oz_hi[:, t, :], oz_lo[:, t, :]),
                        lambda k: pe.wait_ge(xo_lo, k // 2 + 1))
            pe_up(pe)
            pe_residual(pe, "down", N_FINAL, False, 4, ffn_rhs[NX], lambda k: pe.wait_ge(up_hlo, k + 1))
            pe_stat(pe, N_FINAL, KT - 1, False)
            pe_norm(pe, N_FINAL, False)


def shape_constants():
    eye = np.eye(P, dtype=np.float32)
    block = np.kron(np.eye(2), np.ones((HD, HD))).astype(np.float32)
    half = RDK // 2
    swap = np.zeros((P, P), np.float32)
    for h in range(P // RDK):
        for i in range(half):
            swap[h * RDK + half + i, h * RDK + i] = -1.0
            swap[h * RDK + i, h * RDK + half + i] = 1.0
    selneg = np.zeros((HEADS, HEADS, P), np.float32)
    for h in range(HEADS):
        selneg[h, h, :] = -1.0
    freq = np.float32(10000.0) ** (-np.arange(half, dtype=np.float32) / np.float32(half))
    freq = np.tile(freq, P // half).astype(np.float32).reshape(P, 1)

    def bucket(d):
        small = BUCKETS // 2
        large = small + int(np.log(max(d, 1) / small) / np.log(128 / small) * (BUCKETS - small) + 1e-9)
        return max(d, 0) if d < small else min(large, BUCKETS - 1)

    onehot = np.zeros((BUCKETS + 1, REL_X + REL_M), np.float32)
    for v in range(REL_X):
        d = 255 - v
        onehot[bucket(d) if 0 <= d < WINDOW else BUCKETS, v] = 1.0
    for v in range(REL_M):
        onehot[bucket(271 - v), REL_X + v] = 1.0
    log_g = np.log1p(-np.exp2(-5.0 - np.arange(HEADS)))
    j, i = np.arange(P)[:, None], np.arange(NX)[None, :]
    seen = j // HD <= i // HD
    full = np.exp(log_g[:, None, None] * np.abs(i - j)) * seen * RDK ** -0.5
    decay = np.concatenate([full, full[:, :, 0:P]], axis=2).transpose(1, 0, 2)
    return {"ident": eye, "same": block, "swap": swap, "selneg": selneg.reshape(HEADS, HEADS * P), "freq": freq,
            "onehot": onehot, "decay": np.ascontiguousarray(decay.astype(np.float32))}


def strips(w, tiles=KT):
    k, m = w.shape
    a = w.reshape(k // P // tiles, tiles, P, m // P, P).transpose(3, 0, 2, 1, 4)
    return a.reshape(-1, P, tiles * P)


def kernel(**inputs):
    import concourse.bacc as bacc
    from concourse.bass_utils import run_bass_kernel_spmd as run

    a = {k: np.asarray(v) for k, v in inputs.items()}
    const = shape_constants()

    def turns(x, y):
        return np.stack([strips(x), strips(y)], axis=1).reshape(-1, P, KT * P)

    def columns(v):
        return v.reshape(-1, P).T

    arrays = {}
    for f, name in (("f1", "ffn1"), ("f2", "ffn2")):
        w_in, w_out = a[f"{name}_w_in"][0], a[f"{name}_w_out"][0]
        arrays[f"w_{f}in"] = turns(w_in[:, :FF], w_in[:, FF:])
        arrays[f"w_{f}out"] = strips(w_out, WIDE)
    w = a["w_in"][0]
    cut = np.cumsum([512, 512, 512, HEADS, 512, 128, 128, D])
    fq, fk, fv, ff, sq_, sk, sv, ga, gb = np.split(w, cut, axis=1)
    forget = np.zeros((D, P), w.dtype)
    forget[:, :HEADS] = ff
    order = np.concatenate([np.arange(HD) + HD * h for t in range(4) for h in (t, t + 4)])
    arrays["w_mix"] = np.concatenate([strips(x) for x in (forget, fk, fq, sk, sq_[:, order], fv, sv)] + [turns(ga, gb)])
    arrays["w_branch"] = np.concatenate([strips(a["w_branch_fox"][0], 4), strips(a["w_branch_swa"][0][order], 4)], axis=2)
    arrays["w_wo"] = strips(a["w_out"][0])
    w = a["w_in_2"]
    ca, cb, rq, rk, rv, rg = np.split(w, np.cumsum([512, 512, 256, 256, 512]), axis=1)
    arrays["w_mixb"] = np.concatenate([turns(cb, ca)] + [strips(x) for x in (rq, rk, rv, rg)])
    arrays["w_memk"], arrays["w_memv"] = strips(a["xkv_w_2"][:, :D]), strips(a["xkv_w_2"][:, D:])
    arrays["w_wo2"] = strips(np.roll(a["w_out_2"], CONV, axis=0))
    arrays["w_xq"], arrays["w_xo"] = strips(a["xq_w_2"]), strips(a["xo_w_2"])
    arrays["w_up"], arrays["w_down"] = strips(a["mlp_up_w_2"]), strips(a["mlp_down_w_2"])

    x, meta = a["x"][0], a["meta_tokens"]
    tokens = np.concatenate([x[:P], meta, x[P:]])
    arrays["res"] = tokens.T.reshape(KT, P, T).transpose(1, 0, 2)
    arrays["mem"] = a["mem_2"][0].T.reshape(KT, P, NX).transpose(1, 0, 2)
    arrays["gains"] = np.concatenate([columns(a[k].reshape(-1)) for k in (
        "ffn1_norm", "mix_norm", "ffn2_norm", "norm_mix_w_2", "norm_xattn_w_2", "norm_mlp_w_2", "norm_f_w_2",
        "norm_mem_w_2")], axis=1)
    twice = [np.tile(a[k][0], 2).reshape(P, 1) for k in ("fox_q_norm", "fox_k_norm", "swa_q_norm", "swa_k_norm")]
    fbias = np.zeros((P, 1), np.float32)
    fbias[:HEADS, 0] = a["forget_bias"][0]
    arrays["vecs"] = np.concatenate(twice + [fbias, const["freq"]] + [
        columns(a[k]) for k in ("conv_b_2", "conv_ln_w_2", "conv_ln_b_2", "ret_gn_w_2")
    ] + [np.broadcast_to(a["swa_sinks"][0], (P, HEADS))], axis=1)
    arrays["convw"] = a["conv_w_2"].T.reshape(4, P, TAPS).transpose(1, 0, 2).reshape(P, 4 * TAPS)
    arrays["positions"] = np.broadcast_to(a["positions_2"].reshape(1, NX), (P, NX))
    arrays["rel_table"] = a["rel_bias_table"]
    for k in ("ident", "same", "swap", "selneg", "onehot", "decay"):
        arrays[k] = const[k]

    nc = bacc.Bacc("TRN2", target_bir_lowering=False, num_devices=1)
    arrays = {f"in_{k}": np.ascontiguousarray(v) for k, v in arrays.items()}
    io = {k[3:]: nc.dram_tensor(k, v.shape, mybir.dt.from_np(v.dtype), kind="ExternalInput").ap()
          for k, v in arrays.items()}
    io["out"] = nc.dram_tensor("out", (P, KT, NX), F32, kind="ExternalOutput").ap()
    build(nc, io)
    got = run(nc, [arrays], core_ids=[0]).results[0]["out"]
    return np.ascontiguousarray(got.transpose(2, 1, 0).reshape(1, NX, D))
```

```python
from contextlib import ExitStack

import numpy as np

import concourse.bass as bass
from concourse import mybir

F32 = mybir.dt.float32
F32R = mybir.dt.float32r
I32 = mybir.dt.int32
ALU = mybir.AluOpType
ACT = mybir.ActivationFunctionType
AX = mybir.AxisListType

P = 128
D = 1024
KT = D // P
HALF = KT // 2
NX = 256
META = 16
T = NX + META
SEG = P + META
W2 = 2 * SEG
FF = 2816
FT = FF // P
FF2 = 4096
F2T = FF2 // P
HEADS = 8
HD = 64
EPS = 1e-6
NEG = -1e30
WINDOW = 128
BUCKETS = 32
CONV = 512
TAPS = 31
XH_DIM = 256
XHEADS = 4
RDK = 32
RING = 4
LEAD = 3
WIDE = 11

PHASES = [
    ("f1in", 2 * FT, KT, 2 * FT, 4), ("f1out", 2 * KT, WIDE, KT, 2),
    ("mix", 35, KT, 35, 3), ("branch", KT, KT, 2 * KT, 4), ("wo", KT, KT, KT, 4),
    ("f2in", 2 * FT, KT, 2 * FT, 4), ("f2out", 2 * KT, WIDE, KT, 2),
    ("mixb", 20, KT, 20, 3), ("memk", KT, KT, KT, 3), ("wo2", KT, KT, KT, 4),
    ("xq", KT, KT, KT, 3), ("memv", KT, KT, KT, 3), ("xo", KT, KT, KT, 4),
    ("up", F2T, KT, F2T, 4), ("down", 4 * KT, KT, KT, 2),
]
V_FOXQ, V_FOXK, V_SWAQ, V_SWAK, V_FBIAS, V_FREQ, V_CONVB, V_LNW, V_LNB, V_GNW, V_SINK = (
    0, 1, 2, 3, 4, 5, 6, 10, 14, 18, 22)
V_COLS = V_SINK + HEADS
N_F1, N_MIX, N_F2, N_MIXB, N_XATT, N_MLP, N_FINAL, N_MEM = range(8)

ANGLE_STEPS = 19
REL_X = 384
REL_M = 272


def plan():
    first, sizes, banks = {}, [], []
    for name, n, tiles, groups, ring in PHASES:
        first[name] = (len(sizes), len(banks))
        sizes += [tiles] * n
        banks += [(len(banks) + i) % ring for i in range(groups)]
    need = [max([p + 1 for p in range(g) if banks[p] == b], default=0) for g, b in enumerate(banks)]
    return first, sizes, banks, need


def build(nc, io):
    first, sizes, banks, need = plan()
    C = len(sizes)
    counts = {name: n for name, n, *_ in PHASES}
    plain = range(first["memk"][0], first["memk"][0] + KT)

    def splits(c, like=None):
        at = c if like is None else like
        assert at not in plain
        return c + 1 - (len(plain) if at > plain[0] else 0)

    ctx = ExitStack()
    with ctx:
        def sem(name):
            return ctx.enter_context(nc.semaphore(name))

        top = [((nc.sbuf_base + 63) // 64) * 64]

        def place(name, shape, dt=F32, at=None):
            size = int(np.prod(shape[1:])) * 4
            size = (size + 31) // 32 * 32
            where = top[0] if at is None else at[0]
            t = nc.alloc_sbuf_tensor_at(name, shape, dt, offset=where)
            if at is None:
                top[0] += size
            else:
                at[0] += size
                assert at[0] <= nc.sbuf_usable_end, (name, at[0])
            return t

        raw = place("raw", [P, RING, WIDE * P])
        whi = place("whi", [P, RING, WIDE * P], F32R)
        wlo = place("wlo", [P, RING, WIDE * P], F32R)
        xhi = place("xhi", [P, KT, W2], F32R)
        xlo = place("xlo", [P, KT, W2], F32R)
        res = place("res", [P, KT, W2])
        ones = place("ones", [P, P])
        same = place("same_head", [P, P])
        ident = place("ident", [P, P])
        swap = place("swap", [P, P])
        gains = place("gains", [P, 8 * KT])
        vecs = place("vecs", [P, V_COLS])
        convw = place("convw", [P, 4 * TAPS])
        epsc = place("epsc", [P, 2])
        rstd = place("rstd", [P, W2])
        root = place("root", [P, 4])
        inv = place("inv", [P, 4])
        sqsum = place("sqsum", [P, W2])
        work_at = top[0]
        sq = place("sq", [P, 2, W2])
        tg = place("tg", [P, W2])
        tu = place("tu", [P, W2])
        sg = place("sg", [P, W2])
        hd = place("hd", [P, W2])
        qk_root = place("qk_root", [P, 2, 6])
        qk_inv = place("qk_inv", [P, 2, 6])
        angle = place("angle", [P, NX])
        area = top[0]

        at = [area]
        hid_hi = place("hid_hi", [P, F2T * NX], F32R, at)
        hid_lo = place("hid_lo", [P, F2T * NX], F32R, at)

        at = [area]
        oy_hi = place("oy_hi", [P, 16, NX], F32R, at)
        oy_lo = place("oy_lo", [P, 16, NX], F32R, at)
        qn = place("qn", [P, 8, NX], F32, at)
        kn = place("kn", [P, 5, T], F32, at)
        v0 = place("v0", [P, 640], F32, at)
        v1 = place("v1", [P, 640], F32, at)
        vm = place("vm", [META, 640], F32, at)
        gate_at = at[0]
        gate = place("gate", [P, 16, NX], F32, at)
        ckb = place("ckb", [P, HEADS, T], F32, at)
        rel = place("rel", [P, HEADS, SEG + T], F32, at)
        att = place("att", [P, 2, SEG + T], F32, at)
        mask = place("mask", [P, SEG + T], F32, at)
        cq = place("cq", [P, 16], F32, at)
        qk_wide = place("qk_wide", [P, 2, 6 * HD], F32, at)
        small = place("small", [P, 2, 12], F32, at)
        at = [work_at]
        bm = place("bm", [P, SEG + T], F32, at)
        pts = place("pts", [P, 2, 384], F32, at)
        ptm = place("ptm", [META, 2, NX], F32, at)
        at = [gate_at]
        fa = place("fa", [HEADS, T], F32, at)
        fabs = place("fabs", [HEADS, T], F32, at)
        fexp = place("fexp", [HEADS, T], F32, at)
        fmin = place("fmin", [HEADS, T], F32, at)
        flog = place("flog", [HEADS, T], F32, at)
        fones = place("fones", [HEADS, T], F32, at)
        cum = place("cum", [HEADS, T], F32, at)
        table = place("table", [BUCKETS + 1, HEADS], F32, at)
        onehot = place("onehot", [BUCKETS + 1, REL_X + REL_M], F32, at)
        relrow = place("relrow", [HEADS, REL_X + REL_M], F32, at)
        vt = place("vt", [P, 2, T], F32, at)
        assert at[0] <= gate_at + 16 * NX * 4

        at = [area]
        oz_hi = place("oz_hi", [P, 8, NX], F32R, at)
        oz_lo = place("oz_lo", [P, 8, NX], F32R, at)
        mem_hi = place("mem_hi", [P, KT, NX], F32R, at)
        mem_lo = place("mem_lo", [P, KT, NX], F32R, at)
        mem = place("mem", [P, KT, NX], F32, at)
        km = place("km", [P, KT, NX], F32, at)
        glu_at = at[0]
        glu = place("glu", [P, 4, TAPS - 1 + NX], F32, at)
        cy = place("cy", [P, 4, NX], F32, at)
        qr = place("qr", [P, 4, NX], F32, at)
        v2_at = at[0]
        v2 = place("v2", [P, 2, 512], F32, at)
        rg = place("rg", [P, 4, NX], F32, at)
        cosv = place("cosv", [P, NX], F32, at)
        sinv = place("sinv", [P, NX], F32, at)
        amat = place("amat", [P, 2, 384], F32, at)
        yr = place("yr", [P, 2, NX], F32, at)
        zt = place("zt", [P, 2, NX], F32, at)
        csq = place("csq", [P, 4, NX], F32, at)
        memr = place("memr", [P, NX], F32, at)
        col_root = place("col_root", [P, 3, 4], F32, at)
        col_inv = place("col_inv", [P, 3, 4], F32, at)
        msq = place("msq", [P, 2, NX], F32, at)
        decay_at = at[0]
        decay = place("decay", [P, HEADS, 384], F32, at)
        at = [glu_at]
        qx = place("qx", [P, KT, NX], F32, at)
        at = [v2_at]
        vmem = place("vmem", [P, 2, D], F32, at)
        at = [decay_at]
        xatt = place("xatt", [P, XHEADS, 512], F32, at)
        xpt = place("xpt", [P, 2, 512], F32, at)
        xsmall = place("xsmall", [P, XHEADS, 8], F32, at)

        at = [area + 2 * F2T * NX * 4]
        posi = place("posi", [P, NX], I32, at)
        posf = place("posf", [P, NX], F32, at)
        turns = place("turns", [P, NX], F32, at)
        part = place("part", [P, NX], F32, at)
        at = [area]
        outb = place("outb", [P, KT, NX], F32, at)

        ps = [ctx.enter_context(nc.psum_tensor(f"bank{i}", [P, 512], F32)) for i in range(8)]
        STAT = ps[4]

        rel_dram = nc.dram_tensor("rel_rows", (HEADS, REL_X + REL_M), F32, kind="Internal")
        cum_dram = nc.dram_tensor("cum_rows", (HEADS, T), F32, kind="Internal")
        rel_wide = nc.dram_tensor("rel_copies", (P, HEADS, REL_X + REL_M), F32, kind="Internal")

        w_in = [sem(f"w_in{s}") for s in range(RING)]
        w_hi = sem("w_hi")
        w_lo = sem("w_lo")
        pe_done = sem("pe_done")
        acc_free = sem("acc_free")
        x_hi, x_lo = sem("x_hi"), sem("x_lo")
        sq_ready = sem("sq_ready")
        sq_added = sem("sq_added")
        stat_mm = sem("stat_mm")
        norm_sd, norm_inv, norm_bc, norm_r = (sem(s) for s in ("norm_sd", "norm_inv", "norm_bc", "norm_r"))
        res_low, res_high = sem("res_low"), sem("res_high")
        gain_in, vec_in, ident_in = sem("gain_in"), sem("vec_in"), sem("ident_in")
        const_in, pos_in = sem("const_in"), sem("pos_in")
        ones_set, mask_set = sem("ones_set"), sem("mask_set")
        angle_step = sem("angle_step")
        ffs = {f: {s: sem(f"{f}_{s}") for s in ("silu", "prod", "hhi", "hlo")} for f in ("f1", "f2")}
        up_prod, up_hhi, up_hlo = sem("up_prod"), sem("up_hhi"), sem("up_hlo")
        out_tile, out_done = sem("out_tile"), sem("out_done")
        qk_sq, qk_ss, qk_sd, qk_r, qk_bc, qk_n = (
            sem(s) for s in ("qk_sq", "qk_ss", "qk_sd", "qk_r", "qk_bc", "qk_n"))
        qk_inv_set = sem("qk_inv_set")
        v_tr, v_copied = sem("v_tr"), sem("v_copied")
        f_act, f_dve = sem("f_act"), sem("f_dve")
        cq_mm, cq_copied, ck_out, ck_in = (sem(s) for s in ("cq_mm", "cq_copied", "ck_out", "ck_in"))
        table_set, rel_const, rel_mm, rel_row, rel_out, rel_in = (
            sem(s) for s in ("table_set", "rel_const", "rel_mm", "rel_row", "rel_out", "rel_in"))
        at_s, at_bias, at_max, at_neg, at_exp, at_sum, at_inv, at_norm = (
            sem(s) for s in ("at_s", "at_bias", "at_max", "at_neg", "at_exp", "at_sum", "at_inv", "at_norm"))
        at_tr, at_pt, at_pv, o_hi, o_lo = (sem(s) for s in ("at_tr", "at_pt", "at_pv", "o_hi", "o_lo"))
        sig_done, y_step, y_hi, y_lo = (sem(s) for s in ("sig_done", "y_step", "y_hi", "y_lo"))
        decay_in, mem_in, glu_zero = sem("decay_in"), sem("mem_in"), sem("glu_zero")
        cs_act, cs_dve = sem("cs_act"), sem("cs_dve")
        cb_sig, glu_done, conv_step = sem("cb_sig"), sem("glu_done"), sem("conv_step")
        rot_mm, rot_step, rg_done = sem("rot_mm"), sem("rot_step"), sem("rg_done")
        m_scaled, m_hi, m_lo, m_sq, m_stat, m_sd, m_inv, m_bc, m_r = (
            sem(s) for s in ("m_scaled", "m_hi", "m_lo", "m_sq", "m_stat", "m_sd", "m_inv", "m_bc", "m_r"))
        rv_tr, rv_copied = sem("rv_tr"), sem("rv_copied")
        ra_mm, ra_dec, ry_mm, ry_copied = (sem(s) for s in ("ra_mm", "ra_dec", "ry_mm", "ry_copied"))
        gn_mu, gn_cen, gn_sq, gn_var, gn_sd, gn_r, gn_bc, gn_n, gn_z = (
            sem(s) for s in ("gn_mu", "gn_cen", "gn_sq", "gn_var", "gn_sd", "gn_r", "gn_bc", "gn_n", "gn_z"))
        ln_mu, ln_cen, ln_sq, ln_var, ln_sd, ln_r, ln_bc, ln_n, ln_z = (
            sem(s) for s in ("ln_mu", "ln_cen", "ln_sq", "ln_var", "ln_sd", "ln_r", "ln_bc", "ln_n", "ln_z"))
        z_hi, z_lo = sem("z_hi"), sem("z_lo")
        c_hi, c_lo = sem("c_hi"), sem("c_lo")
        xv_tr, xv_copied = sem("xv_tr"), sem("xv_copied")
        xs_s, xs_max, xs_neg, xs_exp, xs_inv, xs_norm, xs_tr, xs_pt, xs_pv, xo_hi, xo_lo = (
            sem(s) for s in ("xs_s", "xs_max", "xs_neg", "xs_exp", "xs_inv", "xs_norm", "xs_tr", "xs_pt",
                             "xs_pv", "xo_hi", "xo_lo"))

        def seg(ap):
            return ap.rearrange("p (s t) -> p s t", s=2)[:, :, 0:P]

        def two(ap):
            return ap.rearrange("p (s t) -> p s t", s=2)

        def res_tile(m, full):
            return res[:, m, 0:T] if full else seg(res[:, m, :])

        def x_tile(t, m, full):
            return t[:, m, 0:T] if full else two(t[:, m, 0:NX])

        def flat_or_two(ap, full):
            return ap[:, 0:T] if full else two(ap[:, 0:NX])

        def gain(n, m):
            return gains[:, n * KT + m:n * KT + m + 1] if isinstance(m, int) else gains[:, bass.ds(m + n * KT, 1)]

        def hid(t, j, n):
            return t[:, 0:FT * T].rearrange("p (j t) -> p j t", t=n)[:, j, :] if n == T else \
                t[:, 0:F2T * NX].rearrange("p (j t) -> p j t", t=n)[:, j, :]

        def bodies(eng, n, per, body):
            count = n // per
            body(0, True)
            if count > 3:
                with eng.Fori(1, count - 1) as i:
                    body(i, False)
            else:
                for i in range(1, count - 1):
                    body(i, False)
            if count > 1:
                body(count - 1, True)

        def split_hi(act, c0, per, i, j):
            static = isinstance(i, int)
            c = c0 + per * i + j
            if static and (c >= C or c in plain):
                return
            s = (c if static else c0 + j) % RING
            tiles = sizes[c] if static else sizes[c0 + per + j]
            act.wait_ge(w_in[s], (c // RING + 1) * 16 if static else (per // RING * i + ((c0 + j) // RING + 1)) * 16)
            if not (static and c < RING):
                act.wait_ge(pe_done, c - (RING - 1))
            nc.scalar.activation(whi[:, s, 0:tiles * P], raw[:, s, 0:tiles * P], ACT.Copy).then_inc(w_hi, 1)

        def split_lo(dve, c0, per, i, j):
            static = isinstance(i, int)
            c = c0 + per * i + j
            if static and (c >= C or c in plain):
                return
            s = (c if static else c0 + j) % RING
            tiles = sizes[c] if static else sizes[c0 + per + j]
            dve.wait_ge(w_hi, splits(c, None if static else c0 + per + j))
            nc.vector.tensor_tensor(wlo[:, s, 0:tiles * P], raw[:, s, 0:tiles * P], whi[:, s, 0:tiles * P],
                                    ALU.subtract).then_inc(w_lo, 1)

        def start_group(pe, g0, per, i, j):
            if isinstance(i, int):
                if need[g0 + per * i + j]:
                    pe.wait_ge(acc_free, need[g0 + per * i + j])
            else:
                pe.wait_ge(acc_free, need[g0 + per + j] + per * (i - 1))
            return ps[banks[g0 + (per if not isinstance(i, int) else per * i) + j]]

        def strip(out, s, tiles, rhs_hi, rhs_lo, start=True, stop=True, at=0, before=None, begin=0, end=None):
            for t in range(begin, tiles if end is None else end):
                if before is not None:
                    before(t)
                w = slice((at + t) * P, (at + t + 1) * P)
                nc.tensor.matmul(out, whi[:, s, w], rhs_hi(t), start=start and t == 0, stop=False)
                nc.tensor.matmul(out, whi[:, s, w], rhs_lo(t), start=False, stop=False)
                mm = nc.tensor.matmul(out, wlo[:, s, w], rhs_hi(t), start=False, stop=stop and t == tiles - 1)
            return mm

        def token_sums(out, src, toks, cols, start, stop):
            n = cols.shape[-1]
            for b, tok in enumerate(toks):
                mm = nc.tensor.matmul(out[:, b * n:(b + 1) * n], src[:, tok:tok + P], cols, start=start and b == 0,
                                      stop=stop and b == len(toks) - 1)
            return mm

        def spread(out, values, toks):
            for b, tok in enumerate(toks):
                mm = nc.tensor.transpose(out[:, tok:tok + P], values[:, b:b + 1].to_broadcast([P, P]), ident[:, :])
            return mm

        def blocks(width):
            return (0, P, SEG) if width == T else (0, P)

        one_col = ones[:, 0:1]
        head_cols = same[:, :].rearrange("p (h d) -> p h d", h=2)[:, :, 0]

        def pe_stat(pe, n, full):
            pe.wait_ge(sq_added, (KT - 1) * (n + 1))
            if n:
                pe.wait_ge(norm_r, n)
            token_sums(STAT, sqsum, blocks(T if full else NX), one_col, True, True).then_inc(stat_mm, 1)

        def pe_norm(pe, n, full):
            pe.wait_ge(norm_inv, n + 1)
            if n == 0:
                pe.wait_ge(ident_in, 16)
            spread(STAT[:, P:], inv, blocks(T if full else NX)).then_inc(norm_bc, 1)

        def act_prep(act, n, m, full, prep, par):
            static = isinstance(m, int)
            before = (KT - 1) * n + max(m - 2, 0) if static else m + ((KT - 1) * n - 2)
            if static and m == 0:
                if n:
                    act.wait_ge(stat_mm, n)
            elif not static or before:
                act.wait_ge(sq_added, before)
            if prep:
                act_x(n, m, full)
            act_square(n, m, full, par)

        def act_x(n, m, full):
            nc.scalar.activation(x_tile(xhi, m, full), res_tile(m, full), ACT.Copy, scale=gain(n, m)).then_inc(x_hi, 1)

        def act_square(n, m, full, par):
            dst = sqsum if isinstance(m, int) and m == 0 else sq[:, par, :]
            nc.scalar.activation(flat_or_two(dst, full), res_tile(m, full), ACT.Square).then_inc(sq_ready, 1)

        def dve_square(dve, n, m, full, par):
            if isinstance(m, int) and m == 0:
                return
            width = T if full else NX
            dve.wait_ge(sq_ready, m + (KT * n + 1))
            if not (isinstance(m, int) and m == 1):
                dve.wait_ge(sq_added, m + ((KT - 1) * n - 1))
            nc.vector.tensor_tensor(sqsum[:, 0:width], sqsum[:, 0:width], sq[:, par, 0:width], ALU.add).then_inc(sq_added, 1)

        def dve_prep(dve, n, m, full):
            dve.wait_ge(x_hi, m + (KT * n + 1))
            nc.vector.scalar_tensor_tensor(x_tile(xlo, m, full), res_tile(m, full), gain(n, m),
                                           x_tile(xhi, m, full), ALU.mult, ALU.subtract).then_inc(x_lo, 1)

        def act_norm(act, n, full):
            width = T if full else NX
            nb = len(blocks(width))
            act.wait_ge(stat_mm, n + 1)
            nc.scalar.activation(root[:, 0:nb], STAT[:, 0:nb], ACT.Sqrt, bias=epsc[:, 0:1],
                                 scale=1.0 / D).then_inc(norm_sd, 1)
            act.wait_ge(norm_bc, n + 1)
            nc.scalar.activation(rstd[:, 0:width], STAT[:, P:P + width], ACT.Copy).then_inc(norm_r, 1)

        def dve_norm(dve, n, full):
            nb = len(blocks(T if full else NX))
            dve.wait_ge(norm_sd, n + 1)
            nc.vector.reciprocal(inv[:, 0:nb], root[:, 0:nb]).then_inc(norm_inv, 1)
            dve.wait_ge(norm_r, n + 1)

        def x_rhs(full_rows):
            if full_rows == "all":
                return (lambda t: xhi[:, t, 0:T]), (lambda t: xlo[:, t, 0:T])
            if full_rows == "x":
                return (lambda t: seg(xhi[:, t, :])), (lambda t: seg(xlo[:, t, :]))
            return (lambda t: xhi[:, t, 0:NX]), (lambda t: xlo[:, t, 0:NX])

        def wait_x(pe, n):
            return lambda t: pe.wait_ge(x_lo, KT * n + t + 1)

        def pe_ff_in(pe, name, n, width):
            c0, g0 = first[name]
            hi, lo = x_rhs("all" if width == T else "packed")

            def body(i, edge):
                for j in range(4):
                    pe.wait_ge(w_lo, splits(c0 + 4 * i + j, c0 + j))
                    out = start_group(pe, g0, 4, i, j)
                    head = edge and i == 0 and j == 0
                    strip(out[:, 0:width], (c0 + j) % RING, KT, hi, lo,
                          before=wait_x(pe, n) if head else None).then_inc(pe_done, 1)
                    if head:
                        pe_stat(pe, n, width == T)
                    if edge and i == 0 and j == 1:
                        pe_norm(pe, n, width == T)
            bodies(pe, counts[name], 4, body)

        def act_ff_in(act, name, n, width):
            c0, g0 = first[name]
            f = ffs[name[:2]]

            def body(i, edge):
                for j in range(4):
                    split_hi(act, c0, 4, i, j + LEAD)
                    if edge and i == 0 and j == 0:
                        act_norm(act, n, width == T)
                    u = 2 * i + j // 2
                    if j % 2 == 0:
                        act.wait_ge(acc_free, g0 + 4 * i + j + 1)
                        nc.scalar.activation(sg[:, 0:width], tg[:, 0:width], ACT.Silu).then_inc(f["silu"], 1)
                    else:
                        act.wait_ge(f["prod"], u + 1)
                        nc.scalar.activation(hid(hid_hi, u, width), hd[:, 0:width], ACT.Copy).then_inc(f["hhi"], 1)
            bodies(act, counts[name], 4, body)

        def dve_ff_in(dve, name, n, width):
            c0, g0 = first[name]
            f = ffs[name[:2]]

            def hidden_lo(u):
                dve.wait_ge(f["hhi"], u + 1)
                nc.vector.tensor_tensor(hid(hid_lo, u, width), hd[:, 0:width], hid(hid_hi, u, width),
                                        ALU.subtract).then_inc(f["hlo"], 1)

            def body(i, edge):
                for j in range(4):
                    head = edge and i == 0 and j == 0
                    if head:
                        split_lo(dve, c0, 4, i, j + LEAD)
                        dve_norm(dve, n, width == T)
                    out = ps[banks[g0 + j]][:, 0:width]
                    u = 2 * i + j // 2
                    dve.wait_ge(pe_done, c0 + 4 * i + j + 1)
                    if j % 2 == 0:
                        nc.vector.tensor_tensor(tg[:, 0:width], out, rstd[:, 0:width], ALU.mult).then_inc(acc_free, 1)
                        if not head:
                            hidden_lo(u - 1)
                    else:
                        nc.vector.tensor_tensor(tu[:, 0:width], out, rstd[:, 0:width], ALU.mult).then_inc(acc_free, 1)
                        dve.wait_ge(f["silu"], u + 1)
                        dve.wait_ge(acc_free, g0 + 4 * i + j + 1)
                        nc.vector.tensor_tensor(hd[:, 0:width], tu[:, 0:width], sg[:, 0:width],
                                                ALU.mult).then_inc(f["prod"], 1)
                    if not head:
                        split_lo(dve, c0, 4, i, j + LEAD)
            bodies(dve, counts[name], 4, body)
            hidden_lo(FT - 1)

        def pe_residual(pe, name, cpm, width, rhs, ready, late=0):
            c0, g0 = first[name]
            tiles = sizes[c0]
            per = 2 * cpm if cpm > 1 else 4
            mpb = per // cpm

            def one(out, j, **part):
                q = j % cpm
                return strip(out, (c0 + j) % RING, tiles, lambda t: rhs(q * tiles + t)[0],
                             lambda t: rhs(q * tiles + t)[1], start=q == 0, stop=q == cpm - 1, **part)

            def head():
                outs = []
                for j in range(2):
                    pe.wait_ge(w_lo, splits(c0 + j))
                    outs.append(start_group(pe, g0, mpb, 0, j)[:, 0:width])
                    one(outs[j], j, end=tiles - late, before=None if j else ready)
                for j in range(2):
                    one(outs[j], j, begin=tiles - late, before=None if j else ready).then_inc(pe_done, 1)

            def body(i, edge):
                opening = edge and i == 0
                if opening and late:
                    head()
                for j in range(2 if opening and late else 0, per):
                    q, m = j % cpm, j // cpm
                    pe.wait_ge(w_lo, splits(c0 + per * i + j, c0 + j))
                    if q == 0:
                        out = start_group(pe, g0, mpb, i, m)[:, 0:width]
                    wait = (lambda t: ready(q * tiles + t)) if opening and m == 0 else None
                    one(out, j, before=wait).then_inc(pe_done, 1)
            bodies(pe, counts[name], per, body)

        def act_residual(act, name, n, full, cpm, prep=True):
            c0, g0 = first[name]
            per = 2 * cpm if cpm > 1 else 4
            mpb = per // cpm

            def body(i, edge):
                for j in range(per):
                    split_hi(act, c0, per, i, j + LEAD)
                    if j % cpm == cpm - 1:
                        m = j // cpm
                        act.wait_ge(acc_free, g0 + mpb * i + m + 1)
                        act_prep(act, n, mpb * i + m, full, prep, par=m % 2)
            bodies(act, counts[name], per, body)

        def dve_residual(dve, name, n, full, cpm, scale, prep=True):
            c0, g0 = first[name]
            width = T if full else NX
            per = 2 * cpm if cpm > 1 else 4
            mpb = per // cpm

            def body(i, edge):
                for j in range(per):
                    if j % cpm == cpm - 1:
                        m = j // cpm
                        k = mpb * i + m
                        out = ps[banks[g0 + (mpb * i if isinstance(i, int) else mpb) + m]]
                        dve.wait_ge(pe_done, c0 + per * i + j + 1)
                        nc.vector.scalar_tensor_tensor(res_tile(k, full), flat_or_two(out, full), scale,
                                                       res_tile(k, full), ALU.mult, ALU.add).then_inc(acc_free, 1)
                        last = edge and isinstance(k, int) and k == KT - 1
                        if last:
                            if prep:
                                dve_prep(dve, n, k, full)
                            dve_square(dve, n, k, full, m % 2)
                    split_lo(dve, c0, per, i, j + LEAD)
                    if j % cpm == cpm - 1 and not last:
                        if prep:
                            dve_prep(dve, n, k, full)
                        dve_square(dve, n, k, full, m % 2)
            bodies(dve, counts[name], per, body)

        mc, mg = first["mix"]
        QKT = 13
        V_FIRST, GATES = 14, 19
        UNITS = 16
        STEP0 = 18

        def qk_tile(t):
            if t < 4:
                return kn[:, t, :], T, V_FOXK
            if t < 8:
                return qn[:, t - 4, :], NX, V_FOXQ
            if t == 8:
                return kn[:, 4, :], T, V_SWAK
            return qn[:, t - 5, :], NX, V_SWAQ

        def unit(u):
            b = HD * (u % 2)
            return (u // 2, u // 2, b, u) if u < 8 else (u // 2, 4, b, (u - 8) // 2 + 4 * (u % 2))

        def pe_mix_chunk(pe, q):
            pe.wait_ge(w_lo, splits(mc + q))
            out = start_group(pe, mg, 1, q, 0)
            wide = q < 5 or q == 9 or V_FIRST <= q < GATES
            hi, lo = x_rhs("all" if wide else "x")
            strip(out[:, 0:T if wide else NX], (mc + q) % RING, KT, hi, lo,
                  before=wait_x(pe, N_MIX) if q == 0 else None).then_inc(pe_done, 1)

        def pe_mix(pe):
            for q in range(STEP0):
                pe_mix_chunk(pe, q)
                pe_mix_extra(pe, q)
            for u in range(UNITS + 2):
                q = STEP0 + u
                if u < UNITS:
                    pe_scores(pe, u)
                if q < counts["mix"]:
                    pe_mix_chunk(pe, q)
                if 1 <= u <= UNITS:
                    pe_turn(pe, u - 1)
                pe_mix_extra(pe, q)
                if u >= 2:
                    pe_values(pe, u - 2)

        def v_bank(t):
            return ps[7] if t else ps[3]

        def pe_mix_extra(pe, q):
            if q == 0:
                pe_stat(pe, N_MIX, True)
            if q == 1:
                pe_norm(pe, N_MIX, True)
            if 4 <= q < 4 + QKT:
                t = q - 4
                pe.wait_ge(qk_r, t + 1)
                if t:
                    pe.wait_ge(qk_n, t)
                for b, tok in enumerate(blocks(qk_tile(t)[1])):
                    mm = nc.tensor.transpose(ps[6][:, tok:tok + P], qk_wide[:, t % 2, b * P:(b + 1) * P], ident[:, :])
                mm.then_inc(qk_bc, 1)
            if 3 <= q < 3 + QKT:
                t = q - 3
                pe.wait_ge(qk_sq, t + 1)
                if t:
                    pe.wait_ge(qk_sd, t)
                token_sums(ps[7], sq[:, t % 2, :], blocks(qk_tile(t)[1]), head_cols, True, True).then_inc(qk_ss, 1)
            if q == 6:
                pe.wait_ge(rel_const, 32)
                pe.wait_ge(table_set, 1)
                pe.wait_ge(norm_r, N_MIX + 1)
                nc.tensor.matmul(ps[4][0:HEADS, 0:REL_X], table[:, :], onehot[:, 0:REL_X], start=True, stop=True)
                nc.tensor.matmul(ps[5][0:HEADS, 0:REL_M], table[:, :], onehot[:, REL_X:], start=True,
                                 stop=True).then_inc(rel_mm, 1)
            if q == 8:
                pe.wait_ge(f_dve, 6)
                pe.wait_ge(rel_row, 2)
                for tt, tok in enumerate((0, SEG)):
                    mm = nc.tensor.matmul(ps[5][:, tt * HEADS:(tt + 1) * HEADS], cum[:, tok:tok + P],
                                          ident[0:HEADS, 0:HEADS], start=True, stop=True)
                mm.then_inc(cq_mm, 1)
            if V_FIRST < q <= GATES:
                t = q - 1 - V_FIRST
                pe.wait_ge(acc_free, mg + q)
                if t:
                    pe.wait_ge(qk_sd, QKT)
                if t >= 2:
                    pe.wait_ge(v_copied, 3 * t)
                for b, tok in enumerate((0, P, SEG)):
                    mm = nc.tensor.transpose(v_bank(t)[:, b * P:(b + 1) * P], vt[:, t % 2, tok:tok + P], ident[:, :])
                mm.then_inc(v_tr, 1)

        def pe_scores(pe, u):
            qt, kt, b, _ = unit(u)
            if u == 0:
                pe.wait_ge(qk_n, QKT)
                pe.wait_ge(cq_copied, 1)
            if u >= 2:
                pe.wait_ge(at_max, 2 * (u - 2) + 2)
            out = ps[4 + u % 2]
            nc.tensor.matmul(out[:, 0:SEG], qn[b:b + HD, qt, 0:P], kn[b:b + HD, kt, 0:SEG], start=True, stop=True)
            nc.tensor.matmul(out[:, SEG:SEG + T], qn[b:b + HD, qt, P:NX], kn[b:b + HD, kt, 0:T],
                             start=True, stop=True).then_inc(at_s, 1)

        def pe_turn(pe, u):
            p = att[:, u % 2, :]
            pe.wait_ge(at_norm, 2 * u + 2)
            if u >= 1:
                pe.wait_ge(at_pt, 2 * u)
            for n, lo in enumerate((0, SEG, 2 * SEG)):
                nc.tensor.transpose(ps[6][:, n * P:(n + 1) * P], p[:, lo:lo + P], ident[:, :])
            for n, lo in enumerate((P, SEG + P)):
                mm = nc.tensor.transpose(ps[3][:, n * P:(n + 1) * P], p[:, lo:lo + P], ident[:, :])
            mm.then_inc(at_tr, 1)

        def pe_values(pe, u):
            b = HD * (u % 2)
            h = unit(u)[3]
            col = h * HD if u < 8 else 512 + (u % 2) * HD
            pe.wait_ge(at_pt, 2 * u + 2)
            if u == 0:
                pe.wait_ge(v_copied, 3 * (GATES - V_FIRST))
            if u >= 2 and u % 2 == 0:
                pe.wait_ge(o_lo, u // 2)
            o = ps[7][b:b + HD, 0:NX]
            keys, meta = pts[:, u % 2, :], ptm[:, u % 2, :]
            nc.tensor.matmul(o, v0[:, col:col + HD], keys[:, 0:NX], start=True, stop=False)
            nc.tensor.matmul(ps[7][b:b + HD, P:NX], v1[:, col:col + HD], keys[:, NX:NX + P], start=False, stop=False)
            nc.tensor.matmul(o, vm[:, col:col + HD], meta, start=False, stop=True).then_inc(at_pv, 1)

        def act_mix(act):
            act.wait_ge(angle_step, ANGLE_STEPS)
            act.wait_ge(vec_in, 16)
            for q in range(STEP0):
                split_hi(act, mc, 1, q, LEAD)
                act_mix_extra(act, q)
            for u in range(UNITS + 2):
                q = STEP0 + u
                if q < counts["mix"]:
                    split_hi(act, mc, 1, q, LEAD)
                if u < UNITS:
                    act_softmax(act, u)
                act_mix_extra(act, q)
                if 1 <= u <= UNITS:
                    v = u - 1
                    act.wait_ge(at_tr, v + 1)
                    if v >= 2:
                        act.wait_ge(at_pv, v - 1)
                    nc.scalar.activation(pts[:, v % 2, :], ps[6][:, 0:384], ACT.Copy).then_inc(at_pt, 1)
                    nc.scalar.activation(ptm[:, v % 2, :], ps[3][0:META, 0:NX], ACT.Copy).then_inc(at_pt, 1)
                if u >= 2 and u % 2 == 1:
                    act_heads_out(act, (u - 2) // 2)

        def act_mix_extra(act, q):
            if q == 0:
                act_norm(act, N_MIX, True)
            if q == 1:
                act.wait_ge(acc_free, mg + 1)
                nc.scalar.activation(fabs[:, :], fa[:, :], ACT.Abs,
                                     bias=vecs[0:HEADS, V_FBIAS:V_FBIAS + 1]).then_inc(f_act, 1)
                act.wait_ge(f_act, 1)
                nc.scalar.activation(fexp[:, :], fabs[:, :], ACT.Exp, scale=-1.0).then_inc(f_act, 1)
                act.wait_ge(f_act, 2)
                nc.scalar.activation(flog[:, :], fexp[:, :], ACT.Ln, bias=ones[0:HEADS, 0:1]).then_inc(f_act, 1)
            if 3 <= q < 3 + QKT:
                t = q - 3
                dst, width, _ = qk_tile(t)
                act.wait_ge(acc_free, mg + t + 2)
                if t >= 2:
                    act.wait_ge(qk_ss, t - 1)
                nc.scalar.activation(sq[:, t % 2, 0:width], dst, ACT.Square).then_inc(qk_sq, 1)
            if 4 <= q < 4 + QKT:
                t = q - 4
                n = 2 * len(blocks(qk_tile(t)[1]))
                is_q = qk_tile(t)[2] in (V_FOXQ, V_SWAQ)
                act.wait_ge(qk_ss, t + 1)
                if t >= 2:
                    act.wait_ge(qk_r, t - 1)
                nc.scalar.activation(qk_root[:, t % 2, 0:n], ps[7][:, 0:n], ACT.Sqrt,
                                     bias=epsc[:, 1:2] if is_q else epsc[:, 0:1],
                                     scale=1.0 if is_q else 1.0 / HD).then_inc(qk_sd, 1)
            if q == 7:
                act.wait_ge(rel_mm, 1)
                nc.scalar.activation(relrow[:, 0:REL_X], ps[4][0:HEADS, 0:REL_X], ACT.Copy).then_inc(rel_row, 1)
                nc.scalar.activation(relrow[:, REL_X:], ps[5][0:HEADS, 0:REL_M], ACT.Copy).then_inc(rel_row, 1)
            if V_FIRST + 2 <= q <= GATES + 1:
                t = q - 2 - V_FIRST
                col = slice(t * P, (t + 1) * P)
                act.wait_ge(v_tr, t + 1)
                nc.scalar.activation(v0[:, col], v_bank(t)[:, 0:P], ACT.Copy).then_inc(v_copied, 1)
                nc.scalar.activation(vm[:, col], v_bank(t)[0:META, P:2 * P], ACT.Copy).then_inc(v_copied, 1)
                nc.scalar.activation(v1[:, col], v_bank(t)[:, 2 * P:3 * P], ACT.Copy).then_inc(v_copied, 1)

        def act_softmax(act, u):
            s = small[:, u % 2, :]
            a = att[:, u % 2, :]
            act.wait_ge(at_neg, u + 1)
            if u >= 2:
                act.wait_ge(at_inv, u - 1)
            nc.scalar.activation(a[:, 0:SEG], a[:, 0:SEG], ACT.Exp, bias=s[:, 2:3], accum_out=s[:, 4:5]).then_inc(at_exp, 1)
            if u >= 8:
                h = unit(u)[3]
                nc.scalar.activation(s[:, 8:10], s[:, 2:4], ACT.Exp,
                                     bias=vecs[:, V_SINK + h:V_SINK + h + 1]).then_inc(at_exp, 1)
            nc.scalar.activation(a[:, SEG:], a[:, SEG:], ACT.Exp, bias=s[:, 3:4], accum_out=s[:, 5:6]).then_inc(at_exp, 1)

        def exps(u):
            return 2 * (u + 1) + max(u - 7, 0)

        def act_heads_out(act, t):
            act.wait_ge(at_pv, 2 * t + 2)
            nc.scalar.activation(oy_hi[:, t, :], ps[7][:, 0:NX], ACT.Copy).then_inc(o_hi, 1)

        def dve_mix(dve):
            dve.wait_ge(angle_step, ANGLE_STEPS)
            dve.wait_ge(vec_in, 16)
            for q in range(STEP0):
                if q == 0:
                    split_lo(dve, mc, 1, q, LEAD)
                    dve_norm(dve, N_MIX, True)
                if 4 <= q < 4 + QKT:
                    t = q - 4
                    n = 2 * len(blocks(qk_tile(t)[1]))
                    dve.wait_ge(qk_sd, t + 1)
                    if t >= 2:
                        dve.wait_ge(qk_bc, t - 1)
                    nc.vector.reciprocal(qk_inv[:, t % 2, 0:n], qk_root[:, t % 2, 0:n]).then_inc(qk_inv_set, 1)
                    dve.wait_ge(qk_inv_set, t + 1)
                    nc.vector.tensor_copy(qk_wide[:, t % 2, 0:n * HD].rearrange("p (n d) -> p n d", d=HD),
                                          qk_inv[:, t % 2, 0:n].unsqueeze(2).to_broadcast([P, n, HD])).then_inc(qk_r, 1)
                if 5 <= q < 5 + QKT:
                    t = q - 5
                    dst, width, col = qk_tile(t)
                    dve.wait_ge(qk_bc, t + 1)
                    nc.vector.scalar_tensor_tensor(dst, dst, vecs[:, col:col + 1], ps[6][:, 0:width], ALU.mult,
                                                   ALU.mult).then_inc(qk_n, 1)
                dve_mix_read(dve, q)
                if q == 0:
                    dve_forget_min(dve)
                if q == 2:
                    dve_forget_scan(dve)
                if q == 9:
                    dve.wait_ge(cq_mm, 1)
                    nc.vector.tensor_scalar(cq[:, :], ps[5][:, 0:16], -1.0, None, ALU.mult).then_inc(cq_copied, 1)
                if q:
                    split_lo(dve, mc, 1, q, LEAD)
            for u in range(UNITS + 2):
                q = STEP0 + u
                if u < UNITS:
                    dve_scores(dve, u)
                if q < counts["mix"]:
                    split_lo(dve, mc, 1, q, LEAD)
                if u < UNITS:
                    dve_probs(dve, u)
                if q < counts["mix"]:
                    dve_mix_read(dve, q)
                if u >= 2 and u % 2 == 1:
                    t = (u - 2) // 2
                    dve.wait_ge(o_hi, t + 1)
                    nc.vector.tensor_tensor(oy_lo[:, t, :], ps[7][:, 0:NX], oy_hi[:, t, :],
                                            ALU.subtract).then_inc(o_lo, 1)

        def dve_mix_read(dve, q):
            out = ps[banks[mg + q]]
            dve.wait_ge(pe_done, mc + q + 1)
            if q == 0:
                nc.vector.tensor_tensor(fa[:, :], out[0:HEADS, 0:T], rstd[0:HEADS, 0:T], ALU.mult).then_inc(acc_free, 1)
            elif q <= QKT:
                dst, width, _ = qk_tile(q - 1)
                if width == T:
                    nc.vector.tensor_tensor(dst, out[:, 0:T], rstd[:, 0:T], ALU.mult).then_inc(acc_free, 1)
                else:
                    nc.vector.tensor_tensor(two(dst), two(out[:, 0:NX]), seg(rstd[:, :]), ALU.mult).then_inc(acc_free, 1)
            elif q < GATES:
                t = q - V_FIRST
                if t >= 2:
                    dve.wait_ge(v_tr, t - 1)
                nc.vector.tensor_tensor(vt[:, t % 2, :], out[:, 0:T], rstd[:, 0:T], ALU.mult).then_inc(acc_free, 1)
            else:
                if q == GATES:
                    dve.wait_ge(rel_out, 16)
                    dve.wait_ge(ck_out, 16)
                nc.vector.tensor_tensor(two(gate[:, q - GATES, :]), two(out[:, 0:NX]), seg(rstd[:, :]),
                                        ALU.mult).then_inc(acc_free, 1)

        def dve_forget_min(dve):
            dve.wait_ge(acc_free, mg + 1)
            nc.vector.tensor_scalar(fmin[:, :], fa[:, :], vecs[0:HEADS, V_FBIAS:V_FBIAS + 1], 0.0, ALU.add,
                                    ALU.min).then_inc(f_dve, 1)
            nc.vector.memset(fones[:, :], 1.0).then_inc(f_dve, 1)

        def dve_forget_scan(dve):
            dve.wait_ge(f_act, 3)
            dve.wait_ge(f_dve, 2)
            nc.vector.tensor_tensor(fa[:, :], flog[:, :], fmin[:, :], ALU.subtract).then_inc(f_dve, 1)
            dve.wait_ge(f_dve, 3)
            nc.vector.tensor_tensor_scan(cum[:, P:SEG], fones[:, P:SEG], fa[:, P:SEG], 0.0, ALU.mult,
                                         ALU.add).then_inc(f_dve, 1)
            dve.wait_ge(f_dve, 4)
            nc.vector.tensor_tensor_scan(cum[:, 0:P], fones[:, 0:P], fa[:, 0:P], cum[:, SEG - 1:SEG], ALU.mult,
                                         ALU.add).then_inc(f_dve, 1)
            dve.wait_ge(f_dve, 5)
            nc.vector.tensor_tensor_scan(cum[:, SEG:T], fones[:, SEG:T], fa[:, SEG:T], cum[:, P - 1:P], ALU.mult,
                                         ALU.add).then_inc(f_dve, 1)

        def dve_scores(dve, u):
            h = unit(u)[3]
            s, a, out = small[:, u % 2, :], att[:, u % 2, :], ps[4 + u % 2]
            if u < 8:
                if u == 0:
                    dve.wait_ge(cq_copied, 1)
                    dve.wait_ge(ck_in, 16)
                    dve.wait_ge(mask_set, 4)
                    dve.wait_ge(qk_n, QKT)
                nc.vector.scalar_tensor_tensor(bm[:, 0:SEG], ckb[:, h, 0:SEG], cq[:, h:h + 1], mask[:, 0:SEG],
                                               ALU.add, ALU.add).then_inc(at_bias, 1)
                nc.vector.scalar_tensor_tensor(bm[:, SEG:], ckb[:, h, :], cq[:, HEADS + h:HEADS + h + 1],
                                               mask[:, SEG:], ALU.add, ALU.add).then_inc(at_bias, 1)
                dve.wait_ge(at_bias, 2 * u + 2)
                bias, least = bm[:, :], (-3.0e38, -3.0e38)
            else:
                if u == 8:
                    dve.wait_ge(rel_in, 80)
                bias, least = rel[:, h, :], (vecs[:, V_SINK + h:V_SINK + h + 1],) * 2
            dve.wait_ge(at_s, u + 1)
            if u >= 2:
                dve.wait_ge(at_tr, u - 1)
            nc.vector.tensor_tensor_reduce(a[:, 0:SEG], out[:, 0:SEG], bias[:, 0:SEG], 1.0, least[0], ALU.add,
                                           ALU.max, s[:, 0:1]).then_inc(at_max, 1)
            nc.vector.tensor_tensor_reduce(a[:, SEG:], out[:, SEG:SEG + T], bias[:, SEG:], 1.0, least[1], ALU.add,
                                           ALU.max, s[:, 1:2]).then_inc(at_max, 1)
            dve.wait_ge(at_max, 2 * u + 2)
            nc.vector.tensor_scalar(s[:, 2:4], s[:, 0:2], -1.0, None, ALU.mult).then_inc(at_neg, 1)

        def dve_probs(dve, u):
            s, a = small[:, u % 2, :], att[:, u % 2, :]
            dve.wait_ge(at_exp, exps(u))
            if u >= 8:
                nc.vector.tensor_tensor(s[:, 4:6], s[:, 4:6], s[:, 8:10], ALU.add).then_inc(at_sum, 1)
                dve.wait_ge(at_sum, u - 7)
            nc.vector.reciprocal(s[:, 6:8], s[:, 4:6]).then_inc(at_inv, 1)
            dve.wait_ge(at_inv, u + 1)
            nc.vector.tensor_scalar(a[:, 0:SEG], a[:, 0:SEG], s[:, 6:7], None, ALU.mult).then_inc(at_norm, 1)
            nc.vector.tensor_scalar(a[:, SEG:], a[:, SEG:], s[:, 7:8], None, ALU.mult).then_inc(at_norm, 1)

        bc, bg = first["branch"]

        def pe_branch(pe):
            for m in range(KT):
                pe.wait_ge(w_lo, splits(bc + m))
                for br in range(2):
                    out = start_group(pe, bg, 2, m, br)
                    if m == 0:
                        pe.wait_ge(o_lo, 4 * br + 4)
                    mm = strip(out[:, 0:NX], (bc + m) % RING, 4, lambda t: oy_hi[:, 4 * br + t, :],
                               lambda t: oy_lo[:, 4 * br + t, :], at=4 * br)
                mm.then_inc(pe_done, 1)

        def act_branch(act):
            for m in range(KT):
                split_hi(act, bc, 1, m, LEAD)
                if m == 0:
                    act.wait_ge(acc_free, mg + counts["mix"])
                for br in range(2):
                    nc.scalar.activation(gate[:, 2 * m + br, :], gate[:, 2 * m + br, :], ACT.Sigmoid).then_inc(sig_done, 1)
                act.wait_ge(y_step, m + 1)
                nc.scalar.activation(oy_hi[:, 8 + m, :], hd[:, 0:NX], ACT.Copy).then_inc(y_hi, 1)

        def dve_branch(dve):
            def low(m):
                dve.wait_ge(y_hi, m + 1)
                nc.vector.tensor_tensor(oy_lo[:, 8 + m, :], hd[:, 0:NX], oy_hi[:, 8 + m, :], ALU.subtract).then_inc(y_lo, 1)

            for m in range(KT):
                dve.wait_ge(pe_done, bc + m + 1)
                dve.wait_ge(sig_done, 2 * m + 2)
                if m:
                    dve.wait_ge(y_step, m)
                for br, dst in enumerate((tg, tu)):
                    nc.vector.tensor_tensor(dst[:, 0:NX], ps[banks[bg + 2 * m + br]][:, 0:NX], gate[:, 2 * m + br, :],
                                            ALU.mult).then_inc(acc_free, 1)
                dve.wait_ge(acc_free, bg + 2 * m + 2)
                if m:
                    dve.wait_ge(y_lo, m)
                nc.vector.tensor_tensor(hd[:, 0:NX], tg[:, 0:NX], tu[:, 0:NX], ALU.add).then_inc(y_step, 1)
                if m == KT - 1:
                    low(m)
                split_lo(dve, bc, 1, m, LEAD)
                if m < KT - 1:
                    low(m)

        sc, sgrp = first["mixb"]
        STEPS = counts["mixb"] + counts["memk"]
        TAP0 = 4
        TAPS_EARLY, TAPS_LATE = 5, 11
        RET0 = 13
        MEM0 = 4
        LN0 = 24

        def taps_before(q):
            n = (min(q, 20) - TAP0) * TAPS_EARLY + max(q - 20, 0) * TAPS_LATE
            return min(n, 4 * TAPS)

        assert taps_before(LN0) == 4 * TAPS
        RV = 12

        def pe_mixb(pe):
            for q in range(STEPS):
                s = (sc + q) % RING
                if q < 20:
                    pe.wait_ge(w_lo, splits(sc + q))
                else:
                    pe.wait_ge(w_in[s], ((sc + q) // RING + 1) * 16)
                out = start_group(pe, sgrp, 1, q, 0)
                if q < 20:
                    hi, lo = x_rhs("packed")
                    mm = strip(out[:, 0:NX], s, KT, hi, lo, before=wait_x(pe, N_MIXB) if q == 0 else None)
                else:
                    if q == 20:
                        pe.wait_ge(m_scaled, KT)
                    for t in range(KT):
                        mm = nc.tensor.matmul(out[:, 0:NX], raw[:, s, t * P:(t + 1) * P], mem[:, t, :], start=t == 0,
                                              stop=t == KT - 1)
                mm.then_inc(pe_done, 1)
                if q == 0:
                    pe_stat(pe, N_MIXB, False)
                if q == 1:
                    pe_norm(pe, N_MIXB, False)
                if MEM0 < q <= MEM0 + KT:
                    e = q - MEM0 - 1
                    pe.wait_ge(m_sq, e + 1)
                    token_sums(ps[5], msq[:, e % 2, :], blocks(NX), one_col, e == 0, e == KT - 1).then_inc(m_stat, 1)
                if q == 15:
                    pe.wait_ge(m_inv, 1)
                    pe.wait_ge(rot_step, 12)
                    spread(ps[7], col_inv[:, 0, :], blocks(NX)).then_inc(m_bc, 1)
                if 9 <= q < 13:
                    e = q - 9
                    pe.wait_ge(acc_free, sgrp + 8 + e + 1)
                    if e >= 2:
                        pe.wait_ge(rot_step, 3 * (e - 2) + 2)
                    nc.tensor.matmul(ps[6 + e % 2][:, 0:NX], swap[:, :], qr[:, e, :], start=True, stop=True).then_inc(rot_mm, 1)
                if RV < q <= RV + 4:
                    t = q - 1 - RV
                    pe.wait_ge(acc_free, sgrp + q)
                    if t:
                        pe.wait_ge(rv_copied, t)
                    src = tu if t % 2 else tg
                    for tt in range(2):
                        mm = nc.tensor.transpose(ps[3][:, NX + tt * P:NX + (tt + 1) * P], src[:, tt * P:(tt + 1) * P],
                                                 ident[:, :])
                    mm.then_inc(rv_tr, 1)
                if q >= RET0:
                    pe_retention(pe, q - RET0)
                if q == LN0 + 1:
                    pe.wait_ge(conv_step, 4 * TAPS)
                    pe.wait_ge(ra_dec, HEADS)
                    for t in range(4):
                        mm = nc.tensor.matmul(ps[4][:, 0:NX], ones[:, :], cy[:, t, :], start=t == 0, stop=t == 3)
                    mm.then_inc(ln_mu, 1)
                if q == LN0 + 2:
                    for t in range(4):
                        pe.wait_ge(ln_sq, t + 1)
                        mm = token_sums(ps[5], csq[:, t, :], blocks(NX), one_col, t == 0, t == 3)
                    mm.then_inc(ln_var, 1)
                if q == LN0 + 3:
                    pe.wait_ge(ln_r, 1)
                    spread(ps[5][:, P:], col_inv[:, 2, :], blocks(NX)).then_inc(ln_bc, 1)

        def pe_retention(pe, r):
            if r < HEADS:
                b = RDK * (r % 4)
                pe.wait_ge(rot_step, 9 if r < 4 else 12)
                if r == 0:
                    pe.wait_ge(norm_r, N_MIXB + 1)
                if r == 1:
                    pe.wait_ge(m_sd, 1)
                if r >= 2:
                    pe.wait_ge(ra_dec, r - 1)
                out = ps[4 + r % 2]
                qh, kh = qr[b:b + RDK, r // 4, :], qr[b:b + RDK, 2 + r // 4, :]
                nc.tensor.matmul(out[:, 0:NX], kh[:, 0:P], qh[:, :], start=True, stop=True)
                nc.tensor.matmul(out[:, NX:NX + P], kh[:, P:NX], qh[:, P:NX], start=True, stop=True).then_inc(ra_mm, 1)
            if 1 <= r <= HEADS:
                h = r - 1
                b = HD * (h % 2)
                pe.wait_ge(ra_dec, h + 1)
                pe.wait_ge(rv_copied, h // 2 + 1)
                if h == 0:
                    pe.wait_ge(rot_step, 8)
                if h >= 2 and h % 2 == 0:
                    pe.wait_ge(ry_copied, h // 2)
                a = amat[:, h % 2, :]
                nc.tensor.matmul(ps[6][b:b + HD, 0:NX], v2[:, 0, h * HD:(h + 1) * HD], a[:, 0:NX], start=True, stop=False)
                nc.tensor.matmul(ps[6][b:b + HD, P:NX], v2[:, 1, h * HD:(h + 1) * HD], a[:, NX:NX + P], start=False,
                                 stop=True).then_inc(ry_mm, 1)
            if r >= 6 and r % 2 == 0 and (r - 6) // 2 < 4:
                t = (r - 6) // 2
                pe.wait_ge(gn_r, t + 1)
                pe.wait_ge(gn_cen, min(t + 2, 4))
                for b, tok in enumerate(blocks(NX)):
                    for h in range(2):
                        v = col_inv[:, 1, 2 * b + h:2 * b + h + 1].to_broadcast([P, HD])
                        mm = nc.tensor.matmul(ps[7][h * HD:(h + 1) * HD, NX + tok:NX + tok + P], v, ident[:, :],
                                              start=True, stop=True)
                mm.then_inc(gn_bc, 1)
            if r >= 3 and r % 2 == 1 and (r - 3) // 2 < 4:
                t = (r - 3) // 2
                pe.wait_ge(ry_copied, t + 1)
                if t == 0:
                    pe.wait_ge(m_r, 1)
                if t >= 2:
                    pe.wait_ge(gn_n, t - 1)
                nc.tensor.matmul(ps[7][:, 0:NX], same[:, :], yr[:, t % 2, :], start=True, stop=True).then_inc(gn_mu, 1)
            if r >= 4 and r % 2 == 0 and (r - 4) // 2 < 4:
                t = (r - 4) // 2
                pe.wait_ge(gn_sq, t + 1)
                if t == 0:
                    pe.wait_ge(rv_copied, 4)
                if t:
                    pe.wait_ge(gn_sd, t)
                token_sums(ps[3], msq[:, t % 2, :], blocks(NX), head_cols, True, True).then_inc(gn_var, 1)

        def act_mixb(act):
            for q in range(STEPS):
                split_hi(act, sc, 1, q, LEAD)
                if q == 0:
                    act_norm(act, N_MIXB, False)
                if q == 1:
                    act.wait_ge(angle_step, ANGLE_STEPS)
                    nc.scalar.activation(sinv[:, :], angle[:, :], ACT.Sin).then_inc(cs_act, 1)
                    nc.scalar.activation(cosv[:, :], angle[:, :], ACT.Sin, scale=0.5).then_inc(cs_act, 1)
                if MEM0 <= q < MEM0 + KT:
                    e = q - MEM0
                    if e == 0:
                        act.wait_ge(mem_in, 16)
                    if e >= 2:
                        act.wait_ge(m_stat, e - 1)
                    nc.scalar.activation(msq[:, e % 2, :], mem[:, e, :], ACT.Square).then_inc(m_sq, 1)
                    act.wait_ge(m_sq, e + 1)
                    nc.scalar.activation(mem[:, e, :], mem[:, e, :], ACT.Copy, scale=gain(N_MEM, e)).then_inc(m_scaled, 1)
                if q < 8 and q % 2 == 0:
                    act.wait_ge(acc_free, sgrp + q + 1)
                    nc.scalar.activation(sg[:, 0:NX], tg[:, 0:NX], ACT.Sigmoid).then_inc(cb_sig, 1)
                if q == MEM0 + KT + 1:
                    act.wait_ge(m_stat, KT)
                    nc.scalar.activation(col_root[:, 0, 0:2], ps[5][:, 0:2], ACT.Sqrt, bias=epsc[:, 0:1],
                                         scale=1.0 / D).then_inc(m_sd, 1)
                if q == 15:
                    act.wait_ge(m_bc, 1)
                    nc.scalar.activation(memr[:, :], ps[7][:, 0:NX], ACT.Copy).then_inc(m_r, 1)
                if RV + 2 <= q < RV + 6:
                    t = q - 2 - RV
                    act.wait_ge(rv_tr, t + 1)
                    nc.scalar.activation(v2[:, :, t * P:(t + 1) * P], two(ps[3][:, NX:512]), ACT.Copy).then_inc(rv_copied, 1)
                if 17 <= q < 21:
                    act.wait_ge(acc_free, sgrp + q)
                    src = tg if q % 2 else tu
                    nc.scalar.activation(rg[:, q - 17, :], src[:, 0:NX], ACT.Silu).then_inc(rg_done, 1)
                if q >= RET0:
                    act_retention(act, q - RET0)
                if q == LN0 + 2:
                    for t in range(4):
                        act.wait_ge(ln_cen, t + 1)
                        nc.scalar.activation(csq[:, t, :], cy[:, t, :], ACT.Square).then_inc(ln_sq, 1)
                if q == LN0 + 3:
                    act.wait_ge(ln_var, 1)
                    nc.scalar.activation(col_root[:, 2, 0:2], ps[5][:, 0:2], ACT.Sqrt, bias=epsc[:, 0:1],
                                         scale=1.0 / CONV).then_inc(ln_sd, 1)
            act_conv_out(act)

        def act_conv_out(act):
            for t in range(4):
                act.wait_ge(ln_n, t + 1)
                nc.scalar.activation(cy[:, t, :], cy[:, t, :], ACT.Silu,
                                     bias=vecs[:, V_LNB + t:V_LNB + t + 1]).then_inc(ln_z, 1)
            for t in range(4):
                act.wait_ge(ln_z, t + 1)
                nc.scalar.activation(oz_hi[:, 4 + t, :], cy[:, t, :], ACT.Copy).then_inc(c_hi, 1)

        def act_retention(act, r):
            if r >= 2 and r % 2 == 0 and (r - 2) // 2 < 4:
                t = (r - 2) // 2
                act.wait_ge(ry_mm, 2 * t + 2)
                if t >= 2:
                    act.wait_ge(gn_z, t - 1)
                nc.scalar.activation(yr[:, t % 2, :], ps[6][:, 0:NX], ACT.Copy).then_inc(ry_copied, 1)
            if r >= 5 and r % 2 == 1 and (r - 5) // 2 < 4:
                t = (r - 5) // 2
                act.wait_ge(gn_var, t + 1)
                if t:
                    act.wait_ge(gn_r, t)
                nc.scalar.activation(col_root[:, 1, :], ps[3][:, 0:4], ACT.Sqrt, bias=epsc[:, 0:1],
                                     scale=1.0 / HD).then_inc(gn_sd, 1)
            if r >= 7 and r % 2 == 1 and (r - 7) // 2 < 4:
                t = (r - 7) // 2
                act.wait_ge(gn_z, t + 1)
                nc.scalar.activation(oz_hi[:, t, :], zt[:, t % 2, :], ACT.Copy).then_inc(z_hi, 1)
            if r >= 3 and r % 2 == 1 and (r - 3) // 2 < 4:
                t = (r - 3) // 2
                act.wait_ge(gn_cen, t + 1)
                if t >= 2:
                    act.wait_ge(gn_var, t - 1)
                nc.scalar.activation(msq[:, t % 2, :], yr[:, t % 2, :], ACT.Square).then_inc(gn_sq, 1)

        def conv_taps(dve, a, b):
            for n in range(a, min(b, 4 * TAPS)):
                t, j = n // (2 * TAPS) * 2 + n % 2, n % (2 * TAPS) // 2
                src = glu[:, t, j:j + NX]
                w = convw[:, t * TAPS + j:t * TAPS + j + 1]
                if j == 0:
                    dve.wait_ge(glu_done, t + 1)
                    nc.vector.tensor_scalar(cy[:, t, :], src, w, vecs[:, V_CONVB + t:V_CONVB + t + 1], ALU.mult,
                                            ALU.add).then_inc(conv_step, 1)
                else:
                    dve.wait_ge(conv_step, n - 1)
                    nc.vector.scalar_tensor_tensor(cy[:, t, :], src, w, cy[:, t, :], ALU.mult, ALU.add).then_inc(conv_step, 1)

        def dve_mixb(dve):
            for q in range(STEPS):
                if q == 0:
                    split_lo(dve, sc, 1, q, LEAD)
                    dve_norm(dve, N_MIXB, False)
                if q == 3:
                    dve.wait_ge(cs_act, 2)
                    nc.vector.tensor_tensor(cosv[:, :], cosv[:, :], cosv[:, :], ALU.mult).then_inc(cs_dve, 1)
                    dve.wait_ge(cs_dve, 1)
                    nc.vector.tensor_scalar(cosv[:, :], cosv[:, :], -2.0, 1.0, ALU.mult, ALU.add).then_inc(cs_dve, 1)
                dve_mixb_read(dve, q)
                if 10 <= q < 14:
                    e = q - 10
                    dve.wait_ge(rot_mm, e + 1)
                    dve.wait_ge(cs_dve, 2)
                    if e:
                        dve.wait_ge(rot_step, 3 * e)
                    nc.vector.tensor_tensor(qr[:, e, :], qr[:, e, :], cosv[:, :], ALU.mult).then_inc(rot_step, 1)
                    nc.vector.tensor_tensor(hd[:, 0:NX], ps[6 + e % 2][:, 0:NX], sinv[:, :], ALU.mult).then_inc(rot_step, 1)
                    dve.wait_ge(rot_step, 3 * e + 2)
                    nc.vector.tensor_tensor(qr[:, e, :], qr[:, e, :], hd[:, 0:NX], ALU.add).then_inc(rot_step, 1)
                if q == 14:
                    dve.wait_ge(m_sd, 1)
                    nc.vector.reciprocal(col_inv[:, 0, 0:2], col_root[:, 0, 0:2]).then_inc(m_inv, 1)
                if q == LN0 + 3:
                    dve.wait_ge(ln_sd, 1)
                    nc.vector.reciprocal(col_inv[:, 2, 0:2], col_root[:, 2, 0:2]).then_inc(ln_r, 1)
                if q >= RET0:
                    dve_retention(dve, q - RET0)
                if q:
                    split_lo(dve, sc, 1, q, LEAD)
                if q >= TAP0:
                    conv_taps(dve, taps_before(q), taps_before(q + 1))
                if q == LN0 + 1:
                    dve.wait_ge(ln_mu, 1)
                    for t in range(4):
                        nc.vector.scalar_tensor_tensor(cy[:, t, :], ps[4][:, 0:NX], -1.0 / CONV, cy[:, t, :], ALU.mult,
                                                       ALU.add).then_inc(ln_cen, 1)
            dve.wait_ge(ln_bc, 1)
            for t in range(4):
                nc.vector.scalar_tensor_tensor(cy[:, t, :], cy[:, t, :], vecs[:, V_LNW + t:V_LNW + t + 1],
                                               ps[5][:, P:P + NX], ALU.mult, ALU.mult).then_inc(ln_n, 1)
            for t in range(4):
                dve.wait_ge(c_hi, t + 1)
                nc.vector.tensor_tensor(oz_lo[:, 4 + t, :], cy[:, t, :], oz_hi[:, 4 + t, :], ALU.subtract).then_inc(c_lo, 1)

        def dve_mixb_read(dve, q):
            out = ps[banks[sgrp + q]][:, 0:NX]
            dve.wait_ge(pe_done, sc + q + 1)
            if 8 <= q < RV:
                nc.vector.tensor_tensor(qr[:, q - 8, :], out, rstd[:, 0:NX], ALU.mult).then_inc(acc_free, 1)
            elif q < 20:
                dst = tu if q % 2 else tg
                if q < 8 and q % 2 and q > 1:
                    dve.wait_ge(glu_done, q // 2)
                if q == RV + 1:
                    dve.wait_ge(glu_done, 4)
                if RV + 2 <= q < RV + 6:
                    dve.wait_ge(rv_tr, q - RV - 1)
                if q >= RV + 6:
                    dve.wait_ge(rg_done, q - RV - 5)
                nc.vector.tensor_tensor(dst[:, 0:NX], out, rstd[:, 0:NX], ALU.mult).then_inc(acc_free, 1)
                if q < 8 and q % 2:
                    dve.wait_ge(cb_sig, q // 2 + 1)
                    dve.wait_ge(acc_free, sgrp + q + 1)
                    nc.vector.tensor_tensor(glu[:, q // 2, TAPS - 1:], tu[:, 0:NX], sg[:, 0:NX],
                                            ALU.mult).then_inc(glu_done, 1)
            else:
                if q == 20:
                    dve.wait_ge(m_r, 1)
                nc.vector.tensor_tensor(km[:, q - 20, :], out, memr[:, :], ALU.mult).then_inc(acc_free, 1)

        def dve_retention(dve, r):
            if r < HEADS:
                if r == 0:
                    dve.wait_ge(decay_in, 16)
                dve.wait_ge(ra_mm, r + 1)
                if r >= 2:
                    dve.wait_ge(ry_mm, r - 1)
                nc.vector.tensor_tensor(amat[:, r % 2, :], ps[4 + r % 2][:, 0:384], decay[:, r, :], ALU.mult).then_inc(ra_dec, 1)
            if r >= 3 and r % 2 == 1 and (r - 3) // 2 < 4:
                t = (r - 3) // 2
                dve.wait_ge(gn_mu, t + 1)
                nc.vector.scalar_tensor_tensor(yr[:, t % 2, :], ps[7][:, 0:NX], -1.0 / HD, yr[:, t % 2, :], ALU.mult,
                                               ALU.add).then_inc(gn_cen, 1)
            if r >= 5 and r % 2 == 1 and (r - 5) // 2 < 4:
                t = (r - 5) // 2
                dve.wait_ge(gn_sd, t + 1)
                if t:
                    dve.wait_ge(gn_bc, t)
                nc.vector.reciprocal(col_inv[:, 1, :], col_root[:, 1, :]).then_inc(gn_r, 1)
            if r >= 6 and r % 2 == 0 and (r - 6) // 2 < 4:
                t = (r - 6) // 2
                dve.wait_ge(gn_bc, t + 1)
                nc.vector.scalar_tensor_tensor(yr[:, t % 2, :], yr[:, t % 2, :], vecs[:, V_GNW + t:V_GNW + t + 1],
                                               ps[7][:, NX:512], ALU.mult, ALU.mult).then_inc(gn_n, 1)
                dve.wait_ge(gn_n, t + 1)
                dve.wait_ge(rg_done, t + 1)
                if t >= 2:
                    dve.wait_ge(z_lo, t - 1)
                nc.vector.tensor_tensor(zt[:, t % 2, :], yr[:, t % 2, :], rg[:, t, :], ALU.mult).then_inc(gn_z, 1)
            if r >= 7 and r % 2 == 1 and (r - 7) // 2 < 4:
                t = (r - 7) // 2
                dve.wait_ge(z_hi, t + 1)
                nc.vector.tensor_tensor(oz_lo[:, t, :], zt[:, t % 2, :], oz_hi[:, t, :], ALU.subtract).then_inc(z_lo, 1)

        qc, qg = first["xq"]
        XSTEPS = counts["xq"] + counts["memv"]

        def pe_xattn(pe):
            hi, lo = x_rhs("packed")
            for m in range(XSTEPS + 2):
                if m < XSTEPS:
                    pe.wait_ge(w_lo, splits(qc + m))
                    out = start_group(pe, qg, 1, m, 0)[:, 0:NX]
                    s = (qc + m) % RING
                    if m < KT:
                        mm = strip(out, s, KT, hi, lo, before=wait_x(pe, N_XATT) if m == 0 else None)
                    else:
                        mm = strip(out, s, KT, lambda t: mem_hi[:, t, :], lambda t: mem_lo[:, t, :],
                                   before=(lambda t: pe.wait_ge(m_lo, t + 1)) if m == KT else None)
                    mm.then_inc(pe_done, 1)
                if m == 0:
                    pe_stat(pe, N_XATT, False)
                if m == 1:
                    pe_norm(pe, N_XATT, False)
                if KT < m <= XSTEPS:
                    e = m - 1 - KT
                    pe.wait_ge(acc_free, qg + m)
                    if e:
                        pe.wait_ge(xv_copied, e)
                    src = tu if e % 2 else tg
                    for tt in range(2):
                        mm = nc.tensor.transpose(ps[3][:, tt * P:(tt + 1) * P], src[:, tt * P:(tt + 1) * P], ident[:, :])
                    mm.then_inc(xv_tr, 1)
                if m % 2 == 0 and 0 <= (m - 2) // 2 < XHEADS:
                    pe_xscores(pe, (m - 2) // 2)
                if m % 2 == 0 and 0 <= (m - 8) // 2 < XHEADS:
                    pe_xturn(pe, (m - 8) // 2)
                if m % 2 == 1 and 0 <= (m - 11) // 2 < XHEADS:
                    pe_xvalues(pe, (m - 11) // 2)

        def pe_xscores(pe, h):
            pe.wait_ge(acc_free, qg + 2 * h + 2)
            if h == 0:
                pe.wait_ge(norm_r, N_XATT + 1)
            if h >= 2:
                pe.wait_ge(xs_exp, 2 * (h - 2) + 2)
            out = ps[4 + h % 2]
            for qt in range(2):
                for t in range(2):
                    mm = nc.tensor.matmul(out[:, qt * NX:(qt + 1) * NX], qx[:, 2 * h + t, qt * P:(qt + 1) * P],
                                          km[:, 2 * h + t, :], start=t == 0, stop=t == 1)
            mm.then_inc(xs_s, 1)

        def pe_xturn(pe, h):
            pe.wait_ge(xs_norm, 2 * h + 2)
            if h:
                pe.wait_ge(xs_pt, h)
            p = xatt[:, h, :]
            for t in range(2):
                for qt in range(2):
                    mm = nc.tensor.transpose(ps[6][:, t * NX + qt * P:t * NX + (qt + 1) * P],
                                             p[:, qt * NX + t * P:qt * NX + (t + 1) * P], ident[:, :])
            mm.then_inc(xs_tr, 1)

        def pe_xvalues(pe, h):
            pe.wait_ge(xs_pt, h + 1)
            pe.wait_ge(xv_copied, 2 * h + 2)
            if h:
                pe.wait_ge(xo_lo, h)
            for dt in range(2):
                col = h * XH_DIM + dt * P
                for t in range(2):
                    mm = nc.tensor.matmul(ps[7][:, dt * NX:(dt + 1) * NX], vmem[:, t, col:col + P],
                                          xpt[:, h % 2, t * NX:(t + 1) * NX], start=t == 0, stop=t == 1)
            mm.then_inc(xs_pv, 1)

        def act_xattn(act):
            for m in range(XSTEPS + 3):
                if m < XSTEPS:
                    split_hi(act, qc, 1, m, LEAD)
                if m == 0:
                    act_norm(act, N_XATT, False)
                if m < KT:
                    nc.scalar.activation(mem_hi[:, m, :], mem[:, m, :], ACT.Copy).then_inc(m_hi, 1)
                if m % 2 == 1 and 0 <= (m - 3) // 2 < XHEADS:
                    act_xexp(act, (m - 3) // 2)
                if KT + 2 <= m < XSTEPS + 2:
                    e = m - 2 - KT
                    act.wait_ge(xv_tr, e + 1)
                    nc.scalar.activation(vmem[:, :, e * P:(e + 1) * P], two(ps[3][:, 0:NX]), ACT.Copy).then_inc(xv_copied, 1)
                if m % 2 == 1 and 0 <= (m - 9) // 2 < XHEADS:
                    act_xcopy(act, (m - 9) // 2)
                if m % 2 == 0 and 0 <= (m - 12) // 2 < XHEADS:
                    act_xout(act, (m - 12) // 2)

        def act_xexp(act, h):
            s = xsmall[:, h, :]
            act.wait_ge(xs_neg, h + 1)
            for qt in range(2):
                nc.scalar.activation(xatt[:, h, qt * NX:(qt + 1) * NX], ps[4 + h % 2][:, qt * NX:(qt + 1) * NX],
                                     ACT.Exp, bias=s[:, 2 + qt:3 + qt], scale=XH_DIM ** -0.5,
                                     accum_out=s[:, 4 + qt:5 + qt]).then_inc(xs_exp, 1)

        def act_xcopy(act, h):
            act.wait_ge(xs_tr, h + 1)
            if h >= 2:
                act.wait_ge(xs_pv, h - 1)
            nc.scalar.activation(xpt[:, h % 2, :], ps[6][:, :], ACT.Copy).then_inc(xs_pt, 1)

        def act_xout(act, h):
            act.wait_ge(xs_pv, h + 1)
            nc.scalar.activation(oz_hi[:, 2 * h:2 * h + 2, :], two(ps[7][:, :]), ACT.Copy).then_inc(xo_hi, 1)

        def dve_xattn(dve):
            for m in range(XSTEPS + 3):
                if m == 0:
                    split_lo(dve, qc, 1, m, LEAD)
                    dve_norm(dve, N_XATT, False)
                if m < XSTEPS:
                    out = ps[banks[qg + m]][:, 0:NX]
                    dve.wait_ge(pe_done, qc + m + 1)
                    if m < KT:
                        nc.vector.tensor_tensor(qx[:, m, :], out, rstd[:, 0:NX], ALU.mult).then_inc(acc_free, 1)
                    else:
                        e = m - KT
                        if e >= 2:
                            dve.wait_ge(xv_tr, e - 1)
                        dst = tu if e % 2 else tg
                        nc.vector.tensor_tensor(dst[:, 0:NX], out, memr[:, :], ALU.mult).then_inc(acc_free, 1)
                if m % 2 == 0 and 0 <= (m - 2) // 2 < XHEADS:
                    dve_xmax(dve, (m - 2) // 2)
                if 0 < m < XSTEPS:
                    split_lo(dve, qc, 1, m, LEAD)
                if m < KT:
                    dve.wait_ge(m_hi, m + 1)
                    nc.vector.tensor_tensor(mem_lo[:, m, :], mem[:, m, :], mem_hi[:, m, :], ALU.subtract).then_inc(m_lo, 1)
                if m % 2 == 1 and 0 <= (m - 3) // 2 < XHEADS:
                    dve_xprobs(dve, (m - 3) // 2)
                if m % 2 == 0 and 0 <= (m - 12) // 2 < XHEADS:
                    dve_xlow(dve, (m - 12) // 2)

        def dve_xmax(dve, h):
            s = xsmall[:, h, :]
            dve.wait_ge(xs_s, h + 1)
            nc.vector.tensor_reduce(s[:, 0:2], two(ps[4 + h % 2][:, :]), AX.X, ALU.max).then_inc(xs_max, 1)
            dve.wait_ge(xs_max, h + 1)
            nc.vector.tensor_scalar(s[:, 2:4], s[:, 0:2], -(XH_DIM ** -0.5), None, ALU.mult).then_inc(xs_neg, 1)

        def dve_xprobs(dve, h):
            s = xsmall[:, h, :]
            dve.wait_ge(xs_exp, 2 * h + 2)
            nc.vector.reciprocal(s[:, 6:8], s[:, 4:6]).then_inc(xs_inv, 1)
            dve.wait_ge(xs_inv, h + 1)
            for qt in range(2):
                a = xatt[:, h, qt * NX:(qt + 1) * NX]
                nc.vector.tensor_scalar(a, a, s[:, 6 + qt:7 + qt], None, ALU.mult).then_inc(xs_norm, 1)

        def dve_xlow(dve, h):
            dve.wait_ge(xo_hi, h + 1)
            nc.vector.tensor_tensor(oz_lo[:, 2 * h:2 * h + 2, :], two(ps[7][:, :]), oz_hi[:, 2 * h:2 * h + 2, :],
                                    ALU.subtract).then_inc(xo_lo, 1)

        uc, ug = first["up"]

        def pe_up(pe):
            hi, lo = x_rhs("packed")

            def body(i, edge):
                for j in range(4):
                    pe.wait_ge(w_lo, splits(uc + 4 * i + j, uc + j))
                    out = start_group(pe, ug, 4, i, j)
                    head = edge and i == 0 and j == 0
                    strip(out[:, 0:NX], (uc + j) % RING, KT, hi, lo,
                          before=wait_x(pe, N_MLP) if head else None).then_inc(pe_done, 1)
                    if head:
                        pe_stat(pe, N_MLP, False)
                    if edge and i == 0 and j == 1:
                        pe_norm(pe, N_MLP, False)
            bodies(pe, F2T, 4, body)

        def act_up(act):
            def body(i, edge):
                for j in range(4):
                    split_hi(act, uc, 4, i, j + LEAD)
                    if edge and i == 0 and j == 0:
                        act_norm(act, N_MLP, False)
                    act.wait_ge(up_prod, 4 * i + j + 1)
                    nc.scalar.activation(hid(hid_hi, 4 * i + j, NX), hd[:, 0:NX], ACT.Copy).then_inc(up_hhi, 1)
            bodies(act, F2T, 4, body)

        def dve_up(dve):
            def low(u):
                dve.wait_ge(up_hhi, u + 1)
                nc.vector.tensor_tensor(hid(hid_lo, u, NX), hd[:, 0:NX], hid(hid_hi, u, NX), ALU.subtract).then_inc(up_hlo, 1)

            def body(i, edge):
                for j in range(4):
                    head = edge and i == 0 and j == 0
                    u = 4 * i + j
                    if head:
                        split_lo(dve, uc, 4, i, j + LEAD)
                        dve_norm(dve, N_MLP, False)
                    dve.wait_ge(pe_done, uc + 4 * i + j + 1)
                    if not head:
                        dve.wait_ge(up_prod, u)
                    nc.vector.tensor_tensor(tg[:, 0:NX], ps[banks[ug + j]][:, 0:NX], rstd[:, 0:NX], ALU.mult).then_inc(acc_free, 1)
                    dve.wait_ge(acc_free, ug + 4 * i + j + 1)
                    if not head:
                        dve.wait_ge(up_hlo, u)
                    nc.vector.scalar_tensor_tensor(hd[:, 0:NX], tg[:, 0:NX], 0.0, tg[:, 0:NX], ALU.max,
                                                   ALU.mult).then_inc(up_prod, 1)
                    if not head:
                        split_lo(dve, uc, 4, i, j + LEAD)
                    low(u)
            bodies(dve, F2T, 4, body)

        ffn_rhs = {w: (lambda t, w=w: (hid(hid_hi, t, w), hid(hid_lo, t, w))) for w in (T, NX)}
        block = ctx.enter_context(nc.Block())

        @block.sync
        def _(sp):
            sp.dma_start(res[:, 0:HALF, 0:T], io["res"][:, 0:HALF, :]).then_inc(res_low, 16)
            sp.dma_start(raw[:, 0, 0:KT * P], io["w_f1in"][0]).then_inc(w_in[0], 16)
            for name, n, tiles, *_ in PHASES:
                c0 = first[name][0]
                w = io[f"w_{name}"]

                def load(j, i, sp=sp, c0=c0, tiles=tiles, w=w):
                    static = isinstance(i, int)
                    c = c0 + 4 * i + j
                    last = c - RING
                    if static and last in plain:
                        sp.wait_ge(pe_done, last + 1)
                    elif not (static and c < RING):
                        sp.wait_ge(w_lo, splits(last, None if static else c0 + j))
                    sp.dma_start(raw[:, (c0 + j) % RING, 0:tiles * P], w[4 * i + j]).then_inc(w_in[(c0 + j) % RING], 16)

                for j in range(4):
                    if c0 + j:
                        load(j, 0)
                if n // 4 == 2:
                    for j in range(4):
                        load(j, 1)
                elif n // 4 > 2:
                    with sp.Fori(1, n // 4) as i:
                        for j in range(4):
                            load(j, i)
                for j in range(n % 4):
                    load(j, n // 4)
            for m in range(KT):
                sp.wait_ge(out_tile, m + 1)
                sp.dma_start(io["out"][:, m, :], outb[:, m, :]).then_inc(out_done, 16)
            sp.wait_ge(out_done, 16 * KT)

        @block.gpsimd
        def _(pool):
            nc.gpsimd.memset(ones[:, :], 1.0).then_inc(ones_set, 1)
            nc.gpsimd.memset(epsc[:, 0:1], EPS).then_inc(ones_set, 1)
            nc.gpsimd.memset(epsc[:, 1:2], HD * EPS).then_inc(ones_set, 1)
            pool.wait_ge(res_high, 16)
            for dst, name in ((same, "same"), (swap, "swap"), (convw, "convw")):
                pool.dma_start(dst[:, :], io[name]).then_inc(const_in, 16)
            pool.dma_start(posi[:, :], io["positions"]).then_inc(pos_in, 16)

            step = [0]

            def done(ins):
                step[0] += 1
                ins.then_inc(angle_step, 1)
                pool.wait_ge(angle_step, step[0])

            pool.wait_ge(pos_in, 16)
            pool.wait_ge(vec_in, 16)
            done(nc.gpsimd.tensor_copy(posf[:, :], posi[:, :]))
            done(nc.gpsimd.tensor_scalar(angle[:, :], posf[:, :], vecs[:, V_FREQ:V_FREQ + 1], None, ALU.mult))
            magic = 1.5 * 2.0 ** 23
            for period, bits in ((512 * np.pi, 10), (2 * np.pi, 15)):
                done(nc.gpsimd.tensor_scalar(turns[:, :], angle[:, :], float(1.0 / period), magic, ALU.mult, ALU.add))
                done(nc.gpsimd.tensor_scalar(turns[:, :], turns[:, :], -magic, None, ALU.add))
                rest = float(period)
                for p in range(3):
                    scale = 2.0 ** (np.floor(np.log2(abs(rest))) + 1 - bits)
                    piece = float(np.floor(rest / scale) * scale) if p < 2 else rest
                    rest -= piece
                    done(nc.gpsimd.tensor_scalar(part[:, :], turns[:, :], piece, None, ALU.mult))
                    done(nc.gpsimd.tensor_tensor(angle[:, :], angle[:, :], part[:, :], ALU.subtract))
            done(nc.gpsimd.tensor_scalar(angle[:, :], angle[:, :], 3.1415925, -3.1415925, ALU.min, ALU.max))
            assert step[0] == ANGLE_STEPS

            pool.wait_ge(pe_done, mc)
            nc.gpsimd.memset(table[:, :], NEG).then_inc(table_set, 1)
            pool.wait_ge(table_set, 1)
            pool.dma_start(table[0:BUCKETS, :], io["rel_table"]).then_inc(rel_const, 16)
            pool.dma_start(onehot[:, :], io["onehot"]).then_inc(rel_const, 16)
            nc.gpsimd.memset(mask[:, :], 0.0).then_inc(mask_set, 1)
            pool.wait_ge(mask_set, 1)
            for n, lo in enumerate((0, 2 * SEG)):
                nc.gpsimd.affine_select(out=mask[:, lo:lo + P], in_=mask[:, lo:lo + P], compare_op=ALU.is_ge, fill=NEG,
                                        base=0, pattern=[[-1, P]], channel_multiplier=1).then_inc(mask_set, 1)
                pool.wait_ge(mask_set, n + 2)
            nc.gpsimd.memset(small[:, :, :], 0.0).then_inc(mask_set, 1)
            pool.wait_ge(f_dve, 6)
            pool.dma_start(cum_dram.ap(), cum[:, :]).then_inc(ck_out, 16)
            pool.wait_ge(ck_out, 16)
            pool.dma_start(ckb[:, :, :], bass.AP(cum_dram, 0, [[0, P], [T, HEADS], [1, T]])).then_inc(ck_in, 16)
            pool.wait_ge(rel_row, 2)
            pool.dma_start(rel_dram.ap(), relrow[:, :]).then_inc(rel_out, 16)
            pool.wait_ge(rel_out, 16)
            rel_row_size = REL_X + REL_M
            copies = bass.AP(rel_dram, 0, [[0, P], [rel_row_size, HEADS], [1, rel_row_size]])
            pool.dma_start(rel_wide.ap(), copies).then_inc(rel_out, 16)
            pool.wait_ge(rel_out, 32)
            for col, n, start in ((0, P, 255), (P, META, REL_X + 255), (SEG, P, 127), (SEG + P, META, REL_X + 127),
                                  (2 * SEG, P, 255)):
                src = bass.AP(rel_wide, start, [[HEADS * rel_row_size - 1, P], [rel_row_size, HEADS], [1, n]])
                pool.dma_start(rel[:, :, col:col + n], src).then_inc(rel_in, 16)

            pool.wait_ge(pe_done, sc)
            nc.gpsimd.memset(glu[:, :, 0:TAPS - 1], 0.0).then_inc(glu_zero, 1)
            pool.dma_start(mem[:, :, :], io["mem"]).then_inc(mem_in, 16)
            pool.dma_start(decay[:, :, :], io["decay"]).then_inc(decay_in, 16)

        @block.scalar
        def _(act):
            act.dma_start(gains[:, :], io["gains"]).then_inc(gain_in, 16)
            act.dma_start(res[:, HALF:, 0:T], io["res"][:, HALF:, :]).then_inc(res_high, 16)
            act.dma_start(vecs[:, :], io["vecs"]).then_inc(vec_in, 16)
            act.dma_start(ident[:, :], io["ident"]).then_inc(ident_in, 16)
            act.wait_ge(gain_in, 16)
            act.wait_ge(ones_set, 3)
            act.wait_ge(res_low, 16)
            for m in range(KT):
                if m == HALF:
                    split_hi(act, 0, 1, 0, 0)
                    act.wait_ge(res_high, 16)
                act_x(N_F1, m, True)
            for m in range(KT):
                if m % HALF == 0:
                    split_hi(act, 0, 1, 1 + m // HALF, 0)
                if m >= 3:
                    act.wait_ge(sq_added, m - 2)
                act_square(N_F1, m, True, m % 2)
            act_ff_in(act, "f1in", N_F1, T)
            act_residual(act, "f1out", N_MIX, True, 2)
            act_mix(act)
            act_branch(act)
            act_residual(act, "wo", N_F2, False, 1)
            act_ff_in(act, "f2in", N_F2, NX)
            act_residual(act, "f2out", N_MIXB, False, 2)
            act_mixb(act)
            act_residual(act, "wo2", N_XATT, False, 1)
            act_xattn(act)
            act_residual(act, "xo", N_MLP, False, 1)
            act_up(act)
            act_residual(act, "down", N_FINAL, False, 4, prep=False)
            act_norm(act, N_FINAL, False)

        @block.vector
        def _(dve):
            dve.wait_ge(gain_in, 16)
            for m in range(KT):
                if m == HALF:
                    split_lo(dve, 0, 1, 0, 0)
                dve_prep(dve, N_F1, m, True)
            for m in range(KT):
                if m % HALF == 0:
                    split_lo(dve, 0, 1, 1 + m // HALF, 0)
                dve_square(dve, N_F1, m, True, m % 2)
            dve_ff_in(dve, "f1in", N_F1, T)
            dve_residual(dve, "f1out", N_MIX, True, 2, 0.5)
            dve_mix(dve)
            dve_branch(dve)
            dve_residual(dve, "wo", N_F2, False, 1, 1.0)
            dve_ff_in(dve, "f2in", N_F2, NX)
            dve_residual(dve, "f2out", N_MIXB, False, 2, 0.5)
            dve.wait_ge(glu_zero, 1)
            dve.wait_ge(const_in, 48)
            dve_mixb(dve)
            dve_residual(dve, "wo2", N_XATT, False, 1, 1.0)
            dve_xattn(dve)
            dve_residual(dve, "xo", N_MLP, False, 1, 1.0)
            dve_up(dve)
            dve_residual(dve, "down", N_FINAL, False, 4, 1.0, prep=False)
            dve_norm(dve, N_FINAL, False)
            for m in range(KT):
                nc.vector.scalar_tensor_tensor(two(outb[:, m, :]), res_tile(m, False), gain(N_FINAL, m),
                                               two(rstd[:, 0:NX]), ALU.mult, ALU.mult).then_inc(out_tile, 1)

        @block.tensor
        def _(pe):
            pe.wait_ge(ones_set, 3)
            pe_ff_in(pe, "f1in", N_F1, T)
            pe_residual(pe, "f1out", 2, T, ffn_rhs[T], lambda k: pe.wait_ge(ffs["f1"]["hlo"], k + 1))
            pe.wait_ge(const_in, 48)
            pe_mix(pe)
            pe_branch(pe)
            pe_residual(pe, "wo", 1, NX, lambda t: (oy_hi[:, 8 + t, :], oy_lo[:, 8 + t, :]),
                        lambda k: pe.wait_ge(y_lo, k + 1), late=1)
            pe_ff_in(pe, "f2in", N_F2, NX)
            pe_residual(pe, "f2out", 2, NX, ffn_rhs[NX], lambda k: pe.wait_ge(ffs["f2"]["hlo"], k + 1))
            pe_mixb(pe)
            pe_residual(pe, "wo2", 1, NX, lambda t: (oz_hi[:, t, :], oz_lo[:, t, :]),
                        lambda k: pe.wait_ge(z_lo, k + 1) if k < 4 else pe.wait_ge(c_lo, k - 3), late=4)
            pe_xattn(pe)
            pe_residual(pe, "xo", 1, NX, lambda t: (oz_hi[:, t, :], oz_lo[:, t, :]),
                        lambda k: pe.wait_ge(xo_lo, k // 2 + 1), late=2)
            pe_up(pe)
            pe_residual(pe, "down", 4, NX, ffn_rhs[NX], lambda k: pe.wait_ge(up_hlo, k + 1))
            pe_stat(pe, N_FINAL, False)
            pe_norm(pe, N_FINAL, False)


def shape_constants():
    eye = np.eye(P, dtype=np.float32)
    block = np.kron(np.eye(2), np.ones((HD, HD))).astype(np.float32)
    half = RDK // 2
    swap = np.zeros((P, P), np.float32)
    for h in range(P // RDK):
        for i in range(half):
            swap[h * RDK + half + i, h * RDK + i] = -1.0
            swap[h * RDK + i, h * RDK + half + i] = 1.0
    freq = np.float32(10000.0) ** (-np.arange(half, dtype=np.float32) / np.float32(half))
    freq = np.tile(freq, P // half).astype(np.float32).reshape(P, 1)

    def bucket(d):
        small = BUCKETS // 2
        large = small + int(np.log(max(d, 1) / small) / np.log(128 / small) * (BUCKETS - small) + 1e-9)
        return max(d, 0) if d < small else min(large, BUCKETS - 1)

    onehot = np.zeros((BUCKETS + 1, REL_X + REL_M), np.float32)
    for v in range(REL_X):
        d = 255 - v
        onehot[bucket(d) if 0 <= d < WINDOW else BUCKETS, v] = 1.0
    for v in range(REL_M):
        onehot[bucket(271 - v), REL_X + v] = 1.0
    log_g = np.log1p(-np.exp2(-5.0 - np.arange(HEADS)))
    j, i = np.arange(P)[:, None], np.arange(NX)[None, :]
    seen = j // HD <= i // HD
    full = np.exp(log_g[:, None, None] * np.abs(i - j)) * seen * RDK ** -0.5
    decay = np.concatenate([full, full[:, :, 0:P]], axis=2).transpose(1, 0, 2)
    return {"ident": eye, "same": block, "swap": swap, "freq": freq,
            "onehot": onehot, "decay": np.ascontiguousarray(decay.astype(np.float32))}


def strips(w, tiles=KT):
    k, m = w.shape
    a = w.reshape(k // P // tiles, tiles, P, m // P, P).transpose(3, 0, 2, 1, 4)
    return a.reshape(-1, P, tiles * P)


def kernel(**inputs):
    import concourse.bacc as bacc
    from concourse.bass_utils import run_bass_kernel_spmd as run

    a = {k: np.asarray(v) for k, v in inputs.items()}
    const = shape_constants()

    def turns(x, y):
        return np.stack([strips(x), strips(y)], axis=1).reshape(-1, P, KT * P)

    def columns(v):
        return v.reshape(-1, P).T

    arrays = {}
    for f, name in (("f1", "ffn1"), ("f2", "ffn2")):
        w_in, w_out = a[f"{name}_w_in"][0], a[f"{name}_w_out"][0]
        arrays[f"w_{f}in"] = turns(w_in[:, :FF], w_in[:, FF:])
        arrays[f"w_{f}out"] = strips(w_out, WIDE)
    w = a["w_in"][0]
    cut = np.cumsum([512, 512, 512, HEADS, 512, 128, 128, D])
    fq, fk, fv, ff, sq_, sk, sv, ga, gb = np.split(w, cut, axis=1)
    forget = np.zeros((D, P), w.dtype)
    forget[:, :HEADS] = ff
    order = np.concatenate([np.arange(HD) + HD * h for t in range(4) for h in (t, t + 4)])
    arrays["w_mix"] = np.concatenate([strips(x) for x in (forget, fk, fq, sk, sq_[:, order], fv, sv)] + [turns(ga, gb)])
    arrays["w_branch"] = np.concatenate([strips(a["w_branch_fox"][0], 4), strips(a["w_branch_swa"][0][order], 4)], axis=2)
    arrays["w_wo"] = strips(a["w_out"][0])
    w = a["w_in_2"]
    ca, cb, rq, rk, rv, rg = np.split(w, np.cumsum([512, 512, 256, 256, 512]), axis=1)
    arrays["w_mixb"] = np.concatenate([turns(cb, ca)] + [strips(x) for x in (rq, rk, rv, rg)])
    arrays["w_memk"], arrays["w_memv"] = strips(a["xkv_w_2"][:, :D]), strips(a["xkv_w_2"][:, D:])
    arrays["w_wo2"] = strips(np.roll(a["w_out_2"], CONV, axis=0))
    arrays["w_xq"], arrays["w_xo"] = strips(a["xq_w_2"]), strips(a["xo_w_2"])
    arrays["w_up"], arrays["w_down"] = strips(a["mlp_up_w_2"]), strips(a["mlp_down_w_2"])

    x, meta = a["x"][0], a["meta_tokens"]
    tokens = np.concatenate([x[:P], meta, x[P:]])
    arrays["res"] = tokens.T.reshape(KT, P, T).transpose(1, 0, 2)
    arrays["mem"] = a["mem_2"][0].T.reshape(KT, P, NX).transpose(1, 0, 2)
    arrays["gains"] = np.concatenate([columns(a[k].reshape(-1)) for k in (
        "ffn1_norm", "mix_norm", "ffn2_norm", "norm_mix_w_2", "norm_xattn_w_2", "norm_mlp_w_2", "norm_f_w_2",
        "norm_mem_w_2")], axis=1)
    twice = [np.tile(a[k][0], 2).reshape(P, 1) for k in ("fox_q_norm", "fox_k_norm", "swa_q_norm", "swa_k_norm")]
    fbias = np.zeros((P, 1), np.float32)
    fbias[:HEADS, 0] = a["forget_bias"][0]
    arrays["vecs"] = np.concatenate(twice + [fbias, const["freq"]] + [
        columns(a[k]) for k in ("conv_b_2", "conv_ln_w_2", "conv_ln_b_2", "ret_gn_w_2")
    ] + [np.broadcast_to(a["swa_sinks"][0], (P, HEADS))], axis=1)
    arrays["convw"] = a["conv_w_2"].T.reshape(4, P, TAPS).transpose(1, 0, 2).reshape(P, 4 * TAPS)
    arrays["positions"] = np.broadcast_to(a["positions_2"].reshape(1, NX), (P, NX))
    arrays["rel_table"] = a["rel_bias_table"]
    for k in ("ident", "same", "swap", "onehot", "decay"):
        arrays[k] = const[k]

    nc = bacc.Bacc("TRN2", target_bir_lowering=False, num_devices=1)
    arrays = {f"in_{k}": np.ascontiguousarray(v) for k, v in arrays.items()}
    io = {k[3:]: nc.dram_tensor(k, v.shape, mybir.dt.from_np(v.dtype), kind="ExternalInput").ap()
          for k, v in arrays.items()}
    io["out"] = nc.dram_tensor("out", (P, KT, NX), F32, kind="ExternalOutput").ap()
    build(nc, io)
    got = run(nc, [arrays], core_ids=[0]).results[0]["out"]
    return np.ascontiguousarray(got.transpose(2, 1, 0).reshape(1, NX, D))
```
